# Optimizing a Trainium2 kernel written in Bass

```python
import jax, jax.numpy as jnp
from jax import lax
import numpy as np

D_MODEL = 1024
BATCH = 1
SEQ = 256
DEPTH = 2

H_A = 8
DH_A = 128
D_CQ = 256
ROT_A = DH_A // 4
H_IDX = 8
D_IDX = 64
ROT_IDX = D_IDX // 4
TOPK_MAX = 256
Q_BLOCK = 128
ROPE_THETA = 500000.0
MAX_POS_OFFSET = 1024
N_R = 64
H_R = D_MODEL // N_R
D_R = H_R * N_R
LORA_W = 64
LORA_A = 64
LORA_V = 32
LORA_G = 128
GN_EPS = 64e-5
D_FF = ((8 * D_MODEL // 3 + 127) // 128) * 128
CONV_W = 3
LN_EPS = 1e-5

ATT_SIZES = (D_CQ, DH_A, DH_A, D_IDX, H_IDX)
RWKV_SIZES = (D_R, D_R, D_R, LORA_W, LORA_A, LORA_G)
N_ATT = sum(ATT_SIZES)
N_GATE = 2 * D_MODEL
N_RWKV = sum(RWKV_SIZES)
N_IN0 = N_ATT + N_GATE + N_RWKV
N_IN = N_IN0 + LORA_V

kernel_name = 'hybrid_dsa_rwkv7_deepnorm_trunk'

def split_cols(t, sizes):
    offs = np.cumsum(sizes)[:-1].tolist()
    return jnp.split(t, offs, axis=-1)

def layer_norm(x, g, b, eps=LN_EPS):
    xf = x.astype(jnp.float32)
    mu = jnp.mean(xf, -1, keepdims=True)
    var = jnp.mean(jnp.square(xf - mu), -1, keepdims=True)
    return ((xf - mu) * lax.rsqrt(var + eps) * g + b).astype(x.dtype)

def rms_norm(x, g, eps=1e-6):
    xf = x.astype(jnp.float32)
    return (xf * lax.rsqrt(jnp.mean(jnp.square(xf), -1, keepdims=True) + eps) * g).astype(x.dtype)

def rope_tables(positions, rot_dim):
    inv_freq = jnp.power(jnp.float32(ROPE_THETA), -jnp.arange(0, rot_dim, 2, dtype=jnp.float32) / rot_dim)
    ang = positions.astype(jnp.float32)[..., None] * inv_freq
    return jnp.cos(ang)[:, :, None, :], jnp.sin(ang)[:, :, None, :]

def partial_rope(x, cos, sin):
    half = cos.shape[-1]
    xf = x.astype(jnp.float32)
    x1, x2, rest = xf[..., :half], xf[..., half:2 * half], xf[..., 2 * half:]
    return jnp.concatenate([x1 * cos - x2 * sin, x2 * cos + x1 * sin, rest], -1).astype(x.dtype)

def token_shift(p, mu):
    prev = jnp.pad(p, ((0, 0), (1, 0), (0, 0)))[:, :-1]
    return p + (prev - p) * mu

def dsa_sparse_mqa(cq_raw, k_raw, v_raw, ik_raw, iw_raw, g_cq, w_uq, w_iq, g_ik, b_ik, w_oa, rope_a, rope_i):
    B, S, _ = cq_raw.shape
    topk = min(TOPK_MAX, S // 4)
    nb = S // Q_BLOCK
    c_q = rms_norm(cq_raw, g_cq)
    q = partial_rope((c_q @ w_uq).reshape(B, S, H_A, DH_A), *rope_a)
    k = partial_rope(k_raw[:, :, None, :], *rope_a)[:, :, 0]
    v = v_raw
    qi = partial_rope((c_q @ w_iq).reshape(B, S, H_IDX, D_IDX), *rope_i)
    ki = partial_rope(layer_norm(ik_raw, g_ik, b_ik)[:, :, None, :], *rope_i)[:, :, 0]
    wi = iw_raw.astype(jnp.float32) * (H_IDX ** -0.5 * D_IDX ** -0.5)
    key_pos = jnp.arange(S, dtype=jnp.int32)

    def to_blocks(t):
        return t.reshape(B, nb, Q_BLOCK, *t.shape[2:]).swapaxes(0, 1)

    gather = jax.vmap(lambda t, i: t[i])

    def block(args):
        qb, qib, wib, tb = args
        rel = jax.nn.relu(jnp.einsum('bqhd,bsd->bqhs', qib, ki).astype(jnp.float32))
        score = jnp.einsum('bqhs,bqh->bqs', rel, wib)
        score = jnp.where((key_pos[None, :] <= tb[:, None])[None], score, -jnp.inf)
        _, idx = lax.top_k(score, topk)
        valid = idx <= tb[None, :, None]
        k_sel = gather(k, idx)
        v_sel = gather(v, idx)
        logits = jnp.einsum('bqhd,bqkd->bqhk', qb, k_sel).astype(jnp.float32) * DH_A ** -0.5
        logits = jnp.where(valid[:, :, None, :], logits, -jnp.inf)
        probs = jax.nn.softmax(logits, axis=-1).astype(v.dtype)
        return jnp.einsum('bqhk,bqkd->bqhd', probs, v_sel)

    o = lax.map(block, (to_blocks(q), to_blocks(qi), to_blocks(wi), key_pos.reshape(nb, Q_BLOCK)))
    o = o.swapaxes(0, 1).reshape(B, S, H_A * DH_A)
    return o @ w_oa

def rwkv7_time_mix(r, k, v, p_w, p_a, p_g, w0, w2, a0, a2, g2, k_k, k_a, r_k, g_lnx, b_lnx, w_ob):
    B, S, _ = r.shape
    w = -jax.nn.softplus(-(w0 + jnp.tanh(p_w) @ w2)) - 0.5
    decay = jnp.exp(-jnp.exp(w.astype(jnp.float32)))
    a = jax.nn.sigmoid(a0 + p_a @ a2)
    g = jax.nn.sigmoid(p_g) @ g2
    hd = lambda t: t.reshape(B, S, H_R, N_R).astype(jnp.float32)
    kk = hd(k * k_k)
    kk = kk / jnp.maximum(jnp.linalg.norm(kk, axis=-1, keepdims=True), 1e-12)
    k = k * (1 + (a - 1) * k_a)
    r_h, k_h, v_h, a_h, w_h = hd(r), hd(k), hd(v), hd(a), hd(decay)
    b_h = kk * a_h

    def step(state, inp):
        r_t, w_t, k_t, v_t, kk_t, b_t = inp
        sa = jnp.einsum('bhvk,bhk->bhv', state, -kk_t)
        state = state * w_t[:, :, None, :] + sa[..., None] * b_t[:, :, None, :] + v_t[..., None] * k_t[:, :, None, :]
        return state, jnp.einsum('bhvk,bhk->bhv', state, r_t)

    xs = tuple(t.swapaxes(0, 1) for t in (r_h, w_h, k_h, v_h, kk, b_h))
    state0 = jnp.zeros((B, H_R, N_R, N_R), jnp.float32)
    _, y = lax.scan(step, state0, xs)
    y = y.swapaxes(0, 1)
    mu = jnp.mean(y, -1, keepdims=True)
    var = jnp.mean(jnp.square(y - mu), -1, keepdims=True)
    y = ((y - mu) * lax.rsqrt(var + GN_EPS)).reshape(B, S, D_R) * g_lnx + b_lnx
    bonus = jnp.sum(r_h * k_h * r_k.astype(jnp.float32), -1, keepdims=True) * v_h
    y = y + bonus.reshape(B, S, D_R)
    return (y * g).astype(r.dtype) @ w_ob

def conv_glu_ffn(x, w_up, conv_w, conv_b, w_down):
    h_gate, h_val = jnp.split(x @ w_up, 2, axis=-1)
    h_gate = lax.conv_general_dilated(h_gate, conv_w[:, None, :], (1,), ((CONV_W - 1, 0),),
                                      dimension_numbers=('NWC', 'WIO', 'NWC'),
                                      feature_group_count=D_FF) + conv_b
    return (jax.nn.silu(h_gate) * h_val) @ w_down

def setup_inputs(seed: int = 0) -> dict:
    key = jax.random.key(seed)
    ks = iter(jax.random.split(key, 48))
    nrm = lambda shape, scale: jax.random.normal(next(ks), shape, jnp.float32) * scale
    L = DEPTH
    beta = (8 * DEPTH) ** -0.25
    x = nrm((BATCH, SEQ, D_MODEL), 1.0)
    offset = jax.random.randint(next(ks), (BATCH, 1), 0, MAX_POS_OFFSET, dtype=jnp.int32)
    positions = offset + jnp.arange(SEQ, dtype=jnp.int32)[None, :]
    return {
        'x': x,
        'positions': positions,
        'w_in0': nrm((D_MODEL, N_IN0), D_MODEL ** -0.5),
        'w_in_rest': nrm((L - 1, D_MODEL, N_IN), D_MODEL ** -0.5),
        'b_gate': nrm((L, N_GATE), 0.02),
        'g_cq': 1.0 + nrm((L, D_CQ), 0.02),
        'w_uq': nrm((L, D_CQ, H_A * DH_A), D_CQ ** -0.5),
        'w_iq': nrm((L, D_CQ, H_IDX * D_IDX), D_CQ ** -0.5),
        'g_ik': 1.0 + nrm((L, D_IDX), 0.02),
        'b_ik': nrm((L, D_IDX), 0.02),
        'w_oa': nrm((L, H_A * DH_A, D_MODEL), beta * (H_A * DH_A) ** -0.5),
        'mu_rwkv': jax.random.uniform(next(ks), (L, N_RWKV), jnp.float32),
        'mu_vres': jax.random.uniform(next(ks), (L - 1, LORA_V), jnp.float32),
        'w0': jnp.linspace(-6.5, -1.5, D_R, dtype=jnp.float32)[None, :] + nrm((L, D_R), 0.1),
        'w2': nrm((L, LORA_W, D_R), 0.5 * LORA_W ** -0.5),
        'a0': nrm((L, D_R), 0.1),
        'a2': nrm((L, LORA_A, D_R), LORA_A ** -0.5),
        'v0': 0.5 + nrm((L - 1, D_R), 0.1),
        'v2': nrm((L - 1, LORA_V, D_R), LORA_V ** -0.5),
        'g2': nrm((L, LORA_G, D_R), LORA_G ** -0.5),
        'k_k': 0.85 + nrm((L, D_R), 0.05),
        'k_a': 1.0 + nrm((L, D_R), 0.05),
        'r_k': nrm((L, H_R, N_R), 0.1),
        'g_lnx': 1.0 + nrm((L, D_R), 0.02),
        'b_lnx': nrm((L, D_R), 0.02),
        'w_ob': nrm((L, D_R, D_MODEL), beta * D_R ** -0.5),
        'w_out': nrm((L, D_MODEL, D_MODEL), beta * D_MODEL ** -0.5),
        'ln1_g': 1.0 + nrm((L, D_MODEL), 0.02),
        'ln1_b': nrm((L, D_MODEL), 0.02),
        'w_up': nrm((L, D_MODEL, 2 * D_FF), D_MODEL ** -0.5),
        'conv_w': nrm((L, CONV_W, D_FF), CONV_W ** -0.5),
        'conv_b': nrm((L, D_FF), 0.02),
        'w_down': nrm((L, D_FF, D_MODEL), beta * D_FF ** -0.5),
        'ln2_g': 1.0 + nrm((L, D_MODEL), 0.02),
        'ln2_b': nrm((L, D_MODEL), 0.02),
    }

def reference(x, positions, w_in0, w_in_rest, b_gate, g_cq, w_uq, w_iq, g_ik, b_ik, w_oa,
              mu_rwkv, mu_vres, w0, w2, a0, a2, v0, v2, g2, k_k, k_a, r_k, g_lnx, b_lnx, w_ob,
              w_out, ln1_g, ln1_b, w_up, conv_w, conv_b, w_down, ln2_g, ln2_b):
    alpha = (2 * DEPTH) ** 0.25
    rope_a = rope_tables(positions, ROT_A)
    rope_i = rope_tables(positions, ROT_IDX)
    v_first = None
    for i in range(DEPTH):
        p = x @ (w_in0 if i == 0 else w_in_rest[i - 1])
        p_att = p[..., :N_ATT]
        p_gate = p[..., N_ATT:N_ATT + N_GATE]
        p_rw = token_shift(p[..., N_ATT + N_GATE:N_IN0], mu_rwkv[i])
        cq_raw, k_raw, v_raw, ik_raw, iw_raw = split_cols(p_att, ATT_SIZES)
        y_a = dsa_sparse_mqa(cq_raw, k_raw, v_raw, ik_raw, iw_raw, g_cq[i], w_uq[i], w_iq[i],
                             g_ik[i], b_ik[i], w_oa[i], rope_a, rope_i)
        pr, pk, pv, pw, pa, pg = split_cols(p_rw, RWKV_SIZES)
        if i == 0:
            v_first = pv
            v = pv
        else:
            p_vr = token_shift(p[..., N_IN0:], mu_vres[i - 1])
            v = pv + (v_first - pv) * jax.nn.sigmoid(v0[i - 1] + p_vr @ v2[i - 1])
        y_b = rwkv7_time_mix(pr, pk, v, pw, pa, pg, w0[i], w2[i], a0[i], a2[i], g2[i],
                             k_k[i], k_a[i], r_k[i], g_lnx[i], b_lnx[i], w_ob[i])
        g_a, g_b = jnp.split(jax.nn.sigmoid(p_gate + b_gate[i]), 2, axis=-1)
        x = layer_norm(alpha * x + (g_a * y_a + g_b * y_b) @ w_out[i], ln1_g[i], ln1_b[i])
        x = layer_norm(alpha * x + conv_glu_ffn(x, w_up[i], conv_w[i], conv_b[i], w_down[i]), ln2_g[i], ln2_b[i])
    return x


_drawn_inputs = setup_inputs


def setup_inputs(seed=0):
    import zlib

    import numpy as np

    out = dict(_drawn_inputs(seed))
    spreads = {}
    factors = {'b_gate': 8.0,
     'g_cq': 72.534,
     'w_iq': 3.118,
     'g_ik': 94.971,
     'b_ik': 116.01,
     'mu_vres': 7.265,
     'w2': 8.0,
     'a0': 8.0,
     'v0': 8.0,
     'v2': 3.465,
     'k_k': 24.685,
     'k_a': 8.0,
     'r_k': 3.555,
     'g_lnx': 29.439,
     'b_lnx': 28.373,
     'conv_b': 8.0}
    for name, (base, spread) in spreads.items():
        noise = np.random.default_rng([zlib.crc32(name.encode()), seed]).standard_normal(out[name].shape)
        drawn = base * np.exp(spread * noise) if base else spread * noise
        out[name] = __import__('jax').numpy.asarray(drawn.astype(out[name].dtype))
    for name, factor in factors.items():
        out[name] = (out[name] * factor).astype(out[name].dtype)
    return out
```

```python
import math
from contextlib import ExitStack

import numpy as np

import concourse.bass as bass
from concourse import mybir

F32 = mybir.dt.float32
I32 = mybir.dt.int32
U32 = mybir.dt.uint32
ALU = mybir.AluOpType
ACT = mybir.ActivationFunctionType
AX = mybir.AxisListType.X

P = 128
D = 1024
T = 256
DEPTH = 2
TT = T // P
KB = D // P
ALPHA = (2 * DEPTH) ** 0.25
H_A, DH_A, D_CQ, ROT_A = 8, 128, 256, 32
H_IDX, D_IDX, ROT_IDX = 8, 64, 16
TOPK = 64
THETA = 500000.0
N_R = 64
LORA_W, LORA_A, LORA_V, LORA_G = 64, 64, 32, 128
GN_EPS, LN_EPS, RMS_EPS = 64e-5, 1e-5, 1e-6
D_FF = ((8 * D // 3 + 127) // 128) * 128
FB = D_FF // P
N_ATT = D_CQ + 2 * DH_A + D_IDX + H_IDX
N_GATE = 2 * D
N_RWKV = 3 * D + LORA_W + LORA_A + LORA_G
N_IN0 = N_ATT + N_GATE + N_RWKV
C_K, C_V, C_IK, C_IW = D_CQ, D_CQ + DH_A, D_CQ + 2 * DH_A, D_CQ + 2 * DH_A + D_IDX
NFR = ROT_A // 2 + ROT_IDX // 2
DECAY = math.exp(-0.5)
CH = 64
NCH = T // CH
GROUPS = 4
GB = KB // GROUPS
NU = GB * NCH
NEG = -1e30
TAKEN = -3e38

RING = 4


def stream_order(layer):
    s = [("att", i) for i in range(5)]
    s += [("lora", 0), ("lora", 1)] + ([("vres", 0)] if layer else [])
    s += rkv_slots(0)[:4] + [("iq", 0), ("uq", 0), ("uq", 1)] + rkv_slots(0)[4:]
    for g in range(GROUPS):
        if g + 1 < GROUPS:
            s += rkv_slots(g + 1)
        s += [("gate", 4 * g + i) for i in range(4)]
    s += [("oa", i) for i in range(KB)] + [("ob", i) for i in range(KB)] + [("out", i) for i in range(KB)]
    for i in range(FB):
        s += [("up", i), ("up", FB + i)]
    s += [("down", i) for i in range(FB)]
    return s


def rkv_slots(g):
    return [("rkv", 8 * t + GB * g + b) for t in range(3) for b in range(GB)]


SLOTS = [(l, *s) for l in range(DEPTH) for s in stream_order(l)]
SLOT_AT = {s: n for n, s in enumerate(SLOTS)}

CPAR = [("b_gate", 16), ("mu", 27), ("w0", 8), ("a0", 8), ("v0", 8), ("k_k", 8), ("k_a", 8), ("r_k", 8),
        ("g_lnx", 8), ("b_lnx", 8), ("g_cq", 2), ("conv_w", 3 * FB), ("conv_b", FB)]
CPAR_AT = {n: sum(w for _, w in CPAR[:i]) for i, (n, _) in enumerate(CPAR)}
NCPAR = sum(w for _, w in CPAR)
DPAR = [("omu", 27), ("hw0", 8), ("ha0", 8), ("hv0", 8), ("hgate", 16), ("hka", 8), ("omhka", 8)]
DPAR_AT = {n: sum(w for _, w in DPAR[:i]) for i, (n, _) in enumerate(DPAR)}
NDPAR = sum(w for _, w in DPAR)
CONST = [("ident", 128), ("stack", 64), ("strict", 64), ("incl", 64), ("hsel", 2), ("bones", 128),
         ("rowsel", 512), ("scan", 512), ("causal", 128), ("freq", NFR)]
CONST_AT = {n: sum(w for _, w in CONST[:i]) for i, (n, _) in enumerate(CONST)}
NCONST = sum(w for _, w in CONST)
LEVELS = 6


class Steps:

    def __init__(self, sem, names):
        self.sem, self.names, self.value, self.next = sem, names, {}, 0
        for r, steps in enumerate(names):
            for name in steps:
                self.value[r, name] = len(self.value) + 1

    def __call__(self, r, name):
        return self.sem, self.value[r, name]

    def inc(self, r, name):
        self.next += 1
        assert self.value[r, name] == self.next, (r, name, self.value[r, name], self.next)
        return self.sem, 1


def trunk(nc, x_in, pos_in, stream, lora_in, cpar_in, rpar_in, const_in, masks_in, out):
    ctx = ExitStack()
    with ctx:
        def sb(name, shape, dt=F32):
            return ctx.enter_context(nc.sbuf_tensor(name, shape, dt))

        def sem(name):
            return ctx.enter_context(nc.semaphore(name))

        ps = ctx.enter_context(nc.psum_tensor("ps", [P, 8, 512], F32))

        def bank(n):
            return ps[:, n, :]

        def units(n):
            return ps[:, n:n + 2, :].rearrange("p k (u s) -> p (k u) s", s=P)

        def unit64(n):
            return ps[:, n, :].rearrange("p (u s) -> p u s", s=CH)

        def tok(n):
            return ps[:, n, :].rearrange("p (b t) -> p b t", t=T)

        ring = sb("ring", [P, RING, D])
        x_tok = sb("x_tok", [P, TT, D])
        xT = sb("xT", [P, KB, T])
        gates = sb("gates", [P, 2 * KB, T])
        yb = sb("yb", [P, KB, T])
        oT = sb("oT", [P, H_A, T])
        qT = oT
        v_first = sb("v_first", [P, KB, T])
        lora_w = sb("lora_w", [P, 3, D])
        lora = sb("lora", [P, 3, T])
        cpar = sb("cpar", [P, DEPTH, NCPAR])
        dpar = sb("dpar", [P, NDPAR])
        const = sb("const", [P, NCONST])
        masks = sb("masks", [P, 2, LEVELS, CH], U32)
        half = sb("half", [P, 16])
        p_tok = sb("p_tok", [P, TT, N_ATT])
        kid = sb("kid", [P, TT, 2, D_IDX])
        kirow = sb("kirow", [P, 2 * D_IDX])
        cqT = sb("cqT", [P, 2, T])
        kT = sb("kT", [P, T])
        kiT = sb("kiT", [P, 2, T])
        keep = sb("keep", [P, TT, T])
        small = sb("small", [P, 64])
        scratch = sb("scratch", [P, 1536])
        rel = scratch[:, 0:1024].rearrange("p (a n) -> p a n", a=2)
        qi_tok = rel
        lg = scratch[:, 0:768]
        pT = scratch[:, 768:1536].rearrange("p (a n) -> p a n", a=2)
        sines = sb("sines", [P, 2, TT, NFR])
        ang = sb("ang", [P, 3, TT, NFR])
        pos = sb("pos", [P, TT], I32)
        posf = sb("posf", [P, TT])
        ln = sb("ln", [P, TT, 24])
        rs, ks, vs_own = sb("rs", [P, GB, T]), sb("ks", [P, GB, T]), sb("vs", [P, GB, T])
        dA, dB, dC = sb("dA", [P, GB, T]), sb("dB", [P, GB, T]), sb("dC", [P, GB, T])
        tha, tmp, kkn = sb("tha", [P, GB, T]), sb("tmp", [P, GB, T]), sb("kkn", [P, GB, T])
        gT = sb("gT", [P, GB, T])
        arc = sb("arc", [P, NU, 2, CH])
        qiT = arc[:, :, :, :].rearrange("p (h a) b s -> p h (a b s)", h=4)
        vtmp = scratch[:, 1024:1536]
        a_bd, r_bd = sb("a_bd", [P, NU, P]), sb("r_bd", [P, NU, P])
        b_bd, k_bd, v_bd = sb("b_bd", [P, NU, P]), sb("k_bd", [P, NU, P]), sb("v_bd", [P, NU, P])
        W_bd = k_bd
        kt_bd = v_bd
        nT_bd, ak_bd = sb("nT_bd", [P, NU, P]), sb("ak_bd", [P, NU, P])
        rb_bd, rk_bd = sb("rb_bd", [P, NU, P]), sb("rk_bd", [P, NU, P])
        bt_bd = sb("bt_bd", [P, NU, P])
        Y_bd, y_bd = sb("Y_bd", [P, NU, P]), sb("y_bd", [P, NU, P])
        X, Y, W = sb("X", [P, NU, CH]), sb("Y", [P, NU, CH]), sb("W", [P, NU, CH])
        Vc = sb("Vc", [P, NU, CH])
        Zs, Qs, S = sb("Zs", [P, GB, CH]), sb("Qs", [P, GB, CH]), sb("S", [P, 2, GB, CH])
        Sa = sb("Sa", [P, GB, CH])
        pend = sb("pend", [P, 2, GB, NCH])
        yt = sb("yt", [P, NU, CH])
        sq = W
        bv = sb("bv", [P, GB, T])
        ssm, rn, rnT = sb("ssm", [P, 8]), sb("rn", [P, 8]), sb("rnT", [8, P])
        g8 = sb("g8", [P, 5, NU])
        q_tok = [gates[:, 4 * j:4 * j + 4, :].rearrange("p (a b) s -> p a (b s)", a=TT) for j in range(2)]
        lnrow = [bt_bd[:, :, :].rearrange("p u s -> p (u s)"), v_bd[:, :, :].rearrange("p u s -> p (u s)")]
        hid_parts = [a_bd, r_bd, b_bd, k_bd, nT_bd, ak_bd]

        def hid(i):
            return hid_parts[i // 4][:, 2 * (i % 4):2 * (i % 4) + 2, :].rearrange("p a b -> p (a b)")

        conv = [dA, dB]

        def flat(t):
            return t[:, :, :].rearrange("p a b -> p (a b)")

        def by_unit(t):
            return t.rearrange("p b (c s) -> p (b c) s", s=CH)

        def vs(r):
            g = r % GROUPS
            return v_first[:, GB * g:GB * g + GB, :] if r < GROUPS else vs_own[:, :, :]

        C = {n: const[:, CONST_AT[n]:CONST_AT[n] + w] for n, w in CONST}
        ident, stack = C["ident"], C["stack"]

        def cp(layer, name, i=0, n=1):
            a = CPAR_AT[name] + i
            return cpar[:, layer, a:a + n]

        def dp(name, i=0, n=1):
            a = DPAR_AT[name] + i
            return dpar[:, a:a + n]

        def q64(h):
            return slice(64 * h, 64 * h + 64)

        R = DEPTH * GROUPS
        L2 = range(DEPTH)
        lv = range(1, LEVELS)

        landed = [sem(f"slot{i}_landed") for i in range(RING)]
        slot_used = sem("slot_used")
        inputs_in = sem("inputs_in")
        lora_landed = sem("lora_landed")
        rows_landed = sem("rows_landed")
        stored = sem("stored")
        zeroed = sem("zeroed")
        tables_dve = sem("tables_dve")
        kid_half = sem("kid_half")
        tables = sem("tables")

        def used(l, kind, i):
            return slot_used, SLOT_AT[l, kind, i] + 1

        def pair_slots(n):
            kind, i = n
            return {"lora": [("lora", 0), ("lora", 1)], "vres": [("vres", 0)],
                    "rkv": [("rkv", 8 * (i % 3) + GB * (i // 3) + b) for b in range(GB)],
                    "gate": [("gate", 2 * i), ("gate", 2 * i + 1)],
                    "oa": [("oa", 2 * i), ("oa", 2 * i + 1)], "ob": [("ob", 2 * i), ("ob", 2 * i + 1)],
                    "up": [("up", i), ("up", FB + i)]}[kind]

        pairs = []
        for l in L2:
            seen = []
            for s in stream_order(l):
                kind, i = s
                n = {"lora": ("lora", 0), "vres": ("vres", 0), "rkv": ("rkv", i % 8 // 2 * 3 + i // 8),
                     "gate": ("gate", i // 2), "oa": ("oa", i // 2), "ob": ("ob", i // 2),
                     "up": ("up", i % FB)}.get(kind)
                if n and n not in seen:
                    seen.append(n)
            pairs += [(l, n) for n in seen]
        pair_at = {n: d for d, n in enumerate(pairs)}

        def pair_done(l, n):
            return used(l, *pair_slots(n)[-1])

        shifted = ("lora", "vres", "rkv")
        act_dense = Steps(sem("act_dense"), [sum([[n] if n[0] in shifted + ("gate",) else
                                                  [n, (n, "tanh")] if n[0] == "up" else []
                                                  for k, n in pairs if k == l], []) for l in L2])
        dve_dense = Steps(sem("dve_dense"), [sum([[n] if n[0] in shifted + ("oa", "ob") else
                                                  [(n, "conv1"), (n, "conv"), (n, "silu"), n] if n[0] == "up" else []
                                                  for k, n in pairs if k == l], []) for l in L2])

        def pair_free(l, n):
            return act_dense(l, n) if n[0] == "gate" else dve_dense(l, n)

        def by_layer(name, steps):
            return Steps(sem(name), [steps] * DEPTH)

        def by_round(name, steps):
            return Steps(sem(name), [steps] * R)

        pe_x = by_layer("pe_x", [f"T{i}" for i in range(4)] + [f"U{i}" for i in range(4)])
        act_x = by_layer("act_x", [f"T{i}" for i in range(4)] + ["Aax"] + [f"U{i}" for i in range(4)] + ["Bax"])
        dve_par = by_layer("dve_par", ["dpar", "lsig"])
        dve_x = by_layer("dve_x", [f"mix{i}" for i in range(4)]
                         + sum([[f"{w}add", f"{w}st", f"{w}mv", f"{w}c", f"{w}n"] for w in "AB"], []))
        act_lora = by_layer("act_lora", ["tanh"])
        pool_x = by_layer("pool_x", ["Aeps", "A", "Beps", "B"])
        pe_att = by_layer("pe_att", ["cqT", "kT", "qiT", "qT"] + [f"s{i}" for i in range(6)]
                          + sum([[f"lg{g}", f"pT{g}", f"o{g}"] for g in range(GROUPS)], []))
        act_att = by_layer("act_att", ["p", "ssq", "cqT", "kT", "qi", "q0", "q1", "qiT", "qT"]
                           + [f"s{i}" for i in range(6)]
                           + sum([[f"e{g}", f"pT{g}", f"o{g}"] for g in range(GROUPS)], []))
        rope = lambda w: [f"{w}a", f"{w}"]
        dve_att = by_layer("dve_att", ["wi", "kst", "kmv"] + rope("rk") + ["cq", "kic", "ki"] + rope("rki") + rope("rqi")
                           + rope("rq0") + rope("rq1")
                           + [f"s{t}{h}" for t in range(TT) for h in range(H_IDX)]
                           + sum([[f"causal{t}"] + sum([[f"max{t}{i}", f"rep{t}{i}"] for i in range(8)], [])
                                  + [f"sel{t}", f"selb{t}", f"keep{t}"] for t in range(TT)], [])
                           + sum([[f"lg{g}", f"mx{g}", f"rc{g}", f"pn{g}"] for g in range(GROUPS)], []))
        pool_att = by_layer("pool_att", ["eps", "rs"])

        pe_prep = Steps(sem("pe_prep"), [["zw", "za"] + (["zv"] if r >= GROUPS else []) + ["ss", "rnT", "rnx"]
                                         for r in range(R)])
        act_prep = Steps(sem("act_prep"), [["kk2", "thw", "tha", "P", "Pp", "iP", "kt"]
                                           + (["thv"] if r >= GROUPS else []) for r in range(R)])
        dve_prep = Steps(sem("dve_prep"), [["s", "cum", "cp", "pend", "ss", "rnT"]
                                           + (["v1", "v2", "v"] if r >= GROUPS else [])
                                           + ["kkn", "k2", "kb", "arc", "bneg", "kp", "rkk"] for r in range(R)])
        pool_prep = by_round("pool_prep", ["rn"])
        pe_wkv = by_round("pe_wkv", ["gramB", "gramK", "V", "nX", "tokB", "tokK", "bonus", "zg"]
                          + sum([[f"W{l}"] + ([f"XW{l}"] if l < LEVELS - 1 else []) + [f"WtY{l}"] for l in lv], [])
                          + sum([[f"Z{c}", f"Q{c}"] + ([f"S{c}"] if c < NCH - 1 else []) + [f"y{c}"]
                                 for c in range(NCH)], []))
        pe_yT = by_round("pe_yT", ["yT"])
        act_wkv = by_round("act_wkv", ["reset", "vbd", "Vc", "tokB", "tokK", "g"] + [f"W{l}" for l in lv]
                           + [f"Z{c}" for c in range(NCH)])
        act_y = by_round("act_y", ["y", "sq", "yn"])
        dve_wkv = by_round("dve_wkv", ["nT", "Arb", "Y0", "Aak", "Ark", "X0", "bv"]
                           + sum([[f"W{l}"] + ([f"X{l}"] if l < LEVELS - 1 else []) + [f"Y{l}"] for l in lv], [])
                           + sum([[f"Q{c}"] + ([f"S{c}a"] * (c > 0) + [f"S{c}"] if c < NCH - 1 else [])
                                  for c in range(NCH)], []))
        dve_y = by_round("dve_y", ["m", "m2", "yc", "v8", "yr", "yb1", "yb"])
        pool_bd = by_round("pool_bd", ["abd0", "abd1", "rbd0", "rbd"])
        pool_y = by_round("pool_y", ["eps", "rstd"])

        block = ctx.enter_context(nc.Block())

        @block.sync
        def _(sp):
            sp.dma_start(x_tok[:, :, :], x_in.rearrange("(a p) d -> p a d", p=P)).then_inc(inputs_in, 16)
            sp.dma_start(const[:, :], const_in).then_inc(inputs_in, 16)
            for n in range(RING):
                sp.dma_start(ring[:, n, :], stream[n]).then_inc(landed[n], 16)
            sp.dma_start(pos[:, :], pos_in).then_inc(inputs_in, 16)
            sp.dma_start(flat(cpar), cpar_in).then_inc(inputs_in, 16)
            sp.dma_start(masks[:, :, :, :].rearrange("p a l c -> p (a l c)"), masks_in).then_inc(inputs_in, 16)
            with sp.Fori(1, len(SLOTS) // RING) as i:
                for n in range(RING):
                    sp.wait_ge(slot_used, i * RING + (n + 1 - RING))
                    sp.dma_start(ring[:, n, :], stream[bass.ds(i * RING + n, 1)].rearrange("a p d -> p (a d)")
                                 ).then_inc(landed[n], 16)
            for n in range(len(SLOTS) // RING * RING, len(SLOTS)):
                sp.wait_ge(slot_used, n + 1 - RING)
                sp.dma_start(ring[:, n % RING, :], stream[n]).then_inc(landed[n % RING], 16)
            sp.wait_ge(*dve_x(DEPTH - 1, "Bn"))
            sp.dma_start(out.rearrange("(a p) d -> p a d", p=P), x_tok[:, :, :]).then_inc(stored, 16)
            sp.wait_ge(stored, 16)

        @block.gpsimd
        def _(pool):
            def zero_bd(l):
                again = [a_bd, r_bd, b_bd, k_bd, v_bd, nT_bd, ak_bd, y_bd]
                if l:
                    pool.wait_ge(*dve_x(l - 1, "Bn"))
                    again = [a_bd, r_bd, b_bd, k_bd, v_bd, nT_bd, ak_bd]
                else:
                    pool.memset(kiT[:, :, :], 0.0)
                    again += [rb_bd, rk_bd, Y_bd]
                for t in again:
                    last = pool.memset(t[:, :, :], 0.0)
                last.then_inc(zeroed, 1)

            def small_rows(l):
                if l:
                    pool.wait_ge(*pe_wkv(GROUPS * l - 1, "zg"))
                    pool.wait_ge(*pe_prep(GROUPS * l - 1, "za"))
                    pool.wait_ge(*dve_att(l - 1, "ki"))
                pool.dma_start(flat(lora_w), lora_in[l]).then_inc(lora_landed, 16)
                pool.dma_start(kirow[:, :], rpar_in[l:l + 1, 4 * D:4 * D + 2 * D_IDX].broadcast_to([P, 2 * D_IDX])
                               ).then_inc(lora_landed, 16)

            def norm_rows(l, w):
                i = "AB".index(w)
                if i == 0:
                    pool.wait_ge(*pe_wkv(GROUPS * (l + 1) - 1, f"y{NCH - 1}"))
                else:
                    pool.wait_ge(*dve_x(l, "An"))
                for j in range(2):
                    a = (2 * i + j) * D
                    pool.dma_start(lnrow[j], rpar_in[l:l + 1, a:a + D].broadcast_to([P, D])
                                   ).then_inc(rows_landed, 16)

            def norm_rsqrt(l, w):
                pool.wait_ge(*dve_x(l, f"{w}mv"))
                pool.tensor_scalar(ln[:, :, 20], ln[:, :, 13], 1.0, LN_EPS, ALU.mult, ALU.add
                                   ).then_inc(*pool_x.inc(l, f"{w}eps"))
                pool.wait_ge(*pool_x(l, f"{w}eps"))
                pool.tensor_tensor(ln[:, :, 21], ln[:, :, 20], half[:, 0:TT], ALU.pow
                                   ).then_inc(*pool_x.inc(l, w))

            def head_norm(r):
                pool.wait_ge(*dve_prep(r, "ss"))
                pool.tensor_tensor(rn[:, :], ssm[:, :], half[:, 0:8], ALU.pow).then_inc(*pool_prep.inc(r, "rn"))

            pool.memset(half[:, :], -0.5).then_inc(zeroed, 1)
            small_rows(0)
            zero_bd(0)
            pool.wait_ge(zeroed, 2)
            for l in L2:
                if l:
                    zero_bd(l)
                    small_rows(l)
                pool.wait_ge(*act_att(l, "ssq"))
                pool.wait_ge(*dve_att(l, "kmv"))
                pool.tensor_scalar(small[:, 4:6], small[:, 0:2], 1.0 / D_CQ, RMS_EPS, ALU.mult, ALU.add)
                pool.tensor_scalar(small[:, 6:8], ln[:, :, 13], 1.0, LN_EPS, ALU.mult, ALU.add
                                   ).then_inc(*pool_att.inc(l, "eps"))
                pool.wait_ge(*pool_att(l, "eps"))
                pool.tensor_tensor(small[:, 8:12], small[:, 4:8], half[:, 0:4], ALU.pow
                                   ).then_inc(*pool_att.inc(l, "rs"))
                head_norm(GROUPS * l)
                for g in range(GROUPS):
                    r = GROUPS * l + g
                    pool.wait_ge(*dve_prep(r, "arc"))
                    if r:
                        pool.wait_ge(*pe_wkv(r - 1, f"y{NCH - 1}"))
                    pool.wait_ge(*(pool_y(r - 1, "rstd") if g else pool_prep(r, "rn")))
                    steps = [("abd0", a_bd, 0, 0), ("abd1", a_bd, 0, 1), ("rbd0", r_bd, 1, 0), ("rbd", r_bd, 1, 1)]
                    for name, dst, j, h in steps:
                        pool.tensor_copy(dst[q64(h), :, q64(h)], arc[q64(h), :, j, :]).then_inc(*pool_bd.inc(r, name))
                        pool.wait_ge(*pool_bd(r, name))
                    if g + 1 < GROUPS:
                        head_norm(r + 1)
                    pool.wait_ge(*dve_y(r, "v8"))
                    pool.tensor_scalar(g8[:, 3, :], g8[:, 2, :], 1.0 / N_R, GN_EPS, ALU.mult, ALU.add
                                       ).then_inc(*pool_y.inc(r, "eps"))
                    pool.wait_ge(*pool_y(r, "eps"))
                    pool.tensor_tensor(g8[:, 4, :], g8[:, 3, :], half[:, 0:NU], ALU.pow
                                       ).then_inc(*pool_y.inc(r, "rstd"))
                norm_rows(l, "A")
                norm_rsqrt(l, "A")
                norm_rows(l, "B")
                norm_rsqrt(l, "B")

        @block.tensor
        def _(pe):
            def slot(l, kind, i):
                n = SLOT_AT[l, kind, i]
                pe.wait_ge(landed[n % RING], 16 * (n // RING + 1))
                return ring[:, n % RING, :]

            def pair_pieces(l, n, rhs):
                d = pair_at[l, n]
                dst = tok(d % 2)

                def piece(b, name, k0):
                    if b == 0 and k0 == 0 and d >= 2:
                        pe.wait_ge(*pair_free(*pairs[d - 2]))
                    w = slot(l, *name)
                    for kb in range(k0, k0 + 4):
                        mm = pe.matmul(dst[:, b, :], w[:, kb * P:kb * P + P], rhs[:, kb, :],
                                       start=(kb == 0), stop=(kb == KB - 1))
                    if k0:
                        mm.then_inc(slot_used, 1)

                return [lambda b=b, name=name, k0=k0: piece(b, name, k0)
                        for b, name in enumerate(pair_slots(n)) for k0 in (0, 4)]

            def pair(l, n, rhs):
                for p in pair_pieces(l, n, rhs):
                    p()

            def transposed_x(l, w):
                for i in range(4):
                    if i >= 2:
                        pe.wait_ge(*act_x(l, f"{w}{i - 2}"))
                    for b in range(2):
                        for t in range(TT):
                            mm = pe.transpose(tok(i % 2)[:, b, t * P:t * P + P],
                                              x_tok[:, t, (2 * i + b) * P:(2 * i + b + 1) * P], ident)
                    mm.then_inc(*pe_x.inc(l, f"{w}{i}"))

            def prep_1(r):
                l, g = divmod(r, GROUPS)
                if g == 0:
                    pe.wait_ge(*act_lora(l, "tanh"))
                    pe.wait_ge(lora_landed, 32 * (l + 1))
                    pe.wait_ge(*act_att(l, "qT"))
                else:
                    pe.wait_ge(*act_att(l, f"o{g - 1}"))
                for b in range(GB):
                    c = (GB * g + b) * P
                    mm = pe.matmul(tok(6)[:, b, :], lora_w[0:64, 0, c:c + P], lora[0:64, 0, :], start=True, stop=True)
                mm.then_inc(*pe_prep.inc(r, "zw"))
                for b in range(GB):
                    c = (GB * g + b) * P
                    mm = pe.matmul(tok(7)[:, b, :], lora_w[64:128, 0, c:c + P], lora[64:128, 0, :], start=True, stop=True)
                mm.then_inc(*pe_prep.inc(r, "za"))

            def prep_2(r):
                l, g = divmod(r, GROUPS)
                if l:
                    pe.wait_ge(*dve_par(l, "lsig"))
                    pe.wait_ge(*act_prep(r, "thw"))
                    for b in range(GB):
                        c = (GB * g + b) * P
                        mm = pe.matmul(tok(6)[:, b, :], lora_w[:, 2, c:c + P], lora[:, 2, :], start=True, stop=True)
                    mm.then_inc(*pe_prep.inc(r, "zv"))
                pe.wait_ge(*act_prep(r, "tha"))
                pe.wait_ge(*act_prep(r, "kk2"))
                for b in range(GB):
                    for t in range(TT):
                        j = 2 * (TT * b + t)
                        mm = pe.matmul(bank(7)[:, j:j + 2], tmp[:, b, t * P:t * P + P], C["hsel"], start=True, stop=True)
                mm.then_inc(*pe_prep.inc(r, "ss"))

            def prep_3(r):
                pe.wait_ge(*pool_prep(r, "rn"))
                pe.transpose(bank(7)[0:8, 128:256], rn[:, :], ident).then_inc(*pe_prep.inc(r, "rnT"))

            def prep_4(r):
                pe.wait_ge(*dve_prep(r, "rnT"))
                pe.wait_ge(*act_prep(r, "thv" if r >= GROUPS else "thw"))
                for b in range(GB):
                    for t in range(TT):
                        j = TT * b + t
                        mm = pe.matmul(tok(6)[:, b, t * P:t * P + P], C["rowsel"][0:8, j * P:j * P + P], rnT[:, :],
                                       start=True, stop=True)
                mm.then_inc(*pe_prep.inc(r, "rnx"))

            def y_back(r):
                pe.wait_ge(*dve_y(r, "yr"))
                if (r + 1) % GROUPS:
                    pe.wait_ge(*dve_prep(r + 1, "kkn"))
                else:
                    pe.wait_ge(*act_att(r // GROUPS, f"o{GROUPS - 1}"))
                for u in range(NU):
                    mm = pe.matmul(unit64(6)[:, u, :], y_bd[:, u, :], stack, start=True, stop=True)
                mm.then_inc(*pe_yT.inc(r, "yT"))

            def att_logits(l, g):
                r = GROUPS * l + g
                pe.wait_ge(*dve_wkv(r, "bv"))
                pe.wait_ge(*act_wkv(r, "g"))
                for h in range(2):
                    pe.matmul(bank(6)[:, h * T:h * T + T], qT[:, 2 * g + h, P:T], kT[:, :], start=True, stop=True)
                for h in range(2):
                    mm = pe.matmul(bank(7)[:, h * P:h * P + P], qT[:, 2 * g + h, 0:P], kT[:, 0:P], start=True, stop=True)
                mm.then_inc(*pe_att.inc(l, f"lg{g}"))

            def att_probs(l, g):
                pe.wait_ge(*dve_att(l, f"pn{g}"))
                for h in range(2):
                    b = bank(6 + h)
                    pe.transpose(b[:, 0:P], lg[:, 512 + h * P:512 + h * P + P], ident)
                    for s in range(2):
                        mm = pe.transpose(b[:, P + s * P:2 * P + s * P], lg[:, h * T + s * P:h * T + s * P + P], ident)
                mm.then_inc(*pe_att.inc(l, f"pT{g}"))

            def att_values(l, g):
                pe.wait_ge(*act_att(l, f"pT{g}"))
                v0, v1 = p_tok[:, 0, C_V:C_V + DH_A], p_tok[:, 1, C_V:C_V + DH_A]
                for h in range(2):
                    o = tok(6)[:, h, :]
                    pe.matmul(o[:, 0:P], v0, pT[:, h, 0:P], start=True, stop=True)
                    pe.matmul(o[:, P:T], v0, pT[:, h, P:2 * P], start=True, stop=False)
                    mm = pe.matmul(o[:, P:T], v1, pT[:, h, 2 * P:3 * P], start=False, stop=True)
                mm.then_inc(*pe_att.inc(l, f"o{g}"))

            def wkv(r, fill):
                l, g = divmod(r, GROUPS)
                bc = lambda c: [NCH * b + c for b in range(GB)]
                pe.wait_ge(*dve_prep(r, "bneg"))
                if g == 0:
                    pe.wait_ge(zeroed, l + 2)
                    pe.wait_ge(*act_att(l, "s5"))
                else:
                    pe.wait_ge(*act_wkv(r - 1, f"Z{NCH - 1}"))
                    pe.wait_ge(*dve_wkv(r - 1, f"Q{NCH - 1}"))
                rhs = arc[:, :, :, :].rearrange("p u a s -> p u (a s)")
                for u in range(NU):
                    mm = pe.matmul(units(2)[:, u, :], b_bd[:, u, :], rhs[:, u, :], start=True, stop=True)
                mm.then_inc(*pe_wkv.inc(r, "gramB"))
                pe.wait_ge(*dve_prep(r, "kp"))
                if g:
                    pe.wait_ge(*act_y(r - 1, "y"))
                for u in range(NU):
                    mm = pe.matmul(units(4)[:, u, :], k_bd[:, u, :], rhs[:, u, :], start=True, stop=True)
                mm.then_inc(*pe_wkv.inc(r, "gramK"))
                pe.wait_ge(*act_wkv(r, "vbd"))
                pe.wait_ge(*dve_prep(r, "rnT"))
                for u in range(NU):
                    mm = pe.matmul(unit64(7)[:, u, :], v_bd[:, u, :], stack, start=True, stop=True)
                mm.then_inc(*pe_wkv.inc(r, "V"))
                fill(0)
                pe.wait_ge(*dve_wkv(r, "Y0"))
                for u in range(NU):
                    mm = pe.matmul(unit64(2)[:, u, :], nT_bd[:, u, :], stack, start=True, stop=True)
                mm.then_inc(*pe_wkv.inc(r, "nX"))
                fill(1)
                pe.wait_ge(*dve_wkv(r, "Ark"))
                for u in range(NU):
                    mm = pe.transpose(units(4)[:, u, :], b_bd[:, u, :], ident)
                mm.then_inc(*pe_wkv.inc(r, "tokB"))
                fill(2)
                pe.wait_ge(*act_wkv(r, "tokB"))
                for u in range(NU):
                    mm = pe.transpose(units(4)[:, u, :], k_bd[:, u, :], ident)
                mm.then_inc(*pe_wkv.inc(r, "tokK"))
                if g:
                    y_back(r - 1)
                fill(3)
                pe.wait_ge(*dve_prep(r, "rkk"))
                if g:
                    pe.wait_ge(*act_y(r - 1, "yn"))
                pe.matmul(bank(6), C["bones"], flat(tmp), start=True, stop=True).then_inc(*pe_wkv.inc(r, "bonus"))
                pe.wait_ge(*act_wkv(r, "Vc"))
                for b in range(GB):
                    c = (GB * g + b) * P
                    mm = pe.matmul(tok(7)[:, b, :], lora_w[:, 1, c:c + P], lora[:, 1, :], start=True, stop=True)
                mm.then_inc(*pe_wkv.inc(r, "zg"))
                for lev in lv:
                    if lev == 1:
                        pe.wait_ge(*dve_wkv(r, "X0"))
                        pe.wait_ge(*act_wkv(r, "tokK"))
                    else:
                        pe.wait_ge(*dve_wkv(r, f"Y{lev - 1}"))
                    for u in range(NU):
                        mm = pe.matmul(unit64(2)[:, u, :], nT_bd[:, u, :], X[:, u, :], start=True, stop=True)
                    mm.then_inc(*pe_wkv.inc(r, f"W{lev}"))
                    fill(2 + 2 * lev)
                    pe.wait_ge(*act_wkv(r, f"W{lev}"))
                    if lev < LEVELS - 1:
                        for u in range(NU):
                            mm = pe.matmul(unit64(3)[:, u, :], Y_bd[:, u, :], W[:, u, :], start=True, stop=True)
                        mm.then_inc(*pe_wkv.inc(r, f"XW{lev}"))
                    pe.wait_ge(*dve_wkv(r, f"W{lev}"))
                    for u in range(NU):
                        mm = pe.matmul(unit64(4)[:, u, :], W_bd[:, u, :], Y[:, u, :], start=True, stop=True)
                    mm.then_inc(*pe_wkv.inc(r, f"WtY{lev}"))
                    fill(3 + 2 * lev)
                for c in range(NCH):
                    if c == 0:
                        pe.wait_ge(*pool_bd(r, "rbd"))
                        pe.wait_ge(*dve_wkv(r, f"Y{LEVELS - 1}"))
                    else:
                        pe.wait_ge(*dve_wkv(r, f"S{c - 1}"))
                    s_old = S[:, (c + 1) % 2, :, :]
                    for b, u in enumerate(bc(c)):
                        z = bank(2)[:, b * CH:b * CH + CH]
                        if c:
                            pe.matmul(z, a_bd[:, u, :], s_old[:, b, :], start=True, stop=False)
                        mm = pe.matmul(z, ak_bd[:, u, :], Vc[:, u, :], start=(c == 0), stop=True)
                    mm.then_inc(*pe_wkv.inc(r, f"Z{c}"))
                    fill(14 + 2 * c)
                    pe.wait_ge(*act_wkv(r, f"Z{c}"))
                    for b, u in enumerate(bc(c)):
                        mm = pe.matmul(bank(3)[:, b * CH:b * CH + CH], Y_bd[:, u, :], Zs[:, b, :], start=True, stop=True)
                    mm.then_inc(*pe_wkv.inc(r, f"Q{c}"))
                    fill(15 + 2 * c)
                    pe.wait_ge(*dve_wkv(r, f"Q{c}"))
                    if c < NCH - 1:
                        for b, u in enumerate(bc(c)):
                            s_new = bank(4)[:, b * CH:b * CH + CH]
                            pe.matmul(s_new, bt_bd[:, u, :], Qs[:, b, :], start=True, stop=False)
                            mm = pe.matmul(s_new, kt_bd[:, u, :], Vc[:, u, :], start=False, stop=True)
                        mm.then_inc(*pe_wkv.inc(r, f"S{c}"))
                    for b, u in enumerate(bc(c)):
                        y = unit64(5)[:, u, :]
                        pe.matmul(y, rb_bd[:, u, :], Qs[:, b, :], start=True, stop=False)
                        mm = pe.matmul(y, rk_bd[:, u, :], Vc[:, u, :], start=False, stop=(c == 0))
                        if c:
                            mm = pe.matmul(y, r_bd[:, u, :], s_old[:, b, :], start=False, stop=True)
                    mm.then_inc(*pe_wkv.inc(r, f"y{c}"))
                    if g + 1 < GROUPS:
                        [prep_1, prep_2, prep_3, prep_4][c](r + 1)

            pe.wait_ge(inputs_in, 16 * 5)
            for l in L2:
                if l:
                    pe.wait_ge(*dve_x(l - 1, "Bn"))
                transposed_x(l, "T")
                pe.wait_ge(*act_x(l, "T3"))
                for c in range(5):
                    w = slot(l, "att", c)
                    n = min(P, N_ATT - c * P)
                    for t in range(TT):
                        dst = bank(2 + t)[:, c * P:c * P + n] if c < 4 else bank(4)[:, t * P:t * P + n]
                        for kb in range(KB):
                            mm = pe.matmul(dst, xT[:, kb, t * P:t * P + P], w[:, kb * P:kb * P + n],
                                           start=(kb == 0), stop=(kb == KB - 1))
                    mm.then_inc(slot_used, 1)
                pair(l, ("lora", 0), xT)
                if l:
                    w = slot(l, "vres", 0)
                    d = pair_at[l, ("vres", 0)]
                    pe.wait_ge(*pair_free(*pairs[d - 2]))
                    for kb in range(KB):
                        mm = pe.matmul(tok(d % 2)[:, 0, :], w[:, kb * P:kb * P + P], xT[:, kb, :],
                                       start=(kb == 0), stop=(kb == KB - 1))
                    mm.then_inc(slot_used, 1)
                pair(l, ("rkv", 0), xT)
                pe.wait_ge(*dve_att(l, "cq"))
                for kb in range(2):
                    for t in range(TT):
                        mm = pe.transpose(tok(6)[:, kb, t * P:t * P + P], p_tok[:, t, kb * P:kb * P + P], ident)
                mm.then_inc(*pe_att.inc(l, "cqT"))
                pe.wait_ge(*dve_att(l, "rki"))
                for t in range(TT):
                    pe.transpose(bank(7)[:, t * P:t * P + P], p_tok[:, t, C_K:C_K + DH_A], ident)
                for t in range(TT):
                    mm = pe.transpose(bank(7)[:, T + t * P:T + t * P + P],
                                      kid[:, t, :, :].rearrange("p a b -> p (a b)"), ident)
                mm.then_inc(*pe_att.inc(l, "kT"))
                pair(l, ("rkv", 1), xT)
                pe.wait_ge(*act_att(l, "cqT"))
                w = slot(l, "iq", 0)
                for t in range(TT):
                    for kb in range(2):
                        mm = pe.matmul(bank(2 + t), cqT[:, kb, t * P:t * P + P], w[:, kb * 512:kb * 512 + 512],
                                       start=(kb == 0), stop=(kb == 1))
                mm.then_inc(slot_used, 1)
                for j in range(2):
                    w = slot(l, "uq", j)
                    if j:
                        pe.wait_ge(*act_att(l, "kT"))
                    for t in range(TT):
                        for kb in range(2):
                            mm = pe.matmul(bank(4 + 2 * j + t), cqT[:, kb, t * P:t * P + P], w[:, kb * 512:kb * 512 + 512],
                                           start=(kb == 0), stop=(kb == 1))
                    mm.then_inc(slot_used, 1)
                pair(l, ("rkv", 2), xT)
                pe.wait_ge(*dve_att(l, "rqi"))
                for i in range(4):
                    for t in range(TT):
                        mm = pe.transpose(tok(2 + i // 2)[:, i % 2, t * P:t * P + P], qi_tok[:, t, i * P:i * P + P], ident)
                mm.then_inc(*pe_att.inc(l, "qiT"))
                pe.wait_ge(*dve_att(l, "rq1"))
                for h in range(H_A):
                    for t in range(TT):
                        mm = pe.transpose(tok(4 + h // 2)[:, h % 2, t * P:t * P + P],
                                          q_tok[h // 4][:, t, h % 4 * P:h % 4 * P + P], ident)
                mm.then_inc(*pe_att.inc(l, "qT"))
                for i in range(6):
                    pe.wait_ge(*act_att(l, "qiT" if i < 2 else f"s{i - 2}"))
                    heads, t = (range(4 * i, 4 * i + 4), 0) if i < 2 else (range(2 * (i - 2), 2 * (i - 2) + 2), 1)
                    n = T // 2 * (t + 1)
                    for j, h in enumerate(heads):
                        mm = pe.matmul(bank(2 + i % 2)[:, j * n:j * n + n], qiT[:, h // 2, t * P:t * P + P],
                                       kiT[:, h % 2, 0:n], start=True, stop=True)
                    mm.then_inc(*pe_att.inc(l, f"s{i}"))
                r0 = GROUPS * l
                for p in (prep_1, prep_2, prep_3, prep_4):
                    p(r0)
                for g in range(GROUPS):
                    more = []
                    if g + 1 < GROUPS:
                        for t in range(3):
                            more += pair_pieces(l, ("rkv", 3 * (g + 1) + t), xT)
                    else:
                        more += [None] * 8
                    gate = sum([pair_pieces(l, ("gate", 2 * g + i), xT) for i in range(2)], [])
                    gaps = {n: [] for n in range(22)}
                    for n, p in enumerate(more):
                        gaps[n].append(p)
                    for n, p in enumerate(gate):
                        gaps[14 + n].append(p)
                    gaps[6].append(lambda: att_logits(l, g))
                    gaps[9].append(lambda: att_probs(l, g))
                    gaps[11].append(lambda: att_values(l, g))

                    def fill(n):
                        for p in gaps[n]:
                            if p:
                                p()

                    wkv(r0 + g, fill)
                y_back(r0 + GROUPS - 1)
                for i in range(4):
                    pair(l, ("oa", i), oT)
                pe.wait_ge(*dve_y(r0 + GROUPS - 1, "yb"))
                for i in range(4):
                    pair(l, ("ob", i), yb)

                def token_major(kind, n, lhs, wait):
                    for i in range(n):
                        w = slot(l, kind, i)
                        wait(i)
                        for t in range(TT):
                            for j in range(2):
                                mm = pe.matmul(bank(2 + 2 * t + j), lhs(i)[:, t * P:t * P + P], w[:, j * 512:j * 512 + 512],
                                               start=(i == 0), stop=(i == n - 1))
                        mm.then_inc(slot_used, 1)

                token_major("out", KB, lambda i: gates[:, i, :], lambda i: pe.wait_ge(*dve_x(l, f"mix{i // 2}")))
                pe.wait_ge(*dve_x(l, "An"))
                transposed_x(l, "U")
                pe.wait_ge(*act_x(l, "U3"))
                for i in range(FB):
                    pair(l, ("up", i), xT)
                token_major("down", FB, hid, lambda i: pe.wait_ge(*dve_dense(l, ("up", i))))

        @block.scalar
        def _(act):
            def shift_scaled(l, n, dst, blocks):
                act.wait_ge(*pair_done(l, n))
                src = tok(pair_at[l, n] % 2)
                for b, m in enumerate(blocks):
                    last = act.activation(dst[:, b, :], src[:, b, :], ACT.Identity, scale=dp("omu", m))
                last.then_inc(*act_dense.inc(l, n))

            def rkv(l, g, t):
                r = GROUPS * l + g
                if t == 0 and g:
                    act.wait_ge(*dve_wkv(r - 1, "bv"))
                    act.wait_ge(*dve_prep(r - 1, "rkk"))
                dst = [rs[:, :, :], ks[:, :, :], vs(r)][t]
                shift_scaled(l, ("rkv", 3 * g + t), dst, [8 * t + GB * g + b for b in range(GB)])

            def gate(l, i):
                act.wait_ge(*pair_done(l, ("gate", i)))
                src = tok(pair_at[l, ("gate", i)] % 2)
                for b in range(2):
                    last = act.activation(gates[:, 2 * i + b, :], src[:, b, :], ACT.Tanh, scale=0.5,
                                          bias=dp("hgate", 2 * i + b))
                last.then_inc(*act_dense.inc(l, ("gate", i)))

            def xT_out(l, w):
                for i in range(4):
                    act.wait_ge(*pe_x(l, f"{w}{i}"))
                    act.copy(xT[:, 2 * i:2 * i + 2, :], tok(i % 2)).then_inc(*act_x.inc(l, f"{w}{i}"))

            def prep_kk(r):
                l, g = divmod(r, GROUPS)
                act.wait_ge(*dve_dense(l, ("rkv", 3 * g + 1)))
                if r:
                    act.wait_ge(*pe_wkv(r - 1, "bonus"))
                for b in range(GB):
                    last = act.activation(tmp[:, b, :], ks[:, b, :], ACT.Square, scale=cp(l, "k_k", GB * g + b))
                last.then_inc(*act_prep.inc(r, "kk2"))

            def prep_tanh(r, what, bias, dst, src):
                g = r % GROUPS
                act.wait_ge(*pe_prep(r, {"thw": "zw", "tha": "za", "thv": "zv"}[what]))
                for b in range(GB):
                    last = act.activation(dst[:, b, :], tok(src)[:, b, :], ACT.Tanh, scale=0.5, bias=dp(bias, GB * g + b))
                last.then_inc(*act_prep.inc(r, what))

            def prep_exp(r):
                g = r % GROUPS
                act.wait_ge(*dve_prep(r, "cp"))
                act.activation(flat(dA), flat(dB), ACT.Exp, scale=-DECAY).then_inc(*act_prep.inc(r, "P"))
                act.activation(flat(dC), flat(dC), ACT.Exp, scale=-DECAY).then_inc(*act_prep.inc(r, "Pp"))
                act.activation(flat(dB), flat(dB), ACT.Exp, scale=DECAY).then_inc(*act_prep.inc(r, "iP"))
                act.wait_ge(*pe_prep(r, "ss"))
                act.wait_ge(*act_prep(r, "tha"))
                for b in range(GB):
                    last = act.activation(tmp[:, b, :], tha[:, b, :], ACT.Identity, scale=dp("hka", GB * g + b),
                                          bias=dp("omhka", GB * g + b))
                last.then_inc(*act_prep.inc(r, "kt"))

            def y_norm(r):
                l, g = divmod(r, GROUPS)
                act.wait_ge(*pe_yT(r, "yT"))
                for b in range(GB):
                    last = act.activation(yt[:, NCH * b:NCH * b + NCH, :].rearrange("p c s -> p (c s)"), tok(6)[:, b, :],
                                          ACT.Identity, scale=cp(l, "g_lnx", GB * g + b), bias=cp(l, "b_lnx", GB * g + b))
                last.then_inc(*act_y.inc(r, "yn"))

            def att_exp(l, g):
                act.wait_ge(*dve_att(l, f"mx{g}"))
                for j in range(4):
                    a, n = (j * T, T) if j < 2 else (2 * T + (j - 2) * P, P)
                    last = act.activation(lg[:, a:a + n], lg[:, a:a + n], ACT.Exp, bias=small[:, 32 + j:33 + j],
                                          accum_out=small[:, 36 + j:37 + j])
                last.then_inc(*act_att.inc(l, f"e{g}"))

            def att_pT(l, g):
                act.wait_ge(*pe_att(l, f"pT{g}"))
                act.copy(pT, ps[:, 6:8, 0:384]).then_inc(*act_att.inc(l, f"pT{g}"))

            def att_o(l, g):
                act.wait_ge(*pe_att(l, f"o{g}"))
                act.copy(oT[:, 2 * g:2 * g + 2, :], tok(6)).then_inc(*act_att.inc(l, f"o{g}"))

            def levels(r, lev):
                act.wait_ge(*pe_wkv(r, f"W{lev}"))
                if lev > 1:
                    act.wait_ge(*pe_wkv(r, f"WtY{lev - 1}"))
                act.copy(W[:, :, :], unit64(2))
                act.copy(W_bd[q64(0), :, q64(0)], unit64(2)[q64(0)]).then_inc(*act_wkv.inc(r, f"W{lev}"))

            def z_out(r, c):
                act.wait_ge(*pe_wkv(r, f"Z{c}"))
                act.copy(Zs[:, :, :], bank(2)[:, 0:GB * CH].rearrange("p (b s) -> p b s", s=CH)
                         ).then_inc(*act_wkv.inc(r, f"Z{c}"))

            act.wait_ge(tables, 1)
            act.activation(sines[:, 0, :, :], ang[:, 0, :, :], ACT.Sin)
            act.activation(sines[:, 1, :, :], ang[:, 1, :, :], ACT.Sin).then_inc(tables, 1)
            for l in L2:
                r0 = GROUPS * l
                xT_out(l, "T")
                act.wait_ge(*used(l, "att", 4))
                for t in range(TT):
                    act.copy(p_tok[:, t, 0:512], bank(2 + t))
                act.copy(p_tok[:, :, 512:N_ATT], bank(4)[:, 0:T].rearrange("p (t n) -> p t n", t=TT)[:, :, 0:N_ATT - 512]
                         ).then_inc(*act_att.inc(l, "p"))
                act.wait_ge(*act_att(l, "p"))
                for t in range(TT):
                    last = act.activation(scratch[:, t * D_CQ:t * D_CQ + D_CQ], p_tok[:, t, 0:D_CQ], ACT.Square,
                                          accum_out=small[:, t:t + 1])
                last.then_inc(*act_att.inc(l, "ssq"))
                act.wait_ge(*dve_par(l, "dpar"))
                shift_scaled(l, ("lora", 0), lora[:, 0:2, :], [24, 25])
                act.wait_ge(*dve_dense(l, ("lora", 0)))
                act.activation(lora[0:64, 0, :], lora[0:64, 0, :], ACT.Tanh)
                act.activation(lora[:, 1, :], lora[:, 1, :], ACT.Tanh, scale=0.5).then_inc(*act_lora.inc(l, "tanh"))
                if l:
                    shift_scaled(l, ("vres", 0), lora[:, 2:3, :], [26])
                rkv(l, 0, 0)
                act.wait_ge(*pe_att(l, "cqT"))
                for kb in range(2):
                    last = act.activation(cqT[:, kb, :], tok(6)[:, kb, :], ACT.Identity, scale=cp(l, "g_cq", kb))
                last.then_inc(*act_att.inc(l, "cqT"))
                act.wait_ge(*pe_att(l, "kT"))
                act.wait_ge(zeroed, l + 2)
                act.copy(kT[:, :], bank(7)[:, 0:T])
                act.copy(kiT[q64(0), 0, :], bank(7)[q64(0), T:2 * T])
                act.copy(kiT[q64(1), 1, :], bank(7)[q64(1), T:2 * T]).then_inc(*act_att.inc(l, "kT"))
                rkv(l, 0, 1)
                act.wait_ge(*used(l, "iq", 0))
                for t in range(TT):
                    last = act.copy(qi_tok[:, t, :], bank(2 + t))
                last.then_inc(*act_att.inc(l, "qi"))
                for j in range(2):
                    act.wait_ge(*used(l, "uq", j))
                    for t in range(TT):
                        last = act.copy(q_tok[j][:, t, :], bank(4 + 2 * j + t))
                    last.then_inc(*act_att.inc(l, f"q{j}"))
                rkv(l, 0, 2)
                act.wait_ge(*pe_att(l, "qiT"))
                for i in range(2):
                    last = act.copy(qiT[:, 2 * i:2 * i + 2, :], tok(2 + i))
                last.then_inc(*act_att.inc(l, "qiT"))
                act.wait_ge(*pe_att(l, "qT"))
                for i in range(4):
                    last = act.copy(qT[:, 2 * i:2 * i + 2, :], tok(4 + i))
                last.then_inc(*act_att.inc(l, "qT"))
                for i in range(6):
                    act.wait_ge(*pe_att(l, f"s{i}"))
                    if i >= 2:
                        act.wait_ge(*dve_att(l, f"s0{4 * i - 5}" if i < 4 else f"s1{2 * (i - 4) + 1}"))
                    act.activation(rel[:, i % 2, :], bank(2 + i % 2), ACT.Relu).then_inc(*act_att.inc(l, f"s{i}"))
                prep_kk(r0)
                prep_tanh(r0, "thw", "hw0", dA, 6)
                prep_tanh(r0, "tha", "ha0", tha, 7)
                prep_exp(r0)
                if l:
                    prep_tanh(r0, "thv", "hv0", kkn, 6)
                for g in range(GROUPS):
                    r = r0 + g
                    nxt = g + 1 < GROUPS
                    if r:
                        act.wait_ge(*pe_wkv(r - 1, f"y{NCH - 1}"))
                    for h in range(2):
                        act.copy(Y_bd[q64(h), :, q64(h)], stack[q64(h)].unsqueeze(1).broadcast_to([64, NU, CH]))
                    act.copy(Y[:, :, :], stack.unsqueeze(1).broadcast_to([P, NU, CH]))
                    act.copy(X[:, :, :], stack.unsqueeze(1).broadcast_to([P, NU, CH])).then_inc(*act_wkv.inc(r, "reset"))
                    act.wait_ge(*(dve_prep(r, "v") if l else dve_dense(l, ("rkv", 3 * g + 2))))
                    for h in range(2):
                        last = act.copy(v_bd[q64(h), :, q64(h)], by_unit(vs(r))[q64(h)])
                    last.then_inc(*act_wkv.inc(r, "vbd"))
                    act.wait_ge(*pe_wkv(r, "V"))
                    act.copy(Vc[:, :, :], unit64(7)).then_inc(*act_wkv.inc(r, "Vc"))
                    act.wait_ge(*pe_wkv(r, "tokB"))
                    for k in range(2):
                        last = act.copy(bt_bd[:, 4 * k:4 * k + 4, :], units(4)[:, 4 * k:4 * k + 4, :])
                    last.then_inc(*act_wkv.inc(r, "tokB"))
                    act.wait_ge(*pe_wkv(r, "tokK"))
                    for k in range(2):
                        last = act.copy(kt_bd[:, 4 * k:4 * k + 4, :], units(4)[:, 4 * k:4 * k + 4, :])
                    last.then_inc(*act_wkv.inc(r, "tokK"))
                    if g:
                        y_norm(r - 1)
                    act.wait_ge(*pe_wkv(r, "zg"))
                    if g:
                        act.wait_ge(*dve_y(r - 1, "yb"))
                    act.copy(gT[:, :, :], tok(7)).then_inc(*act_wkv.inc(r, "g"))
                    if nxt:
                        rkv(l, g + 1, 0)
                    levels(r, 1)
                    levels(r, 2)
                    levels(r, 3)
                    att_exp(l, g)
                    if nxt:
                        rkv(l, g + 1, 1)
                    levels(r, 4)
                    att_pT(l, g)
                    levels(r, 5)
                    att_o(l, g)
                    if nxt:
                        rkv(l, g + 1, 2)
                        prep_kk(r + 1)
                    z_out(r, 0)
                    if nxt:
                        prep_tanh(r + 1, "thw", "hw0", dA, 6)
                        prep_tanh(r + 1, "tha", "ha0", tha, 7)
                    z_out(r, 1)
                    if nxt:
                        prep_exp(r + 1)
                    gate(l, 2 * g)
                    if nxt and l:
                        prep_tanh(r + 1, "thv", "hv0", kkn, 6)
                    z_out(r, 2)
                    z_out(r, 3)
                    gate(l, 2 * g + 1)
                    act.wait_ge(*pe_wkv(r, f"y{NCH - 1}"))
                    act.copy(yt[:, :, :], unit64(5)).then_inc(*act_y.inc(r, "y"))
                    act.wait_ge(*dve_y(r, "yc"))
                    act.activation(sq[:, :, :], yt[:, :, :], ACT.Square).then_inc(*act_y.inc(r, "sq"))
                y_norm(r0 + GROUPS - 1)
                act.mul(flat(x_tok), flat(x_tok), ALPHA).then_inc(*act_x.inc(l, "Aax"))
                xT_out(l, "U")
                act.mul(flat(x_tok), flat(x_tok), ALPHA).then_inc(*act_x.inc(l, "Bax"))
                for i in range(FB):
                    n = ("up", i)
                    act.wait_ge(*pair_done(l, n))
                    if i >= 2:
                        act.wait_ge(*dve_dense(l, ("up", i - 2)))
                    c = conv[i % 2][:, 0, :]
                    act.activation(c, tok(pair_at[l, n] % 2)[:, 0, :], ACT.Identity, scale=cp(l, "conv_w", 2 * FB + i),
                                   bias=cp(l, "conv_b", i)).then_inc(*act_dense.inc(l, n))
                    act.wait_ge(*dve_dense(l, (n, "conv")))
                    act.activation(conv[i % 2][:, 1, :], c, ACT.Tanh, scale=0.5).then_inc(*act_dense.inc(l, (n, "tanh")))

        @block.vector
        def _(dve):
            def shift_add(l, n, dst, blocks):
                dve.wait_ge(*act_dense(l, n))
                src = tok(pair_at[l, n] % 2)
                for b, m in enumerate(blocks):
                    last = dve.scalar_tensor_tensor(out=dst[:, b, 1:T], in0=src[:, b, 0:T - 1], scalar=cp(l, "mu", m),
                                                    in1=dst[:, b, 1:T], op0=ALU.mult, op1=ALU.add)
                last.then_inc(*dve_dense.inc(l, n))

            def rkv(l, g, t):
                dst = [rs[:, :, :], ks[:, :, :], vs(GROUPS * l + g)][t]
                shift_add(l, ("rkv", 3 * g + t), dst, [8 * t + GB * g + b for b in range(GB)])

            def rotate(l, name, x1, x2, f0, nf, heads, out1=None, out2=None):
                o1, o2 = out1 or x1, out2 or x2
                n = TT * heads * nf
                t = [yt[:, :, :].rearrange("p u s -> p (u s)")[:, 0:n], sq[:, :, :].rearrange("p u s -> p (u s)")[:, 0:n],
                     X[:, :, :].rearrange("p u s -> p (u s)")[:, 0:n], Y[:, :, :].rearrange("p u s -> p (u s)")[:, 0:n]]
                t = [a.rearrange("p (t h f) -> p t h f", t=TT, h=heads) for a in t]
                sin, cos = [sines[:, i, :, f0:f0 + nf].unsqueeze(2).broadcast_to([P, TT, heads, nf]) for i in range(2)]
                dve.tensor_tensor(t[0], x1, cos, ALU.mult)
                dve.tensor_tensor(t[1], x2, sin, ALU.mult)
                dve.tensor_tensor(t[2], x2, cos, ALU.mult)
                dve.tensor_tensor(t[3], x1, sin, ALU.mult).then_inc(*dve_att.inc(l, f"{name}a"))
                dve.wait_ge(*dve_att(l, f"{name}a"))
                dve.tensor_tensor(o1, t[0], t[1], ALU.subtract)
                return dve.tensor_tensor(o2, t[2], t[3], ALU.add)

            def prep_decay(r):
                if r:
                    dve.wait_ge(*dve_wkv(r - 1, "bv"))
                dve.wait_ge(*act_prep(r, "thw"))
                dve.tensor_scalar(flat(dA), flat(dA), 0.5, 0.5, ALU.mult, ALU.add).then_inc(*dve_prep.inc(r, "s"))
                dve.wait_ge(*dve_prep(r, "s"))
                dve.tensor_tensor_scan(flat(dB), C["scan"], flat(dA), 0.0, ALU.mult, ALU.add).then_inc(*dve_prep.inc(r, "cum"))
                dve.wait_ge(*dve_prep(r, "cum"))
                dve.tensor_tensor(flat(dC), flat(dB), flat(dA), ALU.subtract).then_inc(*dve_prep.inc(r, "cp"))

            def prep_sum(r):
                dve.wait_ge(*act_prep(r, "P"))
                dve.tensor_copy(pend[:, r % 2, :, :], dA[:, :, CH - 1::CH]).then_inc(*dve_prep.inc(r, "pend"))
                dve.wait_ge(*pe_prep(r, "ss"))
                dve.tensor_scalar(ssm[:, :], bank(7)[:, 0:8], 1e-24, None, ALU.max).then_inc(*dve_prep.inc(r, "ss"))

            def prep_rn(r):
                dve.wait_ge(*pe_prep(r, "rnT"))
                dve.tensor_copy(rnT[:, :], bank(7)[0:8, 128:256]).then_inc(*dve_prep.inc(r, "rnT"))
                if r >= GROUPS:
                    g = r % GROUPS
                    dve.wait_ge(*act_prep(r, "thv"))
                    if g:
                        dve.wait_ge(*pe_att(r // GROUPS, f"o{g - 1}"))
                    dve.tensor_tensor(y_bd_free(r), flat2(v_first[:, GB * g:GB * g + GB, :]), flat(vs_own), ALU.subtract
                                      ).then_inc(*dve_prep.inc(r, "v1"))
                    dve.wait_ge(*dve_prep(r, "v1"))
                    dve.scalar_tensor_tensor(out=y_bd_free(r), in0=flat(kkn), scalar=1.0, in1=y_bd_free(r), op0=ALU.add,
                                             op1=ALU.mult).then_inc(*dve_prep.inc(r, "v2"))
                    dve.wait_ge(*dve_prep(r, "v2"))
                    dve.scalar_tensor_tensor(out=flat(vs_own), in0=y_bd_free(r), scalar=0.5, in1=flat(vs_own), op0=ALU.mult,
                                             op1=ALU.add).then_inc(*dve_prep.inc(r, "v"))

            def y_bd_free(r):
                return vtmp[:, :]

            def flat2(t):
                return t.rearrange("p a b -> p (a b)")

            def prep_rest(r):
                l, g = divmod(r, GROUPS)
                dve.wait_ge(*pe_prep(r, "rnx"))
                for b in range(GB):
                    last = dve.scalar_tensor_tensor(out=kkn[:, b, :], in0=ks[:, b, :], scalar=cp(l, "k_k", GB * g + b),
                                                    in1=tok(6)[:, b, :], op0=ALU.mult, op1=ALU.mult)
                last.then_inc(*dve_prep.inc(r, "kkn"))
                dve.wait_ge(*act_prep(r, "kt"))
                dve.wait_ge(*dve_prep(r, "kkn"))
                dve.tensor_tensor(flat(ks), flat(ks), flat(tmp), ALU.mult).then_inc(*dve_prep.inc(r, "k2"))
                dve.scalar_tensor_tensor(out=flat(tha), in0=flat(tha), scalar=1.0, in1=flat(kkn), op0=ALU.add, op1=ALU.mult
                                         ).then_inc(*dve_prep.inc(r, "kb"))
                dve.tensor_tensor(arc[:, :, 0, :], by_unit(kkn[:, :, :]), by_unit(dC[:, :, :]), ALU.mult)
                dve.tensor_tensor(arc[:, :, 1, :], by_unit(rs[:, :, :]), by_unit(dA[:, :, :]), ALU.mult
                                  ).then_inc(*dve_prep.inc(r, "arc"))
                if g == 0:
                    dve.wait_ge(zeroed, l + 2)
                dve.wait_ge(*act_prep(r, "iP"))
                dve.wait_ge(*dve_prep(r, "kb"))
                for h in range(2):
                    last = dve.scalar_tensor_tensor(out=b_bd[q64(h), :, q64(h)], in0=by_unit(tha[:, :, :])[q64(h)], scalar=-0.5,
                                                    in1=by_unit(dB[:, :, :])[q64(h)], op0=ALU.mult, op1=ALU.mult)
                last.then_inc(*dve_prep.inc(r, "bneg"))
                for h in range(2):
                    last = dve.tensor_tensor(k_bd[q64(h), :, q64(h)], by_unit(ks[:, :, :])[q64(h)],
                                             by_unit(dB[:, :, :])[q64(h)], ALU.mult)
                last.then_inc(*dve_prep.inc(r, "kp"))

            def prep_bonus(r):
                l, g = divmod(r, GROUPS)
                dve.wait_ge(*dve_prep(r, "kp"))
                for b in range(GB):
                    last = dve.scalar_tensor_tensor(out=tmp[:, b, :], in0=rs[:, b, :], scalar=cp(l, "r_k", GB * g + b),
                                                    in1=ks[:, b, :], op0=ALU.mult, op1=ALU.mult)
                last.then_inc(*dve_prep.inc(r, "rkk"))

            def masked(r, name, dst, src, half_, mask):
                for h in range(2):
                    last = dve.tensor_tensor(dst[q64(h), :, q64(h)], units(src)[q64(h), :, half_ * CH:half_ * CH + CH],
                                             mask[q64(h)].unsqueeze(1).broadcast_to([64, NU, CH]), ALU.mult)
                last.then_inc(*dve_wkv.inc(r, name))

            def mask_of(which, lev, q=slice(0, P)):
                m = masks[q, which, lev, :]
                return m.unsqueeze(1).broadcast_to([q.stop - q.start, NU, CH])

            def grams(r):
                dve.wait_ge(*pe_wkv(r, "gramB"))
                if r % GROUPS == 0:
                    dve.wait_ge(zeroed, r // GROUPS + 2)
                masked(r, "nT", nT_bd, 2, 0, C["strict"])
                masked(r, "Arb", rb_bd, 2, 1, C["incl"])
                dve.wait_ge(*act_wkv(r, "reset"))
                dve.copy_predicated(Y[:, :, :], mask_of(0, 0), units(2)[:, :, 0:CH])
                for h in range(2):
                    last = dve.copy_predicated(Y_bd[q64(h), :, q64(h)], mask_of(0, 0, q64(h)), units(2)[q64(h), :, 0:CH])
                last.then_inc(*dve_wkv.inc(r, "Y0"))
                dve.wait_ge(*pe_wkv(r, "gramK"))
                masked(r, "Aak", ak_bd, 4, 0, C["strict"])
                masked(r, "Ark", rk_bd, 4, 1, C["incl"])
                dve.wait_ge(*pe_wkv(r, "nX"))
                dve.copy_predicated(X[:, :, :], mask_of(1, 0), unit64(2)).then_inc(*dve_wkv.inc(r, "X0"))

            def level(r, lev):
                dve.wait_ge(*act_wkv(r, f"W{lev}"))
                dve.tensor_copy(W_bd[q64(1), :, q64(1)], unit64(2)[q64(1)]).then_inc(*dve_wkv.inc(r, f"W{lev}"))
                if lev < LEVELS - 1:
                    dve.wait_ge(*pe_wkv(r, f"XW{lev}"))
                    dve.copy_predicated(X[:, :, :], mask_of(1, lev), unit64(3)).then_inc(*dve_wkv.inc(r, f"X{lev}"))
                dve.wait_ge(*pe_wkv(r, f"WtY{lev}"))
                if lev < LEVELS - 1:
                    dve.copy_predicated(Y[:, :, :], mask_of(0, lev), unit64(4))
                for h in range(2):
                    last = dve.copy_predicated(Y_bd[q64(h), :, q64(h)], mask_of(0, lev, q64(h)), unit64(4)[q64(h)])
                last.then_inc(*dve_wkv.inc(r, f"Y{lev}"))

            def chunk(r, c):
                two = lambda n: bank(n)[:, 0:GB * CH].rearrange("p (b s) -> p b s", s=CH)
                dve.wait_ge(*pe_wkv(r, f"Q{c}"))
                dve.tensor_copy(Qs[:, :, :], two(3)).then_inc(*dve_wkv.inc(r, f"Q{c}"))
                if c < NCH - 1:
                    src = two(4)
                    dve.wait_ge(*pe_wkv(r, f"S{c}"))
                    if c:
                        dve.tensor_tensor(Sa[:, :, :], src, S[:, (c + 1) % 2, :, :], ALU.add
                                          ).then_inc(*dve_wkv.inc(r, f"S{c}a"))
                        dve.wait_ge(*dve_wkv(r, f"S{c}a"))
                        src = Sa[:, :, :]
                    dve.tensor_tensor(S[:, c % 2, :, :], src, pend[:, r % 2, :, c:c + 1].broadcast_to([P, GB, CH]), ALU.mult
                                      ).then_inc(*dve_wkv.inc(r, f"S{c}"))

            def y_center(r):
                dve.wait_ge(*act_y(r, "y"))
                dve.tensor_reduce(g8[:, 0, :], yt[:, :, :], AX, ALU.add).then_inc(*dve_y.inc(r, "m"))
                dve.wait_ge(*dve_y(r, "m"))
                dve.tensor_scalar(g8[:, 1, :], g8[:, 0, :], -1.0 / N_R, None, ALU.mult).then_inc(*dve_y.inc(r, "m2"))
                dve.wait_ge(*dve_y(r, "m2"))
                dve.tensor_tensor(yt[:, :, :], yt[:, :, :], g8[:, 1, :].unsqueeze(2).broadcast_to([P, NU, CH]), ALU.add
                                  ).then_inc(*dve_y.inc(r, "yc"))

            def y_var(r):
                dve.wait_ge(*act_y(r, "sq"))
                dve.tensor_reduce(g8[:, 2, :], sq[:, :, :], AX, ALU.add).then_inc(*dve_y.inc(r, "v8"))

            def y_scale(r):
                dve.wait_ge(*pool_y(r, "rstd"))
                for h in range(2):
                    last = dve.tensor_tensor(y_bd[q64(h), :, q64(h)], yt[q64(h), :, :],
                                             g8[q64(h), 4, :].unsqueeze(2).broadcast_to([64, NU, CH]), ALU.mult)
                last.then_inc(*dve_y.inc(r, "yr"))

            def y_out(r):
                g = r % GROUPS
                dve.wait_ge(*act_y(r, "yn"))
                dve.tensor_tensor(flat(yt), flat(yt), flat(bv), ALU.add).then_inc(*dve_y.inc(r, "yb1"))
                dve.wait_ge(*dve_y(r, "yb1"))
                dve.tensor_tensor(flat2(yb[:, GB * g:GB * g + GB, :]), flat(yt), flat(gT), ALU.mult
                                  ).then_inc(*dve_y.inc(r, "yb"))

            def bonus(r):
                dve.wait_ge(*pe_wkv(r, "bonus"))
                dve.tensor_tensor(flat(bv), bank(6), flat2(vs(r)), ALU.mult).then_inc(*dve_wkv.inc(r, "bv"))

            def att_masked(l, g):
                dve.wait_ge(*pe_att(l, f"lg{g}"))
                if g == 0:
                    dve.wait_ge(*dve_att(l, "keep1"))
                for t, a, n in ((1, 0, T), (0, 2 * T, P)):
                    last = dve.scalar_tensor_tensor(
                        out=lg[:, a:a + 2 * n].rearrange("p (h s) -> p h s", h=2),
                        in0=bank(7 - t)[:, 0:2 * n].rearrange("p (h s) -> p h s", h=2), scalar=DH_A ** -0.5,
                        in1=keep[:, t, 0:n].unsqueeze(1).broadcast_to([P, 2, n]), op0=ALU.mult, op1=ALU.add)
                last.then_inc(*dve_att.inc(l, f"lg{g}"))
                dve.wait_ge(*dve_att(l, f"lg{g}"))
                for j, a, n in ((32, 0, T), (34, 2 * T, P)):
                    last = dve.tensor_reduce(small[:, j:j + 2], lg[:, a:a + 2 * n].rearrange("p (h s) -> p h s", h=2), AX,
                                             ALU.max, negate=True)
                last.then_inc(*dve_att.inc(l, f"mx{g}"))

            def att_norm(l, g):
                dve.wait_ge(*act_att(l, f"e{g}"))
                dve.reciprocal(small[:, 40:44], small[:, 36:40]).then_inc(*dve_att.inc(l, f"rc{g}"))
                dve.wait_ge(*dve_att(l, f"rc{g}"))
                for j in range(4):
                    a, n = (j * T, T) if j < 2 else (2 * T + (j - 2) * P, P)
                    last = dve.tensor_scalar(lg[:, a:a + n], lg[:, a:a + n], small[:, 40 + j:41 + j], None, ALU.mult)
                last.then_inc(*dve_att.inc(l, f"pn{g}"))

            def layer_norm(l, w, kind, n):
                s = 0.5 if w == "A" else 1.0
                i = 2 * l + "AB".index(w)
                dve.wait_ge(*used(l, kind, n - 1))
                dve.wait_ge(*act_x(l, f"{w}ax"))
                for t in range(TT):
                    for j in range(2):
                        c = slice(512 * j, 512 * j + 512)
                        last = dve.scalar_tensor_tensor(out=x_tok[:, t, c], in0=bank(2 + 2 * t + j), scalar=s,
                                                        in1=x_tok[:, t, c], op0=ALU.mult, op1=ALU.add)
                last.then_inc(*dve_x.inc(l, f"{w}add"))
                dve.wait_ge(*dve_x(l, f"{w}add"))
                for t in range(TT):
                    for j in range(2):
                        last = dve.bn_stats(ln[:, t, 6 * j:6 * j + 6], x_tok[:, t, 512 * j:512 * j + 512])
                last.then_inc(*dve_x.inc(l, f"{w}st"))
                dve.wait_ge(*dve_x(l, f"{w}st"))
                for t in range(TT):
                    last = dve.bn_aggr(ln[:, t, 12:14], ln[:, t, 0:12])
                last.then_inc(*dve_x.inc(l, f"{w}mv"))
                dve.wait_ge(*dve_x(l, f"{w}mv"))
                dve.wait_ge(rows_landed, 32 * (i + 1))
                for t in range(TT):
                    last = dve.scalar_tensor_tensor(out=x_tok[:, t, :], in0=x_tok[:, t, :], scalar=ln[:, t, 12:13],
                                                    in1=lnrow[0], op0=ALU.subtract, op1=ALU.mult)
                last.then_inc(*dve_x.inc(l, f"{w}c"))
                dve.wait_ge(*dve_x(l, f"{w}c"))
                dve.wait_ge(*pool_x(l, w))
                for t in range(TT):
                    last = dve.scalar_tensor_tensor(out=x_tok[:, t, :], in0=x_tok[:, t, :], scalar=ln[:, t, 21:22],
                                                    in1=lnrow[1], op0=ALU.mult, op1=ALU.add)
                last.then_inc(*dve_x.inc(l, f"{w}n"))

            turn = 2 * math.pi
            c1 = 6.28125
            c2 = 0.0019340515136718750
            c3 = turn - c1 - c2
            magic = 1.5 * 2 ** 23
            dve.wait_ge(inputs_in, 16 * 5)
            dve.tensor_copy(posf[:, :], pos[:, :]).then_inc(tables_dve, 1)
            dve.wait_ge(tables_dve, 1)
            for t in range(TT):
                last = dve.tensor_scalar(ang[:, 0, t, :], C["freq"], posf[:, t:t + 1], None, ALU.mult)
            last.then_inc(tables_dve, 1)
            dve.wait_ge(tables_dve, 2)
            a0, a1 = ang[:, 0, :, :], ang[:, 1, :, :]
            dve.tensor_scalar(a1, a0, 1.0 / turn, magic, ALU.mult, ALU.add).then_inc(tables_dve, 1)
            dve.wait_ge(tables_dve, 3)
            dve.tensor_scalar(a1, a1, magic, None, ALU.subtract).then_inc(tables_dve, 1)
            for i, c in enumerate((c1, c2, c3)):
                dve.wait_ge(tables_dve, 4 + i)
                dve.scalar_tensor_tensor(out=a0, in0=a1, scalar=-c, in1=a0, op0=ALU.mult, op1=ALU.add).then_inc(tables_dve, 1)
            dve.wait_ge(tables_dve, 7)
            dve.tensor_scalar(a0, a0, math.pi, -math.pi, ALU.min, ALU.max).then_inc(tables_dve, 1)
            dve.wait_ge(tables_dve, 8)
            dve.scalar_tensor_tensor(out=a1, in0=a0, scalar=-1.0, in1=a0, op0=ALU.mult, op1=ALU.max).then_inc(tables_dve, 1)
            dve.wait_ge(tables_dve, 9)
            dve.tensor_scalar(a1, a1, -1.0, math.pi / 2, ALU.mult, ALU.add).then_inc(tables, 1)

            for l in L2:
                r0 = GROUPS * l
                if l:
                    dve.wait_ge(*act_dense(l - 1, ("gate", 7)))
                dve.tensor_scalar(dp("omu", 0, 27), cp(l, "mu", 0, 27), -1.0, 1.0, ALU.mult, ALU.add)
                for a, b, n in (("hw0", "w0", 8), ("ha0", "a0", 8), ("hv0", "v0", 8), ("hgate", "b_gate", 16), ("hka", "k_a", 8)):
                    dve.tensor_scalar(dp(a, 0, n), cp(l, b, 0, n), 0.5, None, ALU.mult)
                dve.tensor_scalar(dp("omhka", 0, 8), cp(l, "k_a", 0, 8), -0.5, 1.0, ALU.mult, ALU.add
                                  ).then_inc(*dve_par.inc(l, "dpar"))
                dve.wait_ge(*act_att(l, "p"))
                dve.tensor_scalar(p_tok[:, :, C_IW:C_IW + H_IDX], p_tok[:, :, C_IW:C_IW + H_IDX],
                                  H_IDX ** -0.5 * D_IDX ** -0.5, None, ALU.mult).then_inc(*dve_att.inc(l, "wi"))
                for t in range(TT):
                    last = dve.bn_stats(ln[:, t, 0:6], p_tok[:, t, C_IK:C_IK + D_IDX])
                last.then_inc(*dve_att.inc(l, "kst"))
                dve.wait_ge(*dve_att(l, "kst"))
                for t in range(TT):
                    last = dve.bn_aggr(ln[:, t, 12:14], ln[:, t, 0:6])
                last.then_inc(*dve_att.inc(l, "kmv"))
                dve.wait_ge(tables, 2)
                kv = p_tok[:, :, C_K:C_K + ROT_A].rearrange("p t (h f) -> p t h f", h=1)
                if l:
                    dve.wait_ge(*act_y(r0 - 1, "yn"))
                rotate(l, "rk", kv[:, :, :, 0:16], kv[:, :, :, 16:32], 0, 16, 1).then_inc(*dve_att.inc(l, "rk"))
                shift_add(l, ("lora", 0), lora[:, 0:2, :], [24, 25])
                dve.wait_ge(*pool_att(l, "rs"))
                for t in range(TT):
                    last = dve.tensor_scalar(p_tok[:, t, 0:D_CQ], p_tok[:, t, 0:D_CQ], small[:, 8 + t:9 + t], None, ALU.mult)
                last.then_inc(*dve_att.inc(l, "cq"))
                dve.wait_ge(lora_landed, 32 * (l + 1))
                ik = p_tok[:, :, C_IK:C_IK + D_IDX]
                for t in range(TT):
                    last = dve.scalar_tensor_tensor(out=ik[:, t, :], in0=ik[:, t, :], scalar=ln[:, t, 12:13],
                                                    in1=kirow[:, 0:D_IDX], op0=ALU.subtract, op1=ALU.mult)
                last.then_inc(*dve_att.inc(l, "kic"))
                dve.wait_ge(*dve_att(l, "kic"))
                for t in range(TT):
                    last = dve.scalar_tensor_tensor(out=ik[:, t, :], in0=ik[:, t, :], scalar=small[:, 10 + t:11 + t],
                                                    in1=kirow[:, D_IDX:2 * D_IDX], op0=ALU.mult, op1=ALU.add)
                last.then_inc(*dve_att.inc(l, "ki"))
                dve.wait_ge(*dve_att(l, "ki"))
                dve.wait_ge(*dve_att(l, "rk"))
                ikh = ik.rearrange("p t (h f) -> p t h f", h=1)
                rotate(l, "rki", ikh[:, :, :, 0:8], ikh[:, :, :, 8:16], 16, 8, 1,
                       out1=kid[:, :, 0:1, 0:8], out2=kid[:, :, 0:1, 8:16])
                dve.tensor_copy(kid[:, :, 0, 16:64], ik[:, :, 16:64]).then_inc(kid_half, 1)
                dve.wait_ge(kid_half, l + 1)
                dve.tensor_copy(kid[:, :, 1, :], kid[:, :, 0, :]).then_inc(*dve_att.inc(l, "rki"))
                dve.wait_ge(*act_lora(l, "tanh"))
                dve.tensor_scalar(lora[:, 1, :], lora[:, 1, :], 0.5, 0.5, ALU.mult, ALU.add)
                if l:
                    shift_add(l, ("vres", 0), lora[:, 2:3, :], [26])
                rkv(l, 0, 0)
                dve.tensor_copy(vtmp[:, 0:1], const[:, 0:1]).then_inc(*dve_par.inc(l, "lsig"))
                rkv(l, 0, 1)
                dve.wait_ge(*act_att(l, "qi"))
                qv = qi_tok.rearrange("p t (h f) -> p t h f", h=H_IDX)
                rotate(l, "rqi", qv[:, :, :, 0:8], qv[:, :, :, 8:16], 16, 8, H_IDX).then_inc(*dve_att.inc(l, "rqi"))
                for j in range(2):
                    dve.wait_ge(*act_att(l, f"q{j}"))
                    dve.wait_ge(*dve_att(l, "rqi" if j == 0 else "rq0"))
                    qv = q_tok[j].rearrange("p t (h f) -> p t h f", h=4)
                    rotate(l, f"rq{j}", qv[:, :, :, 0:16], qv[:, :, :, 16:32], 0, 16, 4).then_inc(*dve_att.inc(l, f"rq{j}"))
                rkv(l, 0, 2)
                for i in range(6):
                    dve.wait_ge(*act_att(l, f"s{i}"))
                    heads, t = (range(4 * i, 4 * i + 4), 0) if i < 2 else (range(2 * (i - 2), 2 * (i - 2) + 2), 1)
                    n = P * (t + 1)
                    for j, h in enumerate(heads):
                        wi = p_tok[:, t, C_IW + h:C_IW + h + 1]
                        src = rel[:, i % 2, j * n:j * n + n]
                        if h == 0:
                            last = dve.tensor_scalar(keep[:, t, 0:n], src, wi, None, ALU.mult)
                        else:
                            dve.wait_ge(*dve_att(l, f"s{t}{h - 1}"))
                            last = dve.scalar_tensor_tensor(out=keep[:, t, 0:n], in0=src, scalar=wi, in1=keep[:, t, 0:n],
                                                            op0=ALU.mult, op1=ALU.add)
                        last.then_inc(*dve_att.inc(l, f"s{t}{h}"))
                def topk(t):
                    dve.wait_ge(*dve_att(l, f"s{t}{H_IDX - 1}"))
                    kp = keep[:, t, 0:P * (t + 1)]
                    dve.tensor_tensor(keep[:, t, t * P:t * P + P], keep[:, t, t * P:t * P + P], C["causal"], ALU.add
                                      ).then_inc(*dve_att.inc(l, f"causal{t}"))
                    for i in range(TOPK // 8):
                        dve.wait_ge(*dve_att(l, f"causal{t}" if i == 0 else f"rep{t}{i - 1}"))
                        dve.max(small[:, 16:24], kp).then_inc(*dve_att.inc(l, f"max{t}{i}"))
                        dve.wait_ge(*dve_att(l, f"max{t}{i}"))
                        dve.match_replace(kp, small[:, 16:24], kp, TAKEN).then_inc(*dve_att.inc(l, f"rep{t}{i}"))
                    dve.wait_ge(*dve_att(l, f"rep{t}{TOPK // 8 - 1}"))
                    dve.tensor_scalar(kp, kp, TAKEN / 2, -NEG, ALU.is_lt, ALU.mult).then_inc(*dve_att.inc(l, f"sel{t}"))
                    dve.wait_ge(*dve_att(l, f"sel{t}"))
                    dve.tensor_scalar(kp, kp, NEG, None, ALU.add).then_inc(*dve_att.inc(l, f"selb{t}"))
                    dve.wait_ge(*dve_att(l, f"selb{t}"))
                    dve.tensor_tensor(keep[:, t, t * P:t * P + P], keep[:, t, t * P:t * P + P], C["causal"], ALU.add
                                      ).then_inc(*dve_att.inc(l, f"keep{t}"))

                prep_decay(r0)
                prep_sum(r0)
                topk(0)
                prep_rn(r0)
                topk(1)
                prep_rest(r0)
                prep_bonus(r0)
                for g in range(GROUPS):
                    r = r0 + g
                    nxt = g + 1 < GROUPS
                    grams(r)
                    if g:
                        y_scale(r - 1)
                        y_out(r - 1)
                    bonus(r)
                    if nxt:
                        rkv(l, g + 1, 0)
                    level(r, 1)
                    level(r, 2)
                    att_masked(l, g)
                    level(r, 3)
                    if nxt:
                        rkv(l, g + 1, 1)
                    att_norm(l, g)
                    level(r, 4)
                    level(r, 5)
                    if nxt:
                        rkv(l, g + 1, 2)
                    chunk(r, 0)
                    if nxt:
                        prep_decay(r + 1)
                    chunk(r, 1)
                    if nxt:
                        prep_sum(r + 1)
                    chunk(r, 2)
                    if nxt:
                        prep_rn(r + 1)
                    chunk(r, 3)
                    if nxt:
                        prep_rest(r + 1)
                    y_center(r)
                    if nxt:
                        prep_bonus(r + 1)
                    y_var(r)
                y_scale(r0 + GROUPS - 1)
                y_out(r0 + GROUPS - 1)
                for i in range(4):
                    dve.wait_ge(*pair_done(l, ("oa", i)))
                    dve.wait_ge(*act_dense(l, ("gate", 7)))
                    dst = flat2(gates[:, 2 * i:2 * i + 2, :])
                    dve.scalar_tensor_tensor(out=dst, in0=dst, scalar=1.0, in1=bank(pair_at[l, ("oa", i)] % 2), op0=ALU.add,
                                             op1=ALU.mult).then_inc(*dve_dense.inc(l, ("oa", i)))
                for i in range(4):
                    dve.wait_ge(*pair_done(l, ("ob", i)))
                    dst = flat2(gates[:, KB + 2 * i:KB + 2 * i + 2, :])
                    dve.scalar_tensor_tensor(out=dst, in0=dst, scalar=1.0, in1=bank(pair_at[l, ("ob", i)] % 2), op0=ALU.add,
                                             op1=ALU.mult).then_inc(*dve_dense.inc(l, ("ob", i)))
                    dve.wait_ge(*dve_dense(l, ("ob", i)))
                    a = flat2(gates[:, 2 * i:2 * i + 2, :])
                    dve.tensor_tensor(a, a, dst, ALU.add).then_inc(*dve_x.inc(l, f"mix{i}"))
                layer_norm(l, "A", "out", KB)
                for i in range(FB):
                    n = ("up", i)
                    c, th = conv[i % 2][:, 0, :], conv[i % 2][:, 1, :]
                    src = tok(pair_at[l, n] % 2)
                    for k in (1, 2):
                        dve.wait_ge(*(act_dense(l, n) if k == 1 else dve_dense(l, (n, "conv1"))))
                        dve.scalar_tensor_tensor(out=c[:, k:T], in0=src[:, 0, 0:T - k], scalar=cp(l, "conv_w", (2 - k) * FB + i),
                                                 in1=c[:, k:T], op0=ALU.mult, op1=ALU.add
                                                 ).then_inc(*dve_dense.inc(l, (n, "conv1" if k == 1 else "conv")))
                    dve.wait_ge(*act_dense(l, (n, "tanh")))
                    dve.scalar_tensor_tensor(out=c, in0=th, scalar=1.0, in1=c, op0=ALU.add, op1=ALU.mult
                                             ).then_inc(*dve_dense.inc(l, (n, "silu")))
                    dve.wait_ge(*dve_dense(l, (n, "silu")))
                    dve.scalar_tensor_tensor(out=hid(i), in0=c, scalar=0.5, in1=src[:, 1, :], op0=ALU.mult, op1=ALU.mult
                                             ).then_inc(*dve_dense.inc(l, n))
                layer_norm(l, "B", "down", FB)


def _blocks(w):
    n = -(-w.shape[1] // P) * P
    w = np.pad(w, ((0, 0), (0, n - w.shape[1])))
    return w.reshape(KB, P, n // P, P).transpose(2, 1, 0, 3).reshape(n // P, P, D)


def _rows(w):
    return w.reshape(-1, P, D)


def _halves(w):
    return w.reshape(2, P, -1, 512).transpose(2, 1, 0, 3).reshape(-1, P, D)


def _columns(v):
    return v.reshape(-1, P).T


def _consts():
    c = np.zeros((P, NCONST), np.float32)
    at = {n: slice(CONST_AT[n], CONST_AT[n] + w) for n, w in CONST}
    p, s = np.arange(P)[:, None], np.arange(CH)[None]
    c[:, at["ident"]] = np.eye(P)
    c[:, at["stack"]] = p % CH == s
    c[:, at["strict"]] = p % CH < s
    c[:, at["incl"]] = p % CH <= s
    c[:, at["hsel"]] = p // CH == np.arange(2)[None]
    c[:, at["bones"]] = p // CH == np.arange(P)[None] // CH
    col = np.arange(512)[None]
    c[:8, at["rowsel"]] = np.arange(8)[:, None] == 2 * (col // P) + col % P // CH
    c[:, at["scan"]] = col % CH != 0
    c[:, at["causal"]] = np.where(np.arange(P)[None] <= p, 0, NEG)
    f = [THETA ** (-2 * i / ROT_A) for i in range(ROT_A // 2)] + [THETA ** (-2 * i / ROT_IDX) for i in range(ROT_IDX // 2)]
    c[:, at["freq"]] = np.array(f)
    m = np.zeros((P, 2, LEVELS, CH), np.uint32)
    for lev in range(LEVELS):
        n = 1 << lev
        row, colm = p % CH, s
        upper = (row // (2 * n) == colm // (2 * n)) & (row % (2 * n) < n) & (colm % (2 * n) >= n)
        lower = (row // (2 * n) == colm // (2 * n)) & (row % (2 * n) >= n) & (colm % (2 * n) < n)
        m[:, 0, lev], m[:, 1, lev] = upper, lower
    return c, m.reshape(P, -1)


def kernel(**inputs):
    import concourse.bacc as _bacc
    from concourse.bass_utils import run_bass_kernel_spmd as _run

    a = {n: np.asarray(v) for n, v in inputs.items()}
    stream = []
    cpar = np.zeros((P, DEPTH, NCPAR), np.float32)
    lora = np.zeros((DEPTH, P, 3, D), np.float32)
    rpar = np.zeros((DEPTH, 4 * D + 2 * D_IDX), np.float32)
    for l in range(DEPTH):
        w_in = a["w_in0"] if l == 0 else a["w_in_rest"][l - 1]
        rw = w_in[:, N_ATT + N_GATE:N_IN0]
        parts = {"att": _blocks(w_in[:, :N_ATT]), "gate": _blocks(w_in[:, N_ATT:N_ATT + N_GATE]),
                 "rkv": _blocks(rw[:, :3 * D]), "lora": _blocks(rw[:, 3 * D:]), "vres": _blocks(w_in[:, N_IN0:]),
                 "iq": _halves(a["w_iq"][l]), "uq": _halves(a["w_uq"][l]),
                 "oa": _blocks(a["w_oa"][l]), "ob": _blocks(a["w_ob"][l]), "out": _rows(a["w_out"][l]),
                 "up": _blocks(a["w_up"][l]), "down": _rows(a["w_down"][l])}
        stream += [parts[kind][i] for kind, i in stream_order(l)]
        mu = np.zeros(27 * P, np.float32)
        mu[:N_RWKV] = a["mu_rwkv"][l]
        v0 = np.zeros(D, np.float32)
        if l:
            mu[N_RWKV:N_RWKV + LORA_V] = a["mu_vres"][l - 1]
            v0 = a["v0"][l - 1]
            lora[l, :LORA_V, 2] = a["v2"][l - 1]
        for name, v in (("mu", mu), ("v0", v0), *((n, a[n][l]) for n, _ in CPAR if n not in ("mu", "v0"))):
            c = _columns(np.asarray(v).reshape(-1))
            cpar[:, l, CPAR_AT[name]:CPAR_AT[name] + c.shape[1]] = c
        lora[l, :LORA_W, 0], lora[l, LORA_W:, 0], lora[l, :, 1] = a["w2"][l], a["a2"][l], a["g2"][l]
        rpar[l] = np.concatenate([a[n][l] for n in ("ln1_g", "ln1_b", "ln2_g", "ln2_b", "g_ik", "b_ik")])
    const, masks = _consts()
    arrays = {"x_dram": a["x"][0], "pos_dram": np.ascontiguousarray(a["positions"][0].reshape(TT, P).T),
              "stream_dram": np.stack(stream), "lora_dram": lora.reshape(DEPTH, P, 3 * D),
              "cpar_dram": cpar.reshape(P, -1), "rpar_dram": rpar, "const_dram": const, "masks_dram": masks}
    nc = _bacc.Bacc("TRN2", target_bir_lowering=False, num_devices=1)
    args = []
    for name, v in arrays.items():
        arrays[name] = v = np.ascontiguousarray(v)
        args.append(nc.dram_tensor(name, v.shape, mybir.dt.from_np(v.dtype), kind="ExternalInput").ap())
    args.append(nc.dram_tensor("out_dram", (T, D), F32, kind="ExternalOutput").ap())
    trunk(nc, *args)
    r = _run(nc, [arrays], core_ids=[0])
    return r.results[0]["out_dram"].reshape(1, T, D)
```

```python
import math
from contextlib import ExitStack

import numpy as np

import concourse.bass as bass
from concourse import mybir

F32 = mybir.dt.float32
F32R = mybir.dt.float32r
I32 = mybir.dt.int32
U32 = mybir.dt.uint32
ALU = mybir.AluOpType
ACT = mybir.ActivationFunctionType
AX = mybir.AxisListType.X

P = 128
D = 1024
T = 256
DEPTH = 2
TT = T // P
KB = D // P
ALPHA = (2 * DEPTH) ** 0.25
H_A, DH_A, D_CQ, ROT_A = 8, 128, 256, 32
H_IDX, D_IDX, ROT_IDX = 8, 64, 16
TOPK = 64
THETA = 500000.0
N_R = 64
LORA_W, LORA_A, LORA_V, LORA_G = 64, 64, 32, 128
GN_EPS, LN_EPS, RMS_EPS = 64e-5, 1e-5, 1e-6
D_FF = ((8 * D // 3 + 127) // 128) * 128
FB = D_FF // P
N_ATT = D_CQ + 2 * DH_A + D_IDX + H_IDX
N_GATE = 2 * D
N_RWKV = 3 * D + LORA_W + LORA_A + LORA_G
N_IN0 = N_ATT + N_GATE + N_RWKV
C_K, C_V, C_IK, C_IW = D_CQ, D_CQ + DH_A, D_CQ + 2 * DH_A, D_CQ + 2 * DH_A + D_IDX
NFR = ROT_A // 2 + ROT_IDX // 2
DECAY = math.exp(-0.5)
CH = 64
NCH = T // CH
GROUPS = 4
GB = KB // GROUPS
NU = GB * NCH
NEG = -1e30
TAKEN = -3e38

RING = 4


GATES_FIRST = 3
GATES_CHUNKS = [1,1,1,2]
CHUNK_GAPS = 8
LEVEL_GAPS = [0, 1, 2, 3, 4, 5, 6, 7]


def chunk_pairs(g):
    start = GATES_FIRST + sum(GATES_CHUNKS[:g])
    v = [("rkv", 3 * (g + 1) + 2)] if g + 1 < GROUPS else []
    return v + [("gate", i) for i in range(start, start + GATES_CHUNKS[g])]


def chunk_gap(g, piece):
    return piece * CHUNK_GAPS // max(4 * len(chunk_pairs(g)), CHUNK_GAPS)


def pairs_done(g, c):
    return [p for i, p in enumerate(chunk_pairs(g)) if chunk_gap(g, 4 * i + 3) // 2 == c]


def gate_slots(pairs):
    return [("gate", 2 * i + b) for i in pairs for b in range(2)]


def stream_order(layer):
    s = [("att", i) for i in range(5)]
    s += [("lora", 0), ("lora", 1)] + ([("vres", 0)] if layer else [])
    s += rkv_slots(0)[:4] + [("iq", 0), ("uq", 0), ("uq", 1)] + rkv_slots(0)[4:]
    s += gate_slots(range(GATES_FIRST))
    for g in range(GROUPS):
        if g + 1 < GROUPS:
            s += rkv_slots(g + 1)
        s += gate_slots([i for kind, i in chunk_pairs(g) if kind == "gate"])
    s += [("oa", i) for i in range(KB)] + [("ob", i) for i in range(KB)] + [("out", i) for i in range(KB)]
    for i in range(FB):
        s += [("up", i), ("up", FB + i)]
    s += [("down", i) for i in range(FB)]
    return s


def rkv_slots(g):
    return [("rkv", 8 * t + GB * g + b) for t in range(3) for b in range(GB)]


SLOTS = [(l, *s) for l in range(DEPTH) for s in stream_order(l)]
SLOT_AT = {s: n for n, s in enumerate(SLOTS)}
SPLIT = ("oa", "ob", "out", "up", "down")
SPLITS = [s for s in SLOTS if s[1] in SPLIT]
SPLIT_AT = {s: m for m, s in enumerate(SPLITS)}
NS = 4

CPAR = [("b_gate", 16), ("mu", 27), ("w0", 8), ("a0", 8), ("v0", 8), ("k_k", 8), ("k_a", 8), ("r_k", 8),
        ("g_lnx", 8), ("b_lnx", 8), ("g_cq", 2), ("conv_w", 3 * FB), ("conv_b", FB)]
CPAR_AT = {n: sum(w for _, w in CPAR[:i]) for i, (n, _) in enumerate(CPAR)}
NCPAR = sum(w for _, w in CPAR)
DPAR = [("omu", 27), ("hw0", 8), ("ha0", 8), ("hv0", 8), ("hgate", 16), ("hka", 8), ("omhka", 8)]
DPAR_AT = {n: sum(w for _, w in DPAR[:i]) for i, (n, _) in enumerate(DPAR)}
NDPAR = sum(w for _, w in DPAR)
CONST = [("ident", 128), ("stack", 64), ("strict", 64), ("incl", 64), ("hsel", 2), ("bones", 128),
         ("rowsel", 512), ("scan", 512), ("causal", 128), ("freq", NFR)]
CONST_AT = {n: sum(w for _, w in CONST[:i]) for i, (n, _) in enumerate(CONST)}
NCONST = sum(w for _, w in CONST)
LEVELS = 6


class Steps:

    def __init__(self, sem, names):
        self.sem, self.names, self.value, self.next = sem, names, {}, 0
        for r, steps in enumerate(names):
            for name in steps:
                self.value[r, name] = len(self.value) + 1

    def __call__(self, r, name):
        return self.sem, self.value[r, name]

    def inc(self, r, name):
        self.next += 1
        assert self.value[r, name] == self.next, (r, name, self.value[r, name], self.next)
        return self.sem, 1


def trunk(nc, x_in, pos_in, stream, lora_in, cpar_in, rpar_in, const_in, masks_in, out):
    ctx = ExitStack()
    with ctx:
        def sb(name, shape, dt=F32):
            return ctx.enter_context(nc.sbuf_tensor(name, shape, dt))

        rounded = {}

        def sb_or_parts(name, shape):
            with nc.sbuf_tensor(f"{name}_r", shape, F32R) as t:
                pass
            rounded[name] = t
            return sb(name, shape)

        def sem(name):
            return ctx.enter_context(nc.semaphore(name))

        ps = ctx.enter_context(nc.psum_tensor("ps", [P, 8, 512], F32))

        def bank(n):
            return ps[:, n, :]

        def units(n):
            return ps[:, n:n + 2, :].rearrange("p k (u s) -> p (k u) s", s=P)

        def unit64(n):
            return ps[:, n, :].rearrange("p (u s) -> p u s", s=CH)

        def tok(n):
            return ps[:, n, :].rearrange("p (b t) -> p b t", t=T)

        ring = sb("ring", [P, RING, D])
        x_tok = sb("x_tok", [P, TT, D])
        xT = sb_or_parts("xT", [P, KB, T])
        gates = sb_or_parts("gates", [P, 2 * KB, T])
        yb = sb_or_parts("yb", [P, KB, T])
        oT = sb_or_parts("oT", [P, H_A, T])
        qT = oT
        v_first = sb("v_first", [P, KB, T])
        lora_w = sb("lora_w", [P, 3, D])
        lora = sb("lora", [P, 3, T])
        cpar = sb("cpar", [P, DEPTH, NCPAR])
        dpar = sb("dpar", [P, NDPAR])
        const = sb("const", [P, NCONST])
        masks = sb("masks", [P, 2, LEVELS, CH], U32)
        half = sb("half", [P, 16])
        p_tok = sb("p_tok", [P, TT, N_ATT])
        kid = sb("kid", [P, TT, 2, D_IDX])
        kirow = sb("kirow", [P, 2 * D_IDX])
        cqT = sb("cqT", [P, 2, T])
        kT = sb("kT", [P, T])
        kiT = sb("kiT", [P, 2, T])
        keep = sb("keep", [P, TT, T])
        small = sb("small", [P, 64])
        scratch = sb("scratch", [P, 1536])
        rel = scratch[:, 0:1024].rearrange("p (a n) -> p a n", a=2)
        qi_tok = rel
        lg = scratch[:, 0:768]
        pT = scratch[:, 768:1536].rearrange("p (a n) -> p a n", a=2)
        sines = sb("sines", [P, 2, TT, NFR])
        ang = sb("ang", [P, 3, TT, NFR])
        pos = sb("pos", [P, TT], I32)
        posf = sb("posf", [P, TT])
        ln = sb("ln", [P, TT, 24])
        rs_ks, vs_dC = sb_or_parts("rs_ks", [P, 2, GB, T]), sb_or_parts("vs_dC", [P, 2, GB, T])
        tha_kkn, X_Y = sb_or_parts("tha_kkn", [P, 2, GB, T]), sb_or_parts("X_Y", [P, 2, NU, CH])
        rs, ks = rs_ks[:, 0, :, :], rs_ks[:, 1, :, :]
        vs_own, dC = vs_dC[:, 0, :, :], vs_dC[:, 1, :, :]
        tha, kkn = tha_kkn[:, 0, :, :], tha_kkn[:, 1, :, :]
        dA, dB, tmp = sb("dA", [P, GB, T]), sb("dB", [P, GB, T]), sb("tmp", [P, GB, T])
        gT = sb("gT", [P, GB, T])
        arc = sb_or_parts("arc", [P, NU, 2, CH])
        qiT = arc[:, :, :, :].rearrange("p (h a) b s -> p h (a b s)", h=4)
        vtmp = scratch[:, 1024:1536]
        a_bd, r_bd = sb_or_parts("a_bd", [P, NU, P]), sb_or_parts("r_bd", [P, NU, P])
        b_bd, k_bd, v_bd = sb_or_parts("b_bd", [P, NU, P]), sb_or_parts("k_bd", [P, NU, P]), sb("v_bd", [P, NU, P])
        W_bd = k_bd
        kt_bd = v_bd
        nT_bd, ak_bd = sb_or_parts("nT_bd", [P, NU, P]), sb_or_parts("ak_bd", [P, NU, P])
        rb_bd, rk_bd = sb_or_parts("rb_bd", [P, NU, P]), sb_or_parts("rk_bd", [P, NU, P])
        bt_bd = sb("bt_bd", [P, NU, P])
        Y_bd, y_bd = sb_or_parts("Y_bd", [P, NU, P]), sb("y_bd", [P, NU, P])
        X_bd = X_Y[:, :, :, :].rearrange("p a b c -> p (a b c)").rearrange("p (u s) -> p u s", s=P)
        sq = sb("sq", [P, NU, CH])
        Vc = sb("Vc", [P, NU, CH])
        Zs, Qs, S = sb("Zs", [P, GB, CH]), sb("Qs", [P, GB, CH]), sb("S", [P, 2, GB, CH])
        Sa = sb("Sa", [P, GB, CH])
        pend = sb("pend", [P, 2, GB, NCH])
        yt = sb("yt", [P, NU, CH])
        bv = sb("bv", [P, GB, T])
        ssm, rn, rnT = sb("ssm", [P, 8]), sb("rn", [P, 8]), sb("rnT", [8, P])
        g8 = sb("g8", [P, 5, NU])
        q_tok = [gates[:, 4 * j:4 * j + 4, :].rearrange("p (a b) s -> p a (b s)", a=TT) for j in range(2)]
        lnrow = [bt_bd[:, :, :].rearrange("p u s -> p (u s)"), v_bd[:, :, :].rearrange("p u s -> p (u s)")]
        def words(name):
            t = rounded[name]
            if len(t.shape) == 3:
                return t[:, :, :].rearrange("p a b -> p (a b)")
            return t[:, :, :, :].rearrange("p a b c -> p (a b c)")

        def f32(parts):
            return parts.bitcast(F32)

        w_hi = [words(t) for t in ("arc", "tha_kkn", "b_bd", "rb_bd")]
        w_lo = [words(t) for t in ("rs_ks", "X_Y", "vs_dC", "Y_bd")]
        o_hi = [words(t) for t in ("nT_bd", "k_bd")]
        yb_hi = [words(t) for t in ("a_bd", "r_bd")]
        mix_hi = [rounded["gates"][:, KB + i, :] for i in range(KB)]
        mix_lo = [rounded["gates"][:, i, :] for i in range(KB)]
        xT_hi, xT_lo = rounded["xT"], rounded["oT"]
        hid_hi = [words(t)[:, T * i:T * i + T] for t in ("a_bd", "r_bd", "k_bd", "nT_bd", "ak_bd", "rk_bd") for i in range(4)]
        hid_lo = ([rounded["gates"][:, i, :] for i in range(2 * KB)] + [rounded["yb"][:, i, :] for i in range(KB)])

        def block_of(t, i):
            return t[i // 4][:, T * (i % 4):T * (i % 4) + T]

        def blocks(t, i, n):
            return t[:, i:i + n, :].rearrange("p a b -> p (a b)")

        YB_RUNS = [[(0, 4), (4, 2)], [(6, 2)]]

        def yb_hi_run(i, n):
            return yb_hi[i // 4][:, T * (i % 4):T * (i % 4 + n)]

        conv = [dA, dB]

        def flat(t):
            return t[:, :, :].rearrange("p a b -> p (a b)")

        def by_unit(t):
            return t.rearrange("p b (c s) -> p (b c) s", s=CH)

        def vs(r):
            g = r % GROUPS
            return v_first[:, GB * g:GB * g + GB, :] if r < GROUPS else vs_own[:, :, :]

        C = {n: const[:, CONST_AT[n]:CONST_AT[n] + w] for n, w in CONST}
        ident, stack = C["ident"], C["stack"]

        def cp(layer, name, i=0, n=1):
            a = CPAR_AT[name] + i
            return cpar[:, layer, a:a + n]

        def dp(name, i=0, n=1):
            a = DPAR_AT[name] + i
            return dpar[:, a:a + n]

        def q64(h):
            return slice(64 * h, 64 * h + 64)

        R = DEPTH * GROUPS
        L2 = range(DEPTH)
        lv = range(1, LEVELS)

        landed = [sem(f"slot{i}_landed") for i in range(RING)]
        slot_used = sem("slot_used")
        inputs_in = sem("inputs_in")
        lora_landed = sem("lora_landed")
        rows_landed = sem("rows_landed")
        stored = sem("stored")
        zeroed = sem("zeroed")
        tables_dve = sem("tables_dve")
        kid_half = sem("kid_half")
        tables = sem("tables")

        def used(l, kind, i):
            return slot_used, SLOT_AT[l, kind, i] + 1

        def pair_slots(n):
            kind, i = n
            return {"lora": [("lora", 0), ("lora", 1)], "vres": [("vres", 0)],
                    "rkv": [("rkv", 8 * (i % 3) + GB * (i // 3) + b) for b in range(GB)],
                    "gate": [("gate", 2 * i), ("gate", 2 * i + 1)],
                    "oa": [("oa", 2 * i), ("oa", 2 * i + 1)], "ob": [("ob", 2 * i), ("ob", 2 * i + 1)],
                    "up": [("up", i), ("up", FB + i)]}[kind]

        pairs = []
        for l in L2:
            seen = []
            for s in stream_order(l):
                kind, i = s
                n = {"lora": ("lora", 0), "vres": ("vres", 0), "rkv": ("rkv", i % 8 // 2 * 3 + i // 8),
                     "gate": ("gate", i // 2), "oa": ("oa", i // 2), "ob": ("ob", i // 2),
                     "up": ("up", i % FB)}.get(kind)
                if n and n not in seen:
                    seen.append(n)
            pairs += [(l, n) for n in seen]
        pair_at = {n: d for d, n in enumerate(pairs)}

        def pair_done(l, n):
            return used(l, *pair_slots(n)[-1])

        shifted = ("lora", "vres", "rkv")
        act_dense = Steps(sem("act_dense"), [sum([[n] if n[0] in shifted + ("gate",) else
                                                  [n, (n, "tanh"), (n, "hi")] if n[0] == "up" else []
                                                  for k, n in pairs if k == l], []) for l in L2])
        dve_dense = Steps(sem("dve_dense"), [sum([[n] if n[0] in shifted + ("oa", "ob") else
                                                  [(n, "conv1"), (n, "conv"), (n, "silu"), (n, "whole"), n] if n[0] == "up" else []
                                                  for k, n in pairs if k == l], []) for l in L2])

        def pair_free(l, n):
            return act_dense(l, n) if n[0] == "gate" else dve_dense(l, (n, "whole") if n[0] == "up" else n)

        def by_layer(name, steps):
            return Steps(sem(name), [steps] * DEPTH)

        def by_round(name, steps):
            return Steps(sem(name), [steps] * R)

        per_layer = len(SPLITS) // DEPTH
        act_split = by_layer("act_split", list(range(per_layer)))
        dve_split = by_layer("dve_split", list(range(per_layer)))
        parts = ["o0", "o1", "yb0", "yb1"] + [f"mix{i}" for i in range(4)]
        act_parts = by_layer("act_parts", parts)
        dve_parts = by_layer("dve_parts", parts + [f"x{i}" for i in range(4)])

        pe_x = by_layer("pe_x", [f"T{i}" for i in range(4)] + [f"U{i}" for i in range(4)])
        act_x = by_layer("act_x", [f"T{i}" for i in range(4)] + ["Aax"] + [f"U{i}" for i in range(4)] + ["Bax"])
        dve_par = by_layer("dve_par", ["dpar", "lsig"])
        dve_x = by_layer("dve_x", [f"mix{i}" for i in range(4)]
                         + sum([[f"{w}add", f"{w}st", f"{w}mv", f"{w}c", f"{w}n"] for w in "AB"], []))
        act_lora = by_layer("act_lora", ["tanh"])
        pool_x = by_layer("pool_x", ["Aeps", "A", "Beps", "B"])
        pe_att = by_layer("pe_att", ["cqT", "kT", "qiT", "qT"] + [f"s{i}" for i in range(6)]
                          + sum([[f"lg{g}", f"pT{g}", f"o{g}"] for g in range(GROUPS)], []))
        act_att = by_layer("act_att", ["p", "ssq", "cqT", "kT", "qi", "q0", "q1", "qiT", "qT"]
                           + [f"s{i}" for i in range(6)]
                           + sum([[f"e{g}", f"pT{g}", f"o{g}"] for g in range(GROUPS)], []))
        rope = lambda w: [f"{w}a", f"{w}"]
        dve_att = by_layer("dve_att", ["wi", "kst", "kmv"] + rope("rk") + ["cq", "kic", "ki"] + rope("rki") + rope("rqi")
                           + rope("rq0") + rope("rq1")
                           + [f"s{t}{h}" for t in range(TT) for h in range(H_IDX)]
                           + sum([[f"causal{t}"] + sum([[f"max{t}{i}", f"rep{t}{i}"] for i in range(8)], [])
                                  + [f"sel{t}", f"selb{t}", f"keep{t}"] for t in range(TT)], [])
                           + sum([[f"lg{g}", f"mx{g}", f"rc{g}", f"pn{g}"] for g in range(GROUPS)], []))
        pool_att = by_layer("pool_att", ["eps", "rs"])

        pe_prep = Steps(sem("pe_prep"), [["zw", "za"] + (["zv"] if r >= GROUPS else []) + ["ss", "rnT", "rnx"]
                                         for r in range(R)])
        act_prep = Steps(sem("act_prep"), [["kk2", "thw", "tha", "P", "Pp", "iP", "kt"]
                                           + (["thv"] if r >= GROUPS else []) for r in range(R)])
        dve_prep = Steps(sem("dve_prep"), [["s", "cum", "cp", "pend", "ss", "rnT"]
                                           + (["v1", "v2", "v"] if r >= GROUPS else [])
                                           + ["kkn", "k2", "kb", "arc", "bneg", "kp", "rkk"] for r in range(R)])
        pool_prep = by_round("pool_prep", ["rn"])
        pe_wkv = by_round("pe_wkv", ["gramB", "gramK", "V", "nX", "tokB", "tokK", "bonus", "zg"]
                          + sum([[f"W{l}0", f"W{l}1"] + sum([([f"XW{l}{k}"] if l < LEVELS - 1 else []) + [f"WtY{l}{k}"]
                                                     for k in range(2)], []) for l in lv], [])
                          + sum([[f"Z{c}", f"Q{c}"] + ([f"S{c}"] if c < NCH - 1 else []) + [f"y{c}"]
                                 for c in range(NCH)], []))
        pe_yT = by_round("pe_yT", ["yT"])
        act_wkv = by_round("act_wkv", ["reset", "vbd", "Vc", "tokB", "tokK", "g"] + [f"W{l}{k}" for l in lv for k in range(2)]
                           + [f"Z{c}" for c in range(NCH)])
        act_y = by_round("act_y", ["y", "sq", "yn"])
        dve_wkv = by_round("dve_wkv", ["nT", "Arb", "Y0", "Aak", "Ark", "X00", "X01", "bv"]
                           + sum([([f"X{l}{k}"] if l < LEVELS - 1 else []) + [f"Y{l}{k}"] for l in lv for k in range(2)], [])
                           + sum([[f"Q{c}"] + ([f"S{c}a"] * (c > 0) + [f"S{c}"] if c < NCH - 1 else [])
                                  for c in range(NCH)], []))
        dve_y = by_round("dve_y", ["m", "m2", "yc", "v8", "yr", "yb1", "yb"])
        pool_bd = by_round("pool_bd", ["abd0", "abd1", "rbd0", "rbd"])
        pool_y = by_round("pool_y", ["eps", "rstd"])

        block = ctx.enter_context(nc.Block())

        @block.sync
        def _(sp):
            sp.dma_start(x_tok[:, :, :], x_in.rearrange("(a p) d -> p a d", p=P)).then_inc(inputs_in, 16)
            sp.dma_start(const[:, :], const_in).then_inc(inputs_in, 16)
            for n in range(RING):
                sp.dma_start(ring[:, n, :], stream[n]).then_inc(landed[n], 16)
            sp.dma_start(pos[:, :], pos_in).then_inc(inputs_in, 16)
            sp.dma_start(flat(cpar), cpar_in).then_inc(inputs_in, 16)
            sp.dma_start(masks[:, :, :, :].rearrange("p a l c -> p (a l c)"), masks_in).then_inc(inputs_in, 16)
            def refill(n, k, wait, value):
                sp.wait_ge(wait, value)
                src = stream[n] if isinstance(n, int) else stream[bass.ds(n, 1)].rearrange("a p d -> p (a d)")
                sp.dma_start(ring[:, k, :], src).then_inc(landed[k], 16)

            n = RING
            while n < len(SLOTS):
                split = SLOTS[n - RING] in SPLIT_AT
                end = n
                while end < len(SLOTS) and (SLOTS[end - RING] in SPLIT_AT) == split:
                    end += 1
                wait = dve_split.sem if split else slot_used
                less = n - SPLIT_AT[SLOTS[n - RING]] - 1 if split else RING - 1
                first, last = -(-n // RING), end // RING
                for m in range(n, first * RING):
                    refill(m, m % RING, wait, m - less)
                with sp.Fori(first, last) as i:
                    for k in range(RING):
                        refill(i * RING + k, k, wait, i * RING + (k - less))
                for m in range(last * RING, end):
                    refill(m, m % RING, wait, m - less)
                n = end
            sp.wait_ge(*dve_x(DEPTH - 1, "Bn"))
            sp.dma_start(out.rearrange("(a p) d -> p a d", p=P), x_tok[:, :, :]).then_inc(stored, 16)
            sp.wait_ge(stored, 16)

        @block.gpsimd
        def _(pool):
            def zero_bd(l):
                again = [a_bd, r_bd, b_bd, k_bd, v_bd, nT_bd, ak_bd, y_bd]
                if l:
                    pool.wait_ge(*dve_x(l - 1, "Bn"))
                    again = [a_bd, r_bd, b_bd, k_bd, v_bd, nT_bd, ak_bd, rb_bd, rk_bd]
                else:
                    pool.memset(kiT[:, :, :], 0.0)
                    again += [rb_bd, rk_bd]
                for t in again:
                    last = pool.memset(t[:, :, :], 0.0)
                last.then_inc(zeroed, 1)

            def small_rows(l):
                if l:
                    pool.wait_ge(*pe_wkv(GROUPS * l - 1, "zg"))
                    pool.wait_ge(*pe_prep(GROUPS * l - 1, "za"))
                    pool.wait_ge(*dve_att(l - 1, "ki"))
                pool.dma_start(flat(lora_w), lora_in[l]).then_inc(lora_landed, 16)
                pool.dma_start(kirow[:, :], rpar_in[l:l + 1, 4 * D:4 * D + 2 * D_IDX].broadcast_to([P, 2 * D_IDX])
                               ).then_inc(lora_landed, 16)

            def norm_rows(l, w):
                i = "AB".index(w)
                if i == 0:
                    pool.wait_ge(*pe_wkv(GROUPS * (l + 1) - 1, f"y{NCH - 1}"))
                else:
                    pool.wait_ge(*dve_x(l, "An"))
                for j in range(2):
                    a = (2 * i + j) * D
                    pool.dma_start(lnrow[j], rpar_in[l:l + 1, a:a + D].broadcast_to([P, D])
                                   ).then_inc(rows_landed, 16)

            def norm_rsqrt(l, w):
                pool.wait_ge(*dve_x(l, f"{w}mv"))
                pool.tensor_scalar(ln[:, :, 20], ln[:, :, 13], 1.0, LN_EPS, ALU.mult, ALU.add
                                   ).then_inc(*pool_x.inc(l, f"{w}eps"))
                pool.wait_ge(*pool_x(l, f"{w}eps"))
                pool.tensor_tensor(ln[:, :, 21], ln[:, :, 20], half[:, 0:TT], ALU.pow
                                   ).then_inc(*pool_x.inc(l, w))

            def head_norm(r):
                pool.wait_ge(*dve_prep(r, "ss"))
                pool.tensor_tensor(rn[:, :], ssm[:, :], half[:, 0:8], ALU.pow).then_inc(*pool_prep.inc(r, "rn"))

            pool.memset(half[:, :], -0.5).then_inc(zeroed, 1)
            small_rows(0)
            zero_bd(0)
            pool.wait_ge(zeroed, 2)
            for l in L2:
                if l:
                    zero_bd(l)
                    small_rows(l)
                pool.wait_ge(*act_att(l, "ssq"))
                pool.wait_ge(*dve_att(l, "kmv"))
                pool.tensor_scalar(small[:, 4:6], small[:, 0:2], 1.0 / D_CQ, RMS_EPS, ALU.mult, ALU.add)
                pool.tensor_scalar(small[:, 6:8], ln[:, :, 13], 1.0, LN_EPS, ALU.mult, ALU.add
                                   ).then_inc(*pool_att.inc(l, "eps"))
                pool.wait_ge(*pool_att(l, "eps"))
                pool.tensor_tensor(small[:, 8:12], small[:, 4:8], half[:, 0:4], ALU.pow
                                   ).then_inc(*pool_att.inc(l, "rs"))
                head_norm(GROUPS * l)
                for g in range(GROUPS):
                    r = GROUPS * l + g
                    pool.wait_ge(*dve_prep(r, "arc"))
                    if r:
                        pool.wait_ge(*pe_wkv(r - 1, f"y{NCH - 1}"))
                    pool.wait_ge(*(pool_y(r - 1, "rstd") if g else pool_prep(r, "rn")))
                    steps = [("abd0", a_bd, 0, 0), ("abd1", a_bd, 0, 1), ("rbd0", r_bd, 1, 0), ("rbd", r_bd, 1, 1)]
                    for name, dst, j, h in steps:
                        pool.tensor_copy(dst[q64(h), :, q64(h)], arc[q64(h), :, j, :]).then_inc(*pool_bd.inc(r, name))
                        pool.wait_ge(*pool_bd(r, name))
                    if g + 1 < GROUPS:
                        head_norm(r + 1)
                    pool.wait_ge(*dve_y(r, "v8"))
                    pool.tensor_scalar(g8[:, 3, :], g8[:, 2, :], 1.0 / N_R, GN_EPS, ALU.mult, ALU.add
                                       ).then_inc(*pool_y.inc(r, "eps"))
                    pool.wait_ge(*pool_y(r, "eps"))
                    pool.tensor_tensor(g8[:, 4, :], g8[:, 3, :], half[:, 0:NU], ALU.pow
                                       ).then_inc(*pool_y.inc(r, "rstd"))
                norm_rows(l, "A")
                norm_rsqrt(l, "A")
                norm_rows(l, "B")
                norm_rsqrt(l, "B")

        @block.tensor
        def _(pe):
            def slot(l, kind, i):
                n = SLOT_AT[l, kind, i]
                pe.wait_ge(landed[n % RING], 16 * (n // RING + 1))
                return ring[:, n % RING, :]

            def pair_pieces(l, n, rhs):
                d = pair_at[l, n]
                dst = tok(d % 2)

                def piece(b, name, k0):
                    if b == 0 and k0 == 0 and d >= 2:
                        pe.wait_ge(*pair_free(*pairs[d - 2]))
                    w = slot(l, *name)
                    for kb in range(k0, k0 + 4):
                        mm = pe.matmul(dst[:, b, :], w[:, kb * P:kb * P + P], rhs[:, kb, :],
                                       start=(kb == 0), stop=(kb == KB - 1))
                    if k0:
                        mm.then_inc(slot_used, 1)

                return [lambda b=b, name=name, k0=k0: piece(b, name, k0)
                        for b, name in enumerate(pair_slots(n)) for k0 in (0, 4)]

            def pair(l, n, rhs):
                for p in pair_pieces(l, n, rhs):
                    p()

            def slot_parts(l, kind, i):
                m = SPLIT_AT[l, kind, i] % per_layer
                pe.wait_ge(*dve_split(l, m))
                return w_hi[m % NS], w_lo[m % NS]

            def product(dst, left, right, start, stop):
                (lh, ll), (rh, rl) = left, right
                pe.matmul(dst, lh, rh, start=start, stop=False)
                pe.matmul(dst, lh, rl, start=False, stop=False)
                return pe.matmul(dst, ll, rh, start=False, stop=stop)

            def split_pair(l, n, rhs):
                d = pair_at[l, n]
                pe.wait_ge(*pair_free(*pairs[d - 2]))
                for b, name in enumerate(pair_slots(n)):
                    w = slot_parts(l, *name)
                    for kb in range(KB):
                        mm = product(tok(d % 2)[:, b, :], [x[:, kb * P:kb * P + P] for x in w], rhs(kb),
                                     kb == 0, kb == KB - 1)
                    mm.then_inc(slot_used, 1)

            def transposed_x(l, w):
                for i in range(4):
                    if i >= 2:
                        pe.wait_ge(*(act_x(l, f"T{i - 2}") if w == "T" else dve_parts(l, f"x{i - 2}")))
                    for b in range(2):
                        for t in range(TT):
                            mm = pe.transpose(tok(i % 2)[:, b, t * P:t * P + P],
                                              x_tok[:, t, (2 * i + b) * P:(2 * i + b + 1) * P], ident)
                    mm.then_inc(*pe_x.inc(l, f"{w}{i}"))

            def prep_1(r):
                l, g = divmod(r, GROUPS)
                if g == 0:
                    pe.wait_ge(*act_lora(l, "tanh"))
                    pe.wait_ge(lora_landed, 32 * (l + 1))
                    pe.wait_ge(*act_att(l, "qT"))
                else:
                    pe.wait_ge(*act_att(l, f"o{g - 1}"))
                for b in range(GB):
                    c = (GB * g + b) * P
                    mm = pe.matmul(tok(6)[:, b, :], lora_w[0:64, 0, c:c + P], lora[0:64, 0, :], start=True, stop=True)
                mm.then_inc(*pe_prep.inc(r, "zw"))
                for b in range(GB):
                    c = (GB * g + b) * P
                    mm = pe.matmul(tok(7)[:, b, :], lora_w[64:128, 0, c:c + P], lora[64:128, 0, :], start=True, stop=True)
                mm.then_inc(*pe_prep.inc(r, "za"))

            def prep_2(r):
                l, g = divmod(r, GROUPS)
                if l:
                    pe.wait_ge(*dve_par(l, "lsig"))
                    pe.wait_ge(*act_prep(r, "thw"))
                    for b in range(GB):
                        c = (GB * g + b) * P
                        mm = pe.matmul(tok(6)[:, b, :], lora_w[:, 2, c:c + P], lora[:, 2, :], start=True, stop=True)
                    mm.then_inc(*pe_prep.inc(r, "zv"))
                pe.wait_ge(*act_prep(r, "tha"))
                pe.wait_ge(*act_prep(r, "kk2"))
                for b in range(GB):
                    for t in range(TT):
                        j = 2 * (TT * b + t)
                        mm = pe.matmul(bank(7)[:, j:j + 2], tmp[:, b, t * P:t * P + P], C["hsel"], start=True, stop=True)
                mm.then_inc(*pe_prep.inc(r, "ss"))

            def prep_3(r):
                pe.wait_ge(*pool_prep(r, "rn"))
                pe.transpose(bank(7)[0:8, 128:256], rn[:, :], ident).then_inc(*pe_prep.inc(r, "rnT"))

            def prep_4(r):
                pe.wait_ge(*dve_prep(r, "rnT"))
                pe.wait_ge(*act_prep(r, "thv" if r >= GROUPS else "thw"))
                for b in range(GB):
                    for t in range(TT):
                        j = TT * b + t
                        mm = pe.matmul(tok(6)[:, b, t * P:t * P + P], C["rowsel"][0:8, j * P:j * P + P], rnT[:, :],
                                       start=True, stop=True)
                mm.then_inc(*pe_prep.inc(r, "rnx"))

            def y_back(r):
                pe.wait_ge(*dve_y(r, "yr"))
                if (r + 1) % GROUPS:
                    pe.wait_ge(*dve_prep(r + 1, "kkn"))
                else:
                    pe.wait_ge(*act_att(r // GROUPS, f"o{GROUPS - 1}"))
                for u in range(NU):
                    mm = pe.matmul(unit64(6)[:, u, :], y_bd[:, u, :], stack, start=True, stop=True)
                mm.then_inc(*pe_yT.inc(r, "yT"))

            def att_logits(l, g):
                r = GROUPS * l + g
                pe.wait_ge(*dve_wkv(r, "bv"))
                pe.wait_ge(*act_wkv(r, "g"))
                for h in range(2):
                    pe.matmul(bank(6)[:, h * T:h * T + T], qT[:, 2 * g + h, P:T], kT[:, :], start=True, stop=True)
                for h in range(2):
                    mm = pe.matmul(bank(7)[:, h * P:h * P + P], qT[:, 2 * g + h, 0:P], kT[:, 0:P], start=True, stop=True)
                mm.then_inc(*pe_att.inc(l, f"lg{g}"))

            def att_probs(l, g):
                pe.wait_ge(*dve_att(l, f"pn{g}"))
                for h in range(2):
                    b = bank(6 + h)
                    pe.transpose(b[:, 0:P], lg[:, 512 + h * P:512 + h * P + P], ident)
                    for s in range(2):
                        mm = pe.transpose(b[:, P + s * P:2 * P + s * P], lg[:, h * T + s * P:h * T + s * P + P], ident)
                mm.then_inc(*pe_att.inc(l, f"pT{g}"))

            def att_values(l, g):
                pe.wait_ge(*act_att(l, f"pT{g}"))
                v0, v1 = p_tok[:, 0, C_V:C_V + DH_A], p_tok[:, 1, C_V:C_V + DH_A]
                for h in range(2):
                    o = tok(6)[:, h, :]
                    pe.matmul(o[:, 0:P], v0, pT[:, h, 0:P], start=True, stop=True)
                    pe.matmul(o[:, P:T], v0, pT[:, h, P:2 * P], start=True, stop=False)
                    mm = pe.matmul(o[:, P:T], v1, pT[:, h, 2 * P:3 * P], start=False, stop=True)
                mm.then_inc(*pe_att.inc(l, f"o{g}"))

            def wkv(r, fill):
                l, g = divmod(r, GROUPS)
                bc = lambda c: [NCH * b + c for b in range(GB)]
                pe.wait_ge(*dve_prep(r, "bneg"))
                if g == 0:
                    pe.wait_ge(zeroed, l + 2)
                    pe.wait_ge(*act_att(l, "s5"))
                else:
                    pe.wait_ge(*act_wkv(r - 1, f"Z{NCH - 1}"))
                    pe.wait_ge(*dve_wkv(r - 1, f"Q{NCH - 1}"))
                rhs = arc[:, :, :, :].rearrange("p u a s -> p u (a s)")
                for u in range(NU):
                    mm = pe.matmul(units(2)[:, u, :], b_bd[:, u, :], rhs[:, u, :], start=True, stop=True)
                mm.then_inc(*pe_wkv.inc(r, "gramB"))
                pe.wait_ge(*dve_prep(r, "kp"))
                if g:
                    pe.wait_ge(*act_y(r - 1, "y"))
                for u in range(NU):
                    mm = pe.matmul(units(4)[:, u, :], k_bd[:, u, :], rhs[:, u, :], start=True, stop=True)
                mm.then_inc(*pe_wkv.inc(r, "gramK"))
                pe.wait_ge(*act_wkv(r, "vbd"))
                pe.wait_ge(*dve_prep(r, "rnT"))
                for u in range(NU):
                    mm = pe.matmul(unit64(7)[:, u, :], v_bd[:, u, :], stack, start=True, stop=True)
                mm.then_inc(*pe_wkv.inc(r, "V"))
                fill(0)
                pe.wait_ge(*dve_wkv(r, "Y0"))
                for u in range(NU):
                    mm = pe.transpose(units(2)[:, u, :], nT_bd[:, u, :], ident)
                mm.then_inc(*pe_wkv.inc(r, "nX"))
                fill(1)
                pe.wait_ge(*dve_wkv(r, "Ark"))
                for u in range(NU):
                    mm = pe.transpose(units(4)[:, u, :], b_bd[:, u, :], ident)
                mm.then_inc(*pe_wkv.inc(r, "tokB"))
                fill(2)
                pe.wait_ge(*act_wkv(r, "tokB"))
                for u in range(NU):
                    mm = pe.transpose(units(4)[:, u, :], k_bd[:, u, :], ident)
                mm.then_inc(*pe_wkv.inc(r, "tokK"))
                if g:
                    y_back(r - 1)
                fill(3)
                pe.wait_ge(*dve_prep(r, "rkk"))
                if g:
                    pe.wait_ge(*act_y(r - 1, "yn"))
                pe.matmul(bank(6), C["bones"], flat(tmp), start=True, stop=True).then_inc(*pe_wkv.inc(r, "bonus"))
                pe.wait_ge(*act_wkv(r, "Vc"))
                for b in range(GB):
                    c = (GB * g + b) * P
                    mm = pe.matmul(tok(7)[:, b, :], lora_w[:, 1, c:c + P], lora[:, 1, :], start=True, stop=True)
                mm.then_inc(*pe_wkv.inc(r, "zg"))
                for lev in lv:
                    for k in range(2):
                        if lev == 1:
                            pe.wait_ge(*dve_wkv(r, f"X0{k}"))
                        else:
                            pe.wait_ge(*dve_wkv(r, f"Y{lev - 1}{k}"))
                        for u in range(4 * k, 4 * k + 4):
                            mm = pe.matmul(units(2)[:, u, :], nT_bd[:, u, :], X_bd[:, u, :], start=True, stop=True)
                        mm.then_inc(*pe_wkv.inc(r, f"W{lev}{k}"))
                        if k == 0:
                            fill(2 + 2 * lev)
                            if lev == 1:
                                pe.wait_ge(*act_wkv(r, "tokK"))
                    for k in range(2):
                        pe.wait_ge(*act_wkv(r, f"W{lev}{k}"))
                        if lev < LEVELS - 1:
                            for u in range(4 * k, 4 * k + 4):
                                mm = pe.matmul(units(4)[:, u, :], Y_bd[:, u, :], W_bd[:, u, :], start=True, stop=True)
                            mm.then_inc(*pe_wkv.inc(r, f"XW{lev}{k}"))
                        for u in range(4 * k, 4 * k + 4):
                            mm = pe.matmul(units(2)[:, u, :], W_bd[:, u, :], Y_bd[:, u, :], start=True, stop=True)
                        mm.then_inc(*pe_wkv.inc(r, f"WtY{lev}{k}"))
                        if k == 0:
                            fill(3 + 2 * lev)
                for c in range(NCH):
                    if c == 0:
                        pe.wait_ge(*pool_bd(r, "rbd"))
                        pe.wait_ge(*dve_wkv(r, f"Y{LEVELS - 1}1"))
                    else:
                        pe.wait_ge(*dve_wkv(r, f"S{c - 1}"))
                    s_old = S[:, (c + 1) % 2, :, :]
                    for b, u in enumerate(bc(c)):
                        z = bank(2)[:, b * CH:b * CH + CH]
                        if c:
                            pe.matmul(z, a_bd[:, u, :], s_old[:, b, :], start=True, stop=False)
                        mm = pe.matmul(z, ak_bd[:, u, :], Vc[:, u, :], start=(c == 0), stop=True)
                    mm.then_inc(*pe_wkv.inc(r, f"Z{c}"))
                    fill(14 + 2 * c)
                    pe.wait_ge(*act_wkv(r, f"Z{c}"))
                    for b, u in enumerate(bc(c)):
                        mm = pe.matmul(bank(3)[:, b * CH:b * CH + CH], Y_bd[:, u, :], Zs[:, b, :], start=True, stop=True)
                    mm.then_inc(*pe_wkv.inc(r, f"Q{c}"))
                    fill(15 + 2 * c)
                    pe.wait_ge(*dve_wkv(r, f"Q{c}"))
                    if c < NCH - 1:
                        for b, u in enumerate(bc(c)):
                            s_new = bank(4)[:, b * CH:b * CH + CH]
                            pe.matmul(s_new, bt_bd[:, u, :], Qs[:, b, :], start=True, stop=False)
                            mm = pe.matmul(s_new, kt_bd[:, u, :], Vc[:, u, :], start=False, stop=True)
                        mm.then_inc(*pe_wkv.inc(r, f"S{c}"))
                    for b, u in enumerate(bc(c)):
                        y = unit64(5)[:, u, :]
                        pe.matmul(y, rb_bd[:, u, :], Qs[:, b, :], start=True, stop=False)
                        mm = pe.matmul(y, rk_bd[:, u, :], Vc[:, u, :], start=False, stop=(c == 0))
                        if c:
                            mm = pe.matmul(y, r_bd[:, u, :], s_old[:, b, :], start=False, stop=True)
                    mm.then_inc(*pe_wkv.inc(r, f"y{c}"))
                    if g + 1 < GROUPS and c < 3:
                        [prep_2, prep_3, prep_4][c](r + 1)

            pe.wait_ge(inputs_in, 16 * 5)
            for l in L2:
                if l:
                    pe.wait_ge(*dve_x(l - 1, "Bn"))
                transposed_x(l, "T")
                pe.wait_ge(*act_x(l, "T3"))
                for c in range(5):
                    w = slot(l, "att", c)
                    n = min(P, N_ATT - c * P)
                    for t in range(TT):
                        dst = bank(2 + t)[:, c * P:c * P + n] if c < 4 else bank(4)[:, t * P:t * P + n]
                        for kb in range(KB):
                            mm = pe.matmul(dst, xT[:, kb, t * P:t * P + P], w[:, kb * P:kb * P + n],
                                           start=(kb == 0), stop=(kb == KB - 1))
                    mm.then_inc(slot_used, 1)
                pair(l, ("lora", 0), xT)
                if l:
                    w = slot(l, "vres", 0)
                    d = pair_at[l, ("vres", 0)]
                    pe.wait_ge(*pair_free(*pairs[d - 2]))
                    for kb in range(KB):
                        mm = pe.matmul(tok(d % 2)[:, 0, :], w[:, kb * P:kb * P + P], xT[:, kb, :],
                                       start=(kb == 0), stop=(kb == KB - 1))
                    mm.then_inc(slot_used, 1)
                pair(l, ("rkv", 0), xT)
                pe.wait_ge(*dve_att(l, "cq"))
                for kb in range(2):
                    for t in range(TT):
                        mm = pe.transpose(tok(6)[:, kb, t * P:t * P + P], p_tok[:, t, kb * P:kb * P + P], ident)
                mm.then_inc(*pe_att.inc(l, "cqT"))
                pe.wait_ge(*dve_att(l, "rki"))
                for t in range(TT):
                    pe.transpose(bank(7)[:, t * P:t * P + P], p_tok[:, t, C_K:C_K + DH_A], ident)
                for t in range(TT):
                    mm = pe.transpose(bank(7)[:, T + t * P:T + t * P + P],
                                      kid[:, t, :, :].rearrange("p a b -> p (a b)"), ident)
                mm.then_inc(*pe_att.inc(l, "kT"))
                pair(l, ("rkv", 1), xT)
                pe.wait_ge(*act_att(l, "cqT"))
                w = slot(l, "iq", 0)
                for t in range(TT):
                    for kb in range(2):
                        mm = pe.matmul(bank(2 + t), cqT[:, kb, t * P:t * P + P], w[:, kb * 512:kb * 512 + 512],
                                       start=(kb == 0), stop=(kb == 1))
                mm.then_inc(slot_used, 1)
                for j in range(2):
                    w = slot(l, "uq", j)
                    if j:
                        pe.wait_ge(*act_att(l, "kT"))
                    for t in range(TT):
                        for kb in range(2):
                            mm = pe.matmul(bank(4 + 2 * j + t), cqT[:, kb, t * P:t * P + P], w[:, kb * 512:kb * 512 + 512],
                                           start=(kb == 0), stop=(kb == 1))
                    mm.then_inc(slot_used, 1)
                pair(l, ("rkv", 2), xT)
                pe.wait_ge(*dve_att(l, "rqi"))
                for i in range(4):
                    for t in range(TT):
                        mm = pe.transpose(tok(2 + i // 2)[:, i % 2, t * P:t * P + P], qi_tok[:, t, i * P:i * P + P], ident)
                mm.then_inc(*pe_att.inc(l, "qiT"))
                pe.wait_ge(*dve_att(l, "rq1"))
                for h in range(H_A):
                    for t in range(TT):
                        mm = pe.transpose(tok(4 + h // 2)[:, h % 2, t * P:t * P + P],
                                          q_tok[h // 4][:, t, h % 4 * P:h % 4 * P + P], ident)
                mm.then_inc(*pe_att.inc(l, "qT"))
                for i in range(6):
                    pe.wait_ge(*act_att(l, "qiT" if i < 2 else f"s{i - 2}"))
                    heads, t = (range(4 * i, 4 * i + 4), 0) if i < 2 else (range(2 * (i - 2), 2 * (i - 2) + 2), 1)
                    n = T // 2 * (t + 1)
                    for j, h in enumerate(heads):
                        mm = pe.matmul(bank(2 + i % 2)[:, j * n:j * n + n], qiT[:, h // 2, t * P:t * P + P],
                                       kiT[:, h % 2, 0:n], start=True, stop=True)
                    mm.then_inc(*pe_att.inc(l, f"s{i}"))
                r0 = GROUPS * l
                first = sum([pair_pieces(l, ("gate", i), xT) for i in range(GATES_FIRST)], [])
                for k, p in enumerate((prep_1, prep_2, prep_3, prep_4)):
                    p(r0)
                    for piece in first[2 * k:2 * k + 2]:
                        piece()
                for piece in first[8:]:
                    piece()
                for g in range(GROUPS):
                    gaps = {n: [] for n in range(14 + CHUNK_GAPS)}
                    if g + 1 < GROUPS:
                        more = pair_pieces(l, ("rkv", 3 * (g + 1)), xT) + pair_pieces(l, ("rkv", 3 * (g + 1) + 1), xT)
                        for n, p in enumerate(more):
                            gaps[LEVEL_GAPS[n]].append(p)
                    for n, p in enumerate(sum([pair_pieces(l, p, xT) for p in chunk_pairs(g)], [])):
                        gaps[14 + chunk_gap(g, n)].append(p)
                    gaps[6].append(lambda: att_logits(l, g))
                    gaps[10].append(lambda: att_probs(l, g))
                    gaps[12].append(lambda: att_values(l, g))
                    if g + 1 < GROUPS:
                        gaps[13].append(lambda: prep_1(r0 + g + 1))

                    def fill(n):
                        for p in gaps[n]:
                            p()

                    wkv(r0 + g, fill)
                pe.wait_ge(*dve_parts(l, "o1"))
                split_pair(l, ("oa", 0), lambda kb: (block_of(o_hi, kb), rounded["oT"][:, kb, :]))
                split_pair(l, ("oa", 1), lambda kb: (block_of(o_hi, kb), rounded["oT"][:, kb, :]))
                y_back(r0 + GROUPS - 1)
                for i in (2, 3):
                    split_pair(l, ("oa", i), lambda kb: (block_of(o_hi, kb), rounded["oT"][:, kb, :]))
                pe.wait_ge(*dve_parts(l, "yb1"))
                for i in range(4):
                    split_pair(l, ("ob", i), lambda kb: (block_of(yb_hi, kb), rounded["yb"][:, kb, :]))

                def token_major(kind, n, lhs, wait):
                    for i in range(n):
                        w = slot_parts(l, kind, i)
                        wait(i)
                        for t in range(TT):
                            for j in range(2):
                                mm = product(bank(2 + 2 * t + j), [x[:, t * P:t * P + P] for x in lhs(i)],
                                             [x[:, j * 512:j * 512 + 512] for x in w], i == 0, i == n - 1)
                        mm.then_inc(slot_used, 1)

                token_major("out", KB, lambda i: (mix_hi[i], mix_lo[i]),
                            lambda i: pe.wait_ge(*dve_parts(l, f"mix{i // 2}")))
                pe.wait_ge(*dve_x(l, "An"))
                transposed_x(l, "U")
                pe.wait_ge(*dve_parts(l, "x3"))
                for i in range(FB):
                    split_pair(l, ("up", i), lambda kb: (xT_hi[:, kb, :], xT_lo[:, kb, :]))
                token_major("down", FB, lambda i: (hid_hi[i], hid_lo[i]),
                            lambda i: pe.wait_ge(*dve_dense(l, ("up", i))))

        @block.scalar
        def _(act):
            def shift_scaled(l, n, dst, blocks):
                act.wait_ge(*pair_done(l, n))
                src = tok(pair_at[l, n] % 2)
                for b, m in enumerate(blocks):
                    last = act.activation(dst[:, b, :], src[:, b, :], ACT.Identity, scale=dp("omu", m))
                last.then_inc(*act_dense.inc(l, n))

            def rkv(l, g, t):
                r = GROUPS * l + g
                if t == 0 and g:
                    act.wait_ge(*dve_wkv(r - 1, "bv"))
                    act.wait_ge(*dve_prep(r - 1, "rkk"))
                dst = [rs[:, :, :], ks[:, :, :], vs(r)][t]
                shift_scaled(l, ("rkv", 3 * g + t), dst, [8 * t + GB * g + b for b in range(GB)])

            def gate(l, i):
                act.wait_ge(*pair_done(l, ("gate", i)))
                src = tok(pair_at[l, ("gate", i)] % 2)
                for b in range(2):
                    last = act.activation(gates[:, 2 * i + b, :], src[:, b, :], ACT.Tanh, scale=0.5,
                                          bias=dp("hgate", 2 * i + b))
                last.then_inc(*act_dense.inc(l, ("gate", i)))

            def xT_out(l, w):
                for i in range(4):
                    act.wait_ge(*pe_x(l, f"{w}{i}"))
                    dst = xT if w == "T" else xT_hi
                    act.copy(dst[:, 2 * i:2 * i + 2, :], tok(i % 2)).then_inc(*act_x.inc(l, f"{w}{i}"))

            def split_hi(l, m):
                k = l * per_layer + m
                n = SLOT_AT[SPLITS[k]]
                act.wait_ge(landed[n % RING], 16 * (n // RING + 1))
                if m >= NS:
                    act.wait_ge(*used(*SPLITS[k - NS]))
                act.copy(w_hi[m % NS], ring[:, n % RING, :]).then_inc(*act_split.inc(l, m))

            def splits_up_to(l, end):
                for m in range(act_split.next - l * per_layer, min(end, per_layer)):
                    split_hi(l, m)

            def prep_kk(r):
                l, g = divmod(r, GROUPS)
                act.wait_ge(*dve_dense(l, ("rkv", 3 * g + 1)))
                if r:
                    act.wait_ge(*pe_wkv(r - 1, "bonus"))
                for b in range(GB):
                    last = act.activation(tmp[:, b, :], ks[:, b, :], ACT.Square, scale=cp(l, "k_k", GB * g + b))
                last.then_inc(*act_prep.inc(r, "kk2"))

            def prep_tanh(r, what, bias, dst, src):
                g = r % GROUPS
                act.wait_ge(*pe_prep(r, {"thw": "zw", "tha": "za", "thv": "zv"}[what]))
                for b in range(GB):
                    last = act.activation(dst[:, b, :], tok(src)[:, b, :], ACT.Tanh, scale=0.5, bias=dp(bias, GB * g + b))
                last.then_inc(*act_prep.inc(r, what))

            def prep_exp(r):
                g = r % GROUPS
                act.wait_ge(*dve_prep(r, "cp"))
                act.activation(flat(dA), flat(dB), ACT.Exp, scale=-DECAY).then_inc(*act_prep.inc(r, "P"))
                act.activation(flat(dC), flat(dC), ACT.Exp, scale=-DECAY).then_inc(*act_prep.inc(r, "Pp"))
                act.activation(flat(dB), flat(dB), ACT.Exp, scale=DECAY).then_inc(*act_prep.inc(r, "iP"))
                act.wait_ge(*pe_prep(r, "ss"))
                act.wait_ge(*act_prep(r, "tha"))
                for b in range(GB):
                    last = act.activation(tmp[:, b, :], tha[:, b, :], ACT.Identity, scale=dp("hka", GB * g + b),
                                          bias=dp("omhka", GB * g + b))
                last.then_inc(*act_prep.inc(r, "kt"))

            def y_norm(r):
                l, g = divmod(r, GROUPS)
                act.wait_ge(*pe_yT(r, "yT"))
                for b in range(GB):
                    last = act.activation(yt[:, NCH * b:NCH * b + NCH, :].rearrange("p c s -> p (c s)"), tok(6)[:, b, :],
                                          ACT.Identity, scale=cp(l, "g_lnx", GB * g + b), bias=cp(l, "b_lnx", GB * g + b))
                last.then_inc(*act_y.inc(r, "yn"))

            def att_exp(l, g):
                act.wait_ge(*dve_att(l, f"mx{g}"))
                for j in range(4):
                    a, n = (j * T, T) if j < 2 else (2 * T + (j - 2) * P, P)
                    last = act.activation(lg[:, a:a + n], lg[:, a:a + n], ACT.Exp, bias=small[:, 32 + j:33 + j],
                                          accum_out=small[:, 36 + j:37 + j])
                last.then_inc(*act_att.inc(l, f"e{g}"))

            def att_pT(l, g):
                act.wait_ge(*pe_att(l, f"pT{g}"))
                act.copy(pT, ps[:, 6:8, 0:384]).then_inc(*act_att.inc(l, f"pT{g}"))

            def att_o(l, g):
                act.wait_ge(*pe_att(l, f"o{g}"))
                act.copy(oT[:, 2 * g:2 * g + 2, :], tok(6)).then_inc(*act_att.inc(l, f"o{g}"))

            def levels(r, lev):
                for k in range(2):
                    act.wait_ge(*pe_wkv(r, f"W{lev}{k}"))
                    if lev == 1 and k == 0:
                        act.wait_ge(*pe_wkv(r, "tokK"))
                    act.copy(W_bd[:, 4 * k:4 * k + 4, :], units(2)[:, 4 * k:4 * k + 4, :]
                             ).then_inc(*act_wkv.inc(r, f"W{lev}{k}"))

            def z_out(r, c):
                act.wait_ge(*pe_wkv(r, f"Z{c}"))
                act.copy(Zs[:, :, :], bank(2)[:, 0:GB * CH].rearrange("p (b s) -> p b s", s=CH)
                         ).then_inc(*act_wkv.inc(r, f"Z{c}"))

            act.wait_ge(tables, 1)
            act.activation(sines[:, 0, :, :], ang[:, 0, :, :], ACT.Sin)
            act.activation(sines[:, 1, :, :], ang[:, 1, :, :], ACT.Sin).then_inc(tables, 1)
            for l in L2:
                r0 = GROUPS * l
                xT_out(l, "T")
                act.wait_ge(*used(l, "att", 4))
                for t in range(TT):
                    act.copy(p_tok[:, t, 0:512], bank(2 + t))
                act.copy(p_tok[:, :, 512:N_ATT], bank(4)[:, 0:T].rearrange("p (t n) -> p t n", t=TT)[:, :, 0:N_ATT - 512]
                         ).then_inc(*act_att.inc(l, "p"))
                act.wait_ge(*act_att(l, "p"))
                for t in range(TT):
                    last = act.activation(scratch[:, t * D_CQ:t * D_CQ + D_CQ], p_tok[:, t, 0:D_CQ], ACT.Square,
                                          accum_out=small[:, t:t + 1])
                last.then_inc(*act_att.inc(l, "ssq"))
                act.wait_ge(*dve_par(l, "dpar"))
                shift_scaled(l, ("lora", 0), lora[:, 0:2, :], [24, 25])
                act.wait_ge(*dve_dense(l, ("lora", 0)))
                act.activation(lora[0:64, 0, :], lora[0:64, 0, :], ACT.Tanh)
                act.activation(lora[:, 1, :], lora[:, 1, :], ACT.Tanh, scale=0.5).then_inc(*act_lora.inc(l, "tanh"))
                if l:
                    shift_scaled(l, ("vres", 0), lora[:, 2:3, :], [26])
                rkv(l, 0, 0)
                act.wait_ge(*pe_att(l, "cqT"))
                for kb in range(2):
                    last = act.activation(cqT[:, kb, :], tok(6)[:, kb, :], ACT.Identity, scale=cp(l, "g_cq", kb))
                last.then_inc(*act_att.inc(l, "cqT"))
                act.wait_ge(*pe_att(l, "kT"))
                act.wait_ge(zeroed, l + 2)
                act.copy(kT[:, :], bank(7)[:, 0:T])
                act.copy(kiT[q64(0), 0, :], bank(7)[q64(0), T:2 * T])
                act.copy(kiT[q64(1), 1, :], bank(7)[q64(1), T:2 * T]).then_inc(*act_att.inc(l, "kT"))
                rkv(l, 0, 1)
                act.wait_ge(*used(l, "iq", 0))
                for t in range(TT):
                    last = act.copy(qi_tok[:, t, :], bank(2 + t))
                last.then_inc(*act_att.inc(l, "qi"))
                for j in range(2):
                    act.wait_ge(*used(l, "uq", j))
                    for t in range(TT):
                        last = act.copy(q_tok[j][:, t, :], bank(4 + 2 * j + t))
                    last.then_inc(*act_att.inc(l, f"q{j}"))
                rkv(l, 0, 2)
                act.wait_ge(*pe_att(l, "qiT"))
                for i in range(2):
                    last = act.copy(qiT[:, 2 * i:2 * i + 2, :], tok(2 + i))
                last.then_inc(*act_att.inc(l, "qiT"))
                act.wait_ge(*pe_att(l, "qT"))
                for i in range(4):
                    last = act.copy(qT[:, 2 * i:2 * i + 2, :], tok(4 + i))
                last.then_inc(*act_att.inc(l, "qT"))
                for i in range(6):
                    act.wait_ge(*pe_att(l, f"s{i}"))
                    if i >= 2:
                        act.wait_ge(*dve_att(l, f"s0{4 * i - 5}" if i < 4 else f"s1{2 * (i - 4) + 1}"))
                    act.activation(rel[:, i % 2, :], bank(2 + i % 2), ACT.Relu).then_inc(*act_att.inc(l, f"s{i}"))
                prep_kk(r0)
                prep_tanh(r0, "thw", "hw0", dA, 6)
                prep_tanh(r0, "tha", "ha0", tha, 7)
                prep_exp(r0)
                for i in range(GATES_FIRST)[:1]:
                    gate(l, i)
                if l:
                    prep_tanh(r0, "thv", "hv0", kkn, 6)
                for i in range(GATES_FIRST)[1:]:
                    gate(l, i)
                for g in range(GROUPS):
                    r = r0 + g
                    nxt = g + 1 < GROUPS
                    if r:
                        act.wait_ge(*pe_wkv(r - 1, f"y{NCH - 1}"))
                    act.copy(Y_bd[:, :, :], ident.unsqueeze(1).broadcast_to([P, NU, P]))
                    act.copy(X_bd, ident.unsqueeze(1).broadcast_to([P, NU, P])).then_inc(*act_wkv.inc(r, "reset"))
                    act.wait_ge(*(dve_prep(r, "v") if l else dve_dense(l, ("rkv", 3 * g + 2))))
                    for h in range(2):
                        last = act.copy(v_bd[q64(h), :, q64(h)], by_unit(vs(r))[q64(h)])
                    last.then_inc(*act_wkv.inc(r, "vbd"))
                    act.wait_ge(*pe_wkv(r, "V"))
                    act.copy(Vc[:, :, :], unit64(7)).then_inc(*act_wkv.inc(r, "Vc"))
                    act.wait_ge(*pe_wkv(r, "tokB"))
                    for k in range(2):
                        last = act.copy(bt_bd[:, 4 * k:4 * k + 4, :], units(4)[:, 4 * k:4 * k + 4, :])
                    last.then_inc(*act_wkv.inc(r, "tokB"))
                    act.wait_ge(*pe_wkv(r, "tokK"))
                    for k in range(2):
                        last = act.copy(kt_bd[:, 4 * k:4 * k + 4, :], units(4)[:, 4 * k:4 * k + 4, :])
                    last.then_inc(*act_wkv.inc(r, "tokK"))
                    if g:
                        y_norm(r - 1)
                    act.wait_ge(*pe_wkv(r, "zg"))
                    if g:
                        act.wait_ge(*dve_y(r - 1, "yb"))
                    act.copy(gT[:, :, :], tok(7)).then_inc(*act_wkv.inc(r, "g"))
                    if nxt:
                        rkv(l, g + 1, 0)
                    levels(r, 1)
                    levels(r, 2)
                    levels(r, 3)
                    att_exp(l, g)
                    if nxt:
                        rkv(l, g + 1, 1)
                    levels(r, 4)
                    att_pT(l, g)
                    levels(r, 5)
                    att_o(l, g)
                    if nxt:
                        prep_kk(r + 1)
                        prep_tanh(r + 1, "thw", "hw0", dA, 6)
                        prep_tanh(r + 1, "tha", "ha0", tha, 7)
                    for c in range(NCH):
                        z_out(r, c)
                        if c == 0 and nxt:
                            prep_exp(r + 1)
                        for kind, i in pairs_done(g, c):
                            if kind == "gate":
                                gate(l, i)
                            else:
                                rkv(l, g + 1, 2)
                        if c == 1 and nxt and l:
                            prep_tanh(r + 1, "thv", "hv0", kkn, 6)
                        if not nxt and c in (1, 2):
                            act.wait_ge(*act_att(l, f"o{g}"))
                            act.copy(o_hi[c - 1], blocks(oT, 4 * (c - 1), 4)).then_inc(*act_parts.inc(l, f"o{c - 1}"))
                        if not nxt and c >= 2:
                            splits_up_to(l, c)
                    act.wait_ge(*pe_wkv(r, f"y{NCH - 1}"))
                    act.copy(yt[:, :, :], unit64(5)).then_inc(*act_y.inc(r, "y"))
                    act.wait_ge(*dve_y(r, "yc"))
                    act.activation(sq[:, :, :], yt[:, :, :], ACT.Square).then_inc(*act_y.inc(r, "sq"))
                def yb_high(j):
                    act.wait_ge(*dve_y(r0 + GROUPS - 2 + j, "yb"))
                    for i, n in YB_RUNS[j]:
                        last = act.copy(yb_hi_run(i, n), blocks(yb, i, n))
                    last.then_inc(*act_parts.inc(l, f"yb{j}"))

                splits_up_to(l, NS)
                yb_high(0)
                splits_up_to(l, 2 * NS)
                y_norm(r0 + GROUPS - 1)
                yb_high(1)
                for i in range(4):
                    splits_up_to(l, 2 * i + 2 + NS)
                for i in range(4):
                    splits_up_to(l, KB + 2 * i + 2 + NS)
                    act.wait_ge(*dve_x(l, f"mix{i}"))
                    act.copy(rounded["gates"][:, KB + 2 * i:KB + 2 * i + 2, :], gates[:, 2 * i:2 * i + 2, :]
                             ).then_inc(*act_parts.inc(l, f"mix{i}"))
                act.mul(flat(x_tok), flat(x_tok), ALPHA).then_inc(*act_x.inc(l, "Aax"))
                splits_up_to(l, 3 * KB + NS)
                xT_out(l, "U")
                act.mul(flat(x_tok), flat(x_tok), ALPHA).then_inc(*act_x.inc(l, "Bax"))
                for i in range(FB):
                    n = ("up", i)
                    act.wait_ge(*pair_done(l, n))
                    if i >= 2:
                        act.wait_ge(*dve_dense(l, ("up", i - 2)))
                    c, th = conv[i % 2][:, 0, :], conv[i % 2][:, 1, :]
                    act.activation(c, tok(pair_at[l, n] % 2)[:, 0, :], ACT.Identity, scale=cp(l, "conv_w", 2 * FB + i),
                                   bias=cp(l, "conv_b", i)).then_inc(*act_dense.inc(l, n))
                    splits_up_to(l, 3 * KB + 2 * i + 1 + NS)
                    act.wait_ge(*dve_dense(l, (n, "conv")))
                    act.activation(th, c, ACT.Tanh, scale=0.5).then_inc(*act_dense.inc(l, (n, "tanh")))
                    splits_up_to(l, 3 * KB + 2 * i + 2 + NS)
                    act.wait_ge(*dve_dense(l, (n, "whole")))
                    act.copy(hid_hi[i], th).then_inc(*act_dense.inc(l, (n, "hi")))
                splits_up_to(l, per_layer)

        @block.vector
        def _(dve):
            def shift_add(l, n, dst, blocks):
                dve.wait_ge(*act_dense(l, n))
                src = tok(pair_at[l, n] % 2)
                for b, m in enumerate(blocks):
                    last = dve.scalar_tensor_tensor(out=dst[:, b, 1:T], in0=src[:, b, 0:T - 1], scalar=cp(l, "mu", m),
                                                    in1=dst[:, b, 1:T], op0=ALU.mult, op1=ALU.add)
                last.then_inc(*dve_dense.inc(l, n))

            def rkv(l, g, t):
                dst = [rs[:, :, :], ks[:, :, :], vs(GROUPS * l + g)][t]
                shift_add(l, ("rkv", 3 * g + t), dst, [8 * t + GB * g + b for b in range(GB)])

            def rotate(l, name, x1, x2, f0, nf, heads, out1=None, out2=None):
                o1, o2 = out1 or x1, out2 or x2
                n = TT * heads * nf
                t = [yt[:, :, :].rearrange("p u s -> p (u s)")[:, 0:n], sq[:, :, :].rearrange("p u s -> p (u s)")[:, 0:n],
                     *[X_Y[:, i, :, :].rearrange("p u s -> p (u s)")[:, 0:n] for i in range(2)]]
                t = [a.rearrange("p (t h f) -> p t h f", t=TT, h=heads) for a in t]
                sin, cos = [sines[:, i, :, f0:f0 + nf].unsqueeze(2).broadcast_to([P, TT, heads, nf]) for i in range(2)]
                dve.tensor_tensor(t[0], x1, cos, ALU.mult)
                dve.tensor_tensor(t[1], x2, sin, ALU.mult)
                dve.tensor_tensor(t[2], x2, cos, ALU.mult)
                dve.tensor_tensor(t[3], x1, sin, ALU.mult).then_inc(*dve_att.inc(l, f"{name}a"))
                dve.wait_ge(*dve_att(l, f"{name}a"))
                dve.tensor_tensor(o1, t[0], t[1], ALU.subtract)
                return dve.tensor_tensor(o2, t[2], t[3], ALU.add)

            def prep_decay(r):
                if r:
                    dve.wait_ge(*dve_wkv(r - 1, "bv"))
                dve.wait_ge(*act_prep(r, "thw"))
                dve.tensor_scalar(flat(dA), flat(dA), 0.5, 0.5, ALU.mult, ALU.add).then_inc(*dve_prep.inc(r, "s"))
                dve.wait_ge(*dve_prep(r, "s"))
                dve.tensor_tensor_scan(flat(dB), C["scan"], flat(dA), 0.0, ALU.mult, ALU.add).then_inc(*dve_prep.inc(r, "cum"))
                dve.wait_ge(*dve_prep(r, "cum"))
                dve.tensor_tensor(flat(dC), flat(dB), flat(dA), ALU.subtract).then_inc(*dve_prep.inc(r, "cp"))

            def prep_sum(r):
                dve.wait_ge(*act_prep(r, "P"))
                dve.tensor_copy(pend[:, r % 2, :, :], dA[:, :, CH - 1::CH]).then_inc(*dve_prep.inc(r, "pend"))
                dve.wait_ge(*pe_prep(r, "ss"))
                dve.tensor_scalar(ssm[:, :], bank(7)[:, 0:8], 1e-24, None, ALU.max).then_inc(*dve_prep.inc(r, "ss"))

            def prep_rn(r):
                dve.wait_ge(*pe_prep(r, "rnT"))
                dve.tensor_copy(rnT[:, :], bank(7)[0:8, 128:256]).then_inc(*dve_prep.inc(r, "rnT"))
                if r >= GROUPS:
                    g = r % GROUPS
                    dve.wait_ge(*act_prep(r, "thv"))
                    dve.wait_ge(*dve_dense(r // GROUPS, ("rkv", 3 * g + 2)))
                    if g:
                        dve.wait_ge(*pe_att(r // GROUPS, f"o{g - 1}"))
                    dve.tensor_tensor(y_bd_free(r), flat2(v_first[:, GB * g:GB * g + GB, :]), flat(vs_own), ALU.subtract
                                      ).then_inc(*dve_prep.inc(r, "v1"))
                    dve.wait_ge(*dve_prep(r, "v1"))
                    dve.scalar_tensor_tensor(out=y_bd_free(r), in0=flat(kkn), scalar=1.0, in1=y_bd_free(r), op0=ALU.add,
                                             op1=ALU.mult).then_inc(*dve_prep.inc(r, "v2"))
                    dve.wait_ge(*dve_prep(r, "v2"))
                    dve.scalar_tensor_tensor(out=flat(vs_own), in0=y_bd_free(r), scalar=0.5, in1=flat(vs_own), op0=ALU.mult,
                                             op1=ALU.add).then_inc(*dve_prep.inc(r, "v"))

            def y_bd_free(r):
                return vtmp[:, :]

            def flat2(t):
                return t.rearrange("p a b -> p (a b)")

            def prep_rest(r):
                l, g = divmod(r, GROUPS)
                dve.wait_ge(*pe_prep(r, "rnx"))
                for b in range(GB):
                    last = dve.scalar_tensor_tensor(out=kkn[:, b, :], in0=ks[:, b, :], scalar=cp(l, "k_k", GB * g + b),
                                                    in1=tok(6)[:, b, :], op0=ALU.mult, op1=ALU.mult)
                last.then_inc(*dve_prep.inc(r, "kkn"))
                dve.wait_ge(*act_prep(r, "kt"))
                dve.wait_ge(*dve_prep(r, "kkn"))
                dve.tensor_tensor(flat(ks), flat(ks), flat(tmp), ALU.mult).then_inc(*dve_prep.inc(r, "k2"))
                dve.scalar_tensor_tensor(out=flat(tha), in0=flat(tha), scalar=1.0, in1=flat(kkn), op0=ALU.add, op1=ALU.mult
                                         ).then_inc(*dve_prep.inc(r, "kb"))
                dve.tensor_tensor(arc[:, :, 0, :], by_unit(kkn[:, :, :]), by_unit(dC[:, :, :]), ALU.mult)
                dve.tensor_tensor(arc[:, :, 1, :], by_unit(rs[:, :, :]), by_unit(dA[:, :, :]), ALU.mult
                                  ).then_inc(*dve_prep.inc(r, "arc"))
                if g == 0:
                    dve.wait_ge(zeroed, l + 2)
                dve.wait_ge(*act_prep(r, "iP"))
                dve.wait_ge(*dve_prep(r, "kb"))
                for h in range(2):
                    last = dve.scalar_tensor_tensor(out=b_bd[q64(h), :, q64(h)], in0=by_unit(tha[:, :, :])[q64(h)], scalar=-0.5,
                                                    in1=by_unit(dB[:, :, :])[q64(h)], op0=ALU.mult, op1=ALU.mult)
                last.then_inc(*dve_prep.inc(r, "bneg"))
                for h in range(2):
                    last = dve.tensor_tensor(k_bd[q64(h), :, q64(h)], by_unit(ks[:, :, :])[q64(h)],
                                             by_unit(dB[:, :, :])[q64(h)], ALU.mult)
                last.then_inc(*dve_prep.inc(r, "kp"))

            def prep_bonus(r):
                l, g = divmod(r, GROUPS)
                dve.wait_ge(*dve_prep(r, "kp"))
                for b in range(GB):
                    last = dve.scalar_tensor_tensor(out=tmp[:, b, :], in0=rs[:, b, :], scalar=cp(l, "r_k", GB * g + b),
                                                    in1=ks[:, b, :], op0=ALU.mult, op1=ALU.mult)
                last.then_inc(*dve_prep.inc(r, "rkk"))

            def masked(r, name, dst, src, half_, mask):
                for h in range(2):
                    last = dve.tensor_tensor(dst[q64(h), :, q64(h)], units(src)[q64(h), :, half_ * CH:half_ * CH + CH],
                                             mask[q64(h)].unsqueeze(1).broadcast_to([64, NU, CH]), ALU.mult)
                last.then_inc(*dve_wkv.inc(r, name))

            def mask_of(which, lev, q=slice(0, P)):
                m = masks[q, which, lev, :]
                return m.unsqueeze(1).broadcast_to([q.stop - q.start, NU, CH])

            def update(r, dst, name, which, lev, k, src):
                by_head = lambda t: t[:, 4 * k:4 * k + 4, :].rearrange("p u (h s) -> p (u h) s", h=2)
                dve.copy_predicated(by_head(dst), mask_of(which, lev), by_head(units(src))
                                    ).then_inc(*dve_wkv.inc(r, name))

            def grams(r):
                dve.wait_ge(*pe_wkv(r, "gramB"))
                if r % GROUPS == 0:
                    dve.wait_ge(zeroed, r // GROUPS + 2)
                masked(r, "nT", nT_bd, 2, 0, C["strict"])
                masked(r, "Arb", rb_bd, 2, 1, C["incl"])
                dve.wait_ge(*act_wkv(r, "reset"))
                for h in range(2):
                    last = dve.copy_predicated(Y_bd[q64(h), :, q64(h)], mask_of(0, 0, q64(h)), units(2)[q64(h), :, 0:CH])
                last.then_inc(*dve_wkv.inc(r, "Y0"))
                dve.wait_ge(*pe_wkv(r, "gramK"))
                masked(r, "Aak", ak_bd, 4, 0, C["strict"])
                masked(r, "Ark", rk_bd, 4, 1, C["incl"])
                dve.wait_ge(*pe_wkv(r, "nX"))
                for k in range(2):
                    update(r, X_bd, f"X0{k}", 1, 0, k, 2)

            def level(r, lev):
                for k in range(2):
                    if lev < LEVELS - 1:
                        dve.wait_ge(*pe_wkv(r, f"XW{lev}{k}"))
                        update(r, X_bd, f"X{lev}{k}", 1, lev, k, 4)
                    dve.wait_ge(*pe_wkv(r, f"WtY{lev}{k}"))
                    update(r, Y_bd, f"Y{lev}{k}", 0, lev, k, 2)

            def chunk(r, c):
                two = lambda n: bank(n)[:, 0:GB * CH].rearrange("p (b s) -> p b s", s=CH)
                dve.wait_ge(*pe_wkv(r, f"Q{c}"))
                dve.tensor_copy(Qs[:, :, :], two(3)).then_inc(*dve_wkv.inc(r, f"Q{c}"))
                if c < NCH - 1:
                    src = two(4)
                    dve.wait_ge(*pe_wkv(r, f"S{c}"))
                    if c:
                        dve.tensor_tensor(Sa[:, :, :], src, S[:, (c + 1) % 2, :, :], ALU.add
                                          ).then_inc(*dve_wkv.inc(r, f"S{c}a"))
                        dve.wait_ge(*dve_wkv(r, f"S{c}a"))
                        src = Sa[:, :, :]
                    dve.tensor_tensor(S[:, c % 2, :, :], src, pend[:, r % 2, :, c:c + 1].broadcast_to([P, GB, CH]), ALU.mult
                                      ).then_inc(*dve_wkv.inc(r, f"S{c}"))

            def y_center(r):
                dve.wait_ge(*act_y(r, "y"))
                dve.tensor_reduce(g8[:, 0, :], yt[:, :, :], AX, ALU.add).then_inc(*dve_y.inc(r, "m"))
                dve.wait_ge(*dve_y(r, "m"))
                dve.tensor_scalar(g8[:, 1, :], g8[:, 0, :], -1.0 / N_R, None, ALU.mult).then_inc(*dve_y.inc(r, "m2"))
                dve.wait_ge(*dve_y(r, "m2"))
                dve.tensor_tensor(yt[:, :, :], yt[:, :, :], g8[:, 1, :].unsqueeze(2).broadcast_to([P, NU, CH]), ALU.add
                                  ).then_inc(*dve_y.inc(r, "yc"))

            def y_var(r):
                dve.wait_ge(*act_y(r, "sq"))
                dve.tensor_reduce(g8[:, 2, :], sq[:, :, :], AX, ALU.add).then_inc(*dve_y.inc(r, "v8"))

            def y_scale(r):
                dve.wait_ge(*pool_y(r, "rstd"))
                for h in range(2):
                    last = dve.tensor_tensor(y_bd[q64(h), :, q64(h)], yt[q64(h), :, :],
                                             g8[q64(h), 4, :].unsqueeze(2).broadcast_to([64, NU, CH]), ALU.mult)
                last.then_inc(*dve_y.inc(r, "yr"))

            def y_out(r):
                g = r % GROUPS
                dve.wait_ge(*act_y(r, "yn"))
                dve.tensor_tensor(flat(yt), flat(yt), flat(bv), ALU.add).then_inc(*dve_y.inc(r, "yb1"))
                dve.wait_ge(*dve_y(r, "yb1"))
                dve.tensor_tensor(flat2(yb[:, GB * g:GB * g + GB, :]), flat(yt), flat(gT), ALU.mult
                                  ).then_inc(*dve_y.inc(r, "yb"))

            def bonus(r):
                dve.wait_ge(*pe_wkv(r, "bonus"))
                dve.tensor_tensor(flat(bv), bank(6), flat2(vs(r)), ALU.mult).then_inc(*dve_wkv.inc(r, "bv"))

            def att_masked(l, g):
                dve.wait_ge(*pe_att(l, f"lg{g}"))
                if g == 0:
                    dve.wait_ge(*dve_att(l, "keep1"))
                for t, a, n in ((1, 0, T), (0, 2 * T, P)):
                    last = dve.scalar_tensor_tensor(
                        out=lg[:, a:a + 2 * n].rearrange("p (h s) -> p h s", h=2),
                        in0=bank(7 - t)[:, 0:2 * n].rearrange("p (h s) -> p h s", h=2), scalar=DH_A ** -0.5,
                        in1=keep[:, t, 0:n].unsqueeze(1).broadcast_to([P, 2, n]), op0=ALU.mult, op1=ALU.add)
                last.then_inc(*dve_att.inc(l, f"lg{g}"))
                dve.wait_ge(*dve_att(l, f"lg{g}"))
                for j, a, n in ((32, 0, T), (34, 2 * T, P)):
                    last = dve.tensor_reduce(small[:, j:j + 2], lg[:, a:a + 2 * n].rearrange("p (h s) -> p h s", h=2), AX,
                                             ALU.max, negate=True)
                last.then_inc(*dve_att.inc(l, f"mx{g}"))

            def att_norm(l, g):
                dve.wait_ge(*act_att(l, f"e{g}"))
                dve.reciprocal(small[:, 40:44], small[:, 36:40]).then_inc(*dve_att.inc(l, f"rc{g}"))
                dve.wait_ge(*dve_att(l, f"rc{g}"))
                for j in range(4):
                    a, n = (j * T, T) if j < 2 else (2 * T + (j - 2) * P, P)
                    last = dve.tensor_scalar(lg[:, a:a + n], lg[:, a:a + n], small[:, 40 + j:41 + j], None, ALU.mult)
                last.then_inc(*dve_att.inc(l, f"pn{g}"))

            def splits_up_to(l, end):
                for m in range(dve_split.next - l * per_layer, min(end, per_layer)):
                    k = l * per_layer + m
                    n = SLOT_AT[SPLITS[k]]
                    dve.wait_ge(*act_split(l, m))
                    dve.tensor_tensor(w_lo[m % NS], ring[:, n % RING, :], f32(w_hi[m % NS]), ALU.subtract
                                      ).then_inc(*dve_split.inc(l, m))

            def mix_rest(l, i):
                dve.wait_ge(*act_parts(l, f"mix{i}"))
                parts = rounded["gates"]
                dve.tensor_tensor(parts[:, 2 * i:2 * i + 2, :], gates[:, 2 * i:2 * i + 2, :],
                                  f32(parts[:, KB + 2 * i:KB + 2 * i + 2, :]), ALU.subtract
                                  ).then_inc(*dve_parts.inc(l, f"mix{i}"))

            def layer_norm(l, w, kind, n):
                s = 0.5 if w == "A" else 1.0
                i = 2 * l + "AB".index(w)
                dve.wait_ge(*used(l, kind, n - 1))
                dve.wait_ge(*act_x(l, f"{w}ax"))
                for t in range(TT):
                    for j in range(2):
                        c = slice(512 * j, 512 * j + 512)
                        last = dve.scalar_tensor_tensor(out=x_tok[:, t, c], in0=bank(2 + 2 * t + j), scalar=s,
                                                        in1=x_tok[:, t, c], op0=ALU.mult, op1=ALU.add)
                last.then_inc(*dve_x.inc(l, f"{w}add"))
                dve.wait_ge(*dve_x(l, f"{w}add"))
                for t in range(TT):
                    for j in range(2):
                        last = dve.bn_stats(ln[:, t, 6 * j:6 * j + 6], x_tok[:, t, 512 * j:512 * j + 512])
                last.then_inc(*dve_x.inc(l, f"{w}st"))
                dve.wait_ge(*dve_x(l, f"{w}st"))
                for t in range(TT):
                    last = dve.bn_aggr(ln[:, t, 12:14], ln[:, t, 0:12])
                last.then_inc(*dve_x.inc(l, f"{w}mv"))
                dve.wait_ge(*dve_x(l, f"{w}mv"))
                dve.wait_ge(rows_landed, 32 * (i + 1))
                for t in range(TT):
                    last = dve.scalar_tensor_tensor(out=x_tok[:, t, :], in0=x_tok[:, t, :], scalar=ln[:, t, 12:13],
                                                    in1=lnrow[0], op0=ALU.subtract, op1=ALU.mult)
                last.then_inc(*dve_x.inc(l, f"{w}c"))
                dve.wait_ge(*dve_x(l, f"{w}c"))
                dve.wait_ge(*pool_x(l, w))
                for t in range(TT):
                    last = dve.scalar_tensor_tensor(out=x_tok[:, t, :], in0=x_tok[:, t, :], scalar=ln[:, t, 21:22],
                                                    in1=lnrow[1], op0=ALU.mult, op1=ALU.add)
                last.then_inc(*dve_x.inc(l, f"{w}n"))

            turn = 2 * math.pi
            c1 = 6.28125
            c2 = 0.0019340515136718750
            c3 = turn - c1 - c2
            magic = 1.5 * 2 ** 23
            dve.wait_ge(inputs_in, 16 * 5)
            dve.tensor_copy(posf[:, :], pos[:, :]).then_inc(tables_dve, 1)
            dve.wait_ge(tables_dve, 1)
            for t in range(TT):
                last = dve.tensor_scalar(ang[:, 0, t, :], C["freq"], posf[:, t:t + 1], None, ALU.mult)
            last.then_inc(tables_dve, 1)
            dve.wait_ge(tables_dve, 2)
            a0, a1 = ang[:, 0, :, :], ang[:, 1, :, :]
            dve.tensor_scalar(a1, a0, 1.0 / turn, magic, ALU.mult, ALU.add).then_inc(tables_dve, 1)
            dve.wait_ge(tables_dve, 3)
            dve.tensor_scalar(a1, a1, magic, None, ALU.subtract).then_inc(tables_dve, 1)
            for i, c in enumerate((c1, c2, c3)):
                dve.wait_ge(tables_dve, 4 + i)
                dve.scalar_tensor_tensor(out=a0, in0=a1, scalar=-c, in1=a0, op0=ALU.mult, op1=ALU.add).then_inc(tables_dve, 1)
            dve.wait_ge(tables_dve, 7)
            dve.tensor_scalar(a0, a0, math.pi, -math.pi, ALU.min, ALU.max).then_inc(tables_dve, 1)
            dve.wait_ge(tables_dve, 8)
            dve.scalar_tensor_tensor(out=a1, in0=a0, scalar=-1.0, in1=a0, op0=ALU.mult, op1=ALU.max).then_inc(tables_dve, 1)
            dve.wait_ge(tables_dve, 9)
            dve.tensor_scalar(a1, a1, -1.0, math.pi / 2, ALU.mult, ALU.add).then_inc(tables, 1)

            for l in L2:
                r0 = GROUPS * l
                if l:
                    dve.wait_ge(*act_dense(l - 1, ("gate", 7)))
                dve.tensor_scalar(dp("omu", 0, 27), cp(l, "mu", 0, 27), -1.0, 1.0, ALU.mult, ALU.add)
                for a, b, n in (("hw0", "w0", 8), ("ha0", "a0", 8), ("hv0", "v0", 8), ("hgate", "b_gate", 16), ("hka", "k_a", 8)):
                    dve.tensor_scalar(dp(a, 0, n), cp(l, b, 0, n), 0.5, None, ALU.mult)
                dve.tensor_scalar(dp("omhka", 0, 8), cp(l, "k_a", 0, 8), -0.5, 1.0, ALU.mult, ALU.add
                                  ).then_inc(*dve_par.inc(l, "dpar"))
                dve.wait_ge(*act_att(l, "p"))
                dve.tensor_scalar(p_tok[:, :, C_IW:C_IW + H_IDX], p_tok[:, :, C_IW:C_IW + H_IDX],
                                  H_IDX ** -0.5 * D_IDX ** -0.5, None, ALU.mult).then_inc(*dve_att.inc(l, "wi"))
                for t in range(TT):
                    last = dve.bn_stats(ln[:, t, 0:6], p_tok[:, t, C_IK:C_IK + D_IDX])
                last.then_inc(*dve_att.inc(l, "kst"))
                dve.wait_ge(*dve_att(l, "kst"))
                for t in range(TT):
                    last = dve.bn_aggr(ln[:, t, 12:14], ln[:, t, 0:6])
                last.then_inc(*dve_att.inc(l, "kmv"))
                dve.wait_ge(tables, 2)
                kv = p_tok[:, :, C_K:C_K + ROT_A].rearrange("p t (h f) -> p t h f", h=1)
                if l:
                    dve.wait_ge(*act_y(r0 - 1, "yn"))
                rotate(l, "rk", kv[:, :, :, 0:16], kv[:, :, :, 16:32], 0, 16, 1).then_inc(*dve_att.inc(l, "rk"))
                shift_add(l, ("lora", 0), lora[:, 0:2, :], [24, 25])
                dve.wait_ge(*pool_att(l, "rs"))
                for t in range(TT):
                    last = dve.tensor_scalar(p_tok[:, t, 0:D_CQ], p_tok[:, t, 0:D_CQ], small[:, 8 + t:9 + t], None, ALU.mult)
                last.then_inc(*dve_att.inc(l, "cq"))
                dve.wait_ge(lora_landed, 32 * (l + 1))
                ik = p_tok[:, :, C_IK:C_IK + D_IDX]
                for t in range(TT):
                    last = dve.scalar_tensor_tensor(out=ik[:, t, :], in0=ik[:, t, :], scalar=ln[:, t, 12:13],
                                                    in1=kirow[:, 0:D_IDX], op0=ALU.subtract, op1=ALU.mult)
                last.then_inc(*dve_att.inc(l, "kic"))
                dve.wait_ge(*dve_att(l, "kic"))
                for t in range(TT):
                    last = dve.scalar_tensor_tensor(out=ik[:, t, :], in0=ik[:, t, :], scalar=small[:, 10 + t:11 + t],
                                                    in1=kirow[:, D_IDX:2 * D_IDX], op0=ALU.mult, op1=ALU.add)
                last.then_inc(*dve_att.inc(l, "ki"))
                dve.wait_ge(*dve_att(l, "ki"))
                dve.wait_ge(*dve_att(l, "rk"))
                ikh = ik.rearrange("p t (h f) -> p t h f", h=1)
                rotate(l, "rki", ikh[:, :, :, 0:8], ikh[:, :, :, 8:16], 16, 8, 1,
                       out1=kid[:, :, 0:1, 0:8], out2=kid[:, :, 0:1, 8:16])
                dve.tensor_copy(kid[:, :, 0, 16:64], ik[:, :, 16:64]).then_inc(kid_half, 1)
                dve.wait_ge(kid_half, l + 1)
                dve.tensor_copy(kid[:, :, 1, :], kid[:, :, 0, :]).then_inc(*dve_att.inc(l, "rki"))
                dve.wait_ge(*act_lora(l, "tanh"))
                dve.tensor_scalar(lora[:, 1, :], lora[:, 1, :], 0.5, 0.5, ALU.mult, ALU.add)
                if l:
                    shift_add(l, ("vres", 0), lora[:, 2:3, :], [26])
                rkv(l, 0, 0)
                dve.tensor_copy(vtmp[:, 0:1], const[:, 0:1]).then_inc(*dve_par.inc(l, "lsig"))
                rkv(l, 0, 1)
                dve.wait_ge(*act_att(l, "qi"))
                qv = qi_tok.rearrange("p t (h f) -> p t h f", h=H_IDX)
                rotate(l, "rqi", qv[:, :, :, 0:8], qv[:, :, :, 8:16], 16, 8, H_IDX).then_inc(*dve_att.inc(l, "rqi"))
                for j in range(2):
                    dve.wait_ge(*act_att(l, f"q{j}"))
                    dve.wait_ge(*dve_att(l, "rqi" if j == 0 else "rq0"))
                    qv = q_tok[j].rearrange("p t (h f) -> p t h f", h=4)
                    rotate(l, f"rq{j}", qv[:, :, :, 0:16], qv[:, :, :, 16:32], 0, 16, 4).then_inc(*dve_att.inc(l, f"rq{j}"))
                rkv(l, 0, 2)
                for i in range(6):
                    dve.wait_ge(*act_att(l, f"s{i}"))
                    heads, t = (range(4 * i, 4 * i + 4), 0) if i < 2 else (range(2 * (i - 2), 2 * (i - 2) + 2), 1)
                    n = P * (t + 1)
                    for j, h in enumerate(heads):
                        wi = p_tok[:, t, C_IW + h:C_IW + h + 1]
                        src = rel[:, i % 2, j * n:j * n + n]
                        if h == 0:
                            last = dve.tensor_scalar(keep[:, t, 0:n], src, wi, None, ALU.mult)
                        else:
                            dve.wait_ge(*dve_att(l, f"s{t}{h - 1}"))
                            last = dve.scalar_tensor_tensor(out=keep[:, t, 0:n], in0=src, scalar=wi, in1=keep[:, t, 0:n],
                                                            op0=ALU.mult, op1=ALU.add)
                        last.then_inc(*dve_att.inc(l, f"s{t}{h}"))
                def topk(t):
                    dve.wait_ge(*dve_att(l, f"s{t}{H_IDX - 1}"))
                    kp = keep[:, t, 0:P * (t + 1)]
                    dve.tensor_tensor(keep[:, t, t * P:t * P + P], keep[:, t, t * P:t * P + P], C["causal"], ALU.add
                                      ).then_inc(*dve_att.inc(l, f"causal{t}"))
                    for i in range(TOPK // 8):
                        dve.wait_ge(*dve_att(l, f"causal{t}" if i == 0 else f"rep{t}{i - 1}"))
                        dve.max(small[:, 16:24], kp).then_inc(*dve_att.inc(l, f"max{t}{i}"))
                        dve.wait_ge(*dve_att(l, f"max{t}{i}"))
                        dve.match_replace(kp, small[:, 16:24], kp, TAKEN).then_inc(*dve_att.inc(l, f"rep{t}{i}"))
                    dve.wait_ge(*dve_att(l, f"rep{t}{TOPK // 8 - 1}"))
                    dve.tensor_scalar(kp, kp, TAKEN / 2, -NEG, ALU.is_lt, ALU.mult).then_inc(*dve_att.inc(l, f"sel{t}"))
                    dve.wait_ge(*dve_att(l, f"sel{t}"))
                    dve.tensor_scalar(kp, kp, NEG, None, ALU.add).then_inc(*dve_att.inc(l, f"selb{t}"))
                    dve.wait_ge(*dve_att(l, f"selb{t}"))
                    dve.tensor_tensor(keep[:, t, t * P:t * P + P], keep[:, t, t * P:t * P + P], C["causal"], ALU.add
                                      ).then_inc(*dve_att.inc(l, f"keep{t}"))

                prep_decay(r0)
                prep_sum(r0)
                topk(0)
                prep_rn(r0)
                topk(1)
                prep_rest(r0)
                prep_bonus(r0)
                for g in range(GROUPS):
                    r = r0 + g
                    nxt = g + 1 < GROUPS
                    grams(r)
                    if g:
                        y_scale(r - 1)
                        y_out(r - 1)
                    bonus(r)
                    if nxt:
                        rkv(l, g + 1, 0)
                    level(r, 1)
                    level(r, 2)
                    att_masked(l, g)
                    level(r, 3)
                    if nxt:
                        rkv(l, g + 1, 1)
                    att_norm(l, g)
                    level(r, 4)
                    level(r, 5)
                    if nxt:
                        prep_decay(r + 1)
                    for c in range(NCH):
                        chunk(r, c)
                        if any(kind == "rkv" for kind, _ in pairs_done(g, c)):
                            rkv(l, g + 1, 2)
                        if nxt and c < NCH - 1:
                            [prep_sum, prep_rn, prep_rest][c](r + 1)
                        if not nxt and c in (1, 2):
                            dve.wait_ge(*act_parts(l, f"o{c - 1}"))
                            dve.tensor_tensor(blocks(rounded["oT"], 4 * (c - 1), 4), blocks(oT, 4 * (c - 1), 4),
                                              f32(o_hi[c - 1]), ALU.subtract).then_inc(*dve_parts.inc(l, f"o{c - 1}"))
                        if not nxt and c >= 2:
                            splits_up_to(l, c)
                    y_center(r)
                    if nxt:
                        prep_bonus(r + 1)
                    y_var(r)
                def yb_low(j):
                    dve.wait_ge(*act_parts(l, f"yb{j}"))
                    for i, n in YB_RUNS[j]:
                        last = dve.tensor_tensor(blocks(rounded["yb"], i, n), blocks(yb, i, n), f32(yb_hi_run(i, n)),
                                                 ALU.subtract)
                    last.then_inc(*dve_parts.inc(l, f"yb{j}"))

                def gated_o(i):
                    dve.wait_ge(*pair_done(l, ("oa", i)))
                    dve.wait_ge(*act_dense(l, ("gate", 7)))
                    dst = flat2(gates[:, 2 * i:2 * i + 2, :])
                    dve.scalar_tensor_tensor(out=dst, in0=dst, scalar=1.0, in1=bank(pair_at[l, ("oa", i)] % 2), op0=ALU.add,
                                             op1=ALU.mult).then_inc(*dve_dense.inc(l, ("oa", i)))

                splits_up_to(l, NS)
                y_scale(r0 + GROUPS - 1)
                splits_up_to(l, NS + 1)
                gated_o(0)
                yb_low(0)
                splits_up_to(l, 2 * NS)
                y_out(r0 + GROUPS - 1)
                yb_low(1)
                for i in range(1, 4):
                    splits_up_to(l, 2 * i + 2 + NS)
                    gated_o(i)
                for i in range(4):
                    splits_up_to(l, KB + 2 * i + 2 + NS)
                    dve.wait_ge(*pair_done(l, ("ob", i)))
                    dst = flat2(gates[:, KB + 2 * i:KB + 2 * i + 2, :])
                    dve.scalar_tensor_tensor(out=dst, in0=dst, scalar=1.0, in1=bank(pair_at[l, ("ob", i)] % 2), op0=ALU.add,
                                             op1=ALU.mult).then_inc(*dve_dense.inc(l, ("ob", i)))
                    dve.wait_ge(*dve_dense(l, ("ob", i)))
                    a = flat2(gates[:, 2 * i:2 * i + 2, :])
                    dve.tensor_tensor(a, a, dst, ALU.add).then_inc(*dve_x.inc(l, f"mix{i}"))
                    if i:
                        mix_rest(l, i - 1)
                mix_rest(l, 3)
                splits_up_to(l, 3 * KB + NS)
                layer_norm(l, "A", "out", KB)
                for i in range(4):
                    dve.wait_ge(*act_x(l, f"U{i}"))
                    dve.tensor_tensor(xT_lo[:, 2 * i:2 * i + 2, :], tok(i % 2), f32(xT_hi[:, 2 * i:2 * i + 2, :]), ALU.subtract
                                      ).then_inc(*dve_parts.inc(l, f"x{i}"))
                for i in range(FB):
                    n = ("up", i)
                    c, th = conv[i % 2][:, 0, :], conv[i % 2][:, 1, :]
                    src = tok(pair_at[l, n] % 2)
                    for k in (1, 2):
                        dve.wait_ge(*(act_dense(l, n) if k == 1 else dve_dense(l, (n, "conv1"))))
                        dve.scalar_tensor_tensor(out=c[:, k:T], in0=src[:, 0, 0:T - k], scalar=cp(l, "conv_w", (2 - k) * FB + i),
                                                 in1=c[:, k:T], op0=ALU.mult, op1=ALU.add
                                                 ).then_inc(*dve_dense.inc(l, (n, "conv1" if k == 1 else "conv")))
                    splits_up_to(l, 3 * KB + 2 * i + 1 + NS)
                    dve.wait_ge(*act_dense(l, (n, "tanh")))
                    dve.scalar_tensor_tensor(out=c, in0=th, scalar=1.0, in1=c, op0=ALU.add, op1=ALU.mult
                                             ).then_inc(*dve_dense.inc(l, (n, "silu")))
                    dve.wait_ge(*dve_dense(l, (n, "silu")))
                    dve.scalar_tensor_tensor(out=th, in0=c, scalar=0.5, in1=src[:, 1, :], op0=ALU.mult, op1=ALU.mult
                                             ).then_inc(*dve_dense.inc(l, (n, "whole")))
                    splits_up_to(l, 3 * KB + 2 * i + 2 + NS)
                    dve.wait_ge(*act_dense(l, (n, "hi")))
                    dve.tensor_tensor(hid_lo[i], th, f32(hid_hi[i]), ALU.subtract).then_inc(*dve_dense.inc(l, n))
                splits_up_to(l, per_layer)
                layer_norm(l, "B", "down", FB)


def _blocks(w):
    n = -(-w.shape[1] // P) * P
    w = np.pad(w, ((0, 0), (0, n - w.shape[1])))
    return w.reshape(KB, P, n // P, P).transpose(2, 1, 0, 3).reshape(n // P, P, D)


def _rows(w):
    return w.reshape(-1, P, D)


def _halves(w):
    return w.reshape(2, P, -1, 512).transpose(2, 1, 0, 3).reshape(-1, P, D)


def _columns(v):
    return v.reshape(-1, P).T


def _consts():
    c = np.zeros((P, NCONST), np.float32)
    at = {n: slice(CONST_AT[n], CONST_AT[n] + w) for n, w in CONST}
    p, s = np.arange(P)[:, None], np.arange(CH)[None]
    c[:, at["ident"]] = np.eye(P)
    c[:, at["stack"]] = p % CH == s
    c[:, at["strict"]] = p % CH < s
    c[:, at["incl"]] = p % CH <= s
    c[:, at["hsel"]] = p // CH == np.arange(2)[None]
    c[:, at["bones"]] = p // CH == np.arange(P)[None] // CH
    col = np.arange(512)[None]
    c[:8, at["rowsel"]] = np.arange(8)[:, None] == 2 * (col // P) + col % P // CH
    c[:, at["scan"]] = col % CH != 0
    c[:, at["causal"]] = np.where(np.arange(P)[None] <= p, 0, NEG)
    f = [THETA ** (-2 * i / ROT_A) for i in range(ROT_A // 2)] + [THETA ** (-2 * i / ROT_IDX) for i in range(ROT_IDX // 2)]
    c[:, at["freq"]] = np.array(f)
    m = np.zeros((P, 2, LEVELS, CH), np.uint32)
    for lev in range(LEVELS):
        n = 1 << lev
        row, colm = p % CH, s
        upper = (row // (2 * n) == colm // (2 * n)) & (row % (2 * n) < n) & (colm % (2 * n) >= n)
        lower = (row // (2 * n) == colm // (2 * n)) & (row % (2 * n) >= n) & (colm % (2 * n) < n)
        m[:, 0, lev], m[:, 1, lev] = upper, lower
    return c, m.reshape(P, -1)


def kernel(**inputs):
    import concourse.bacc as _bacc
    from concourse.bass_utils import run_bass_kernel_spmd as _run

    a = {n: np.asarray(v) for n, v in inputs.items()}
    stream = []
    cpar = np.zeros((P, DEPTH, NCPAR), np.float32)
    lora = np.zeros((DEPTH, P, 3, D), np.float32)
    rpar = np.zeros((DEPTH, 4 * D + 2 * D_IDX), np.float32)
    for l in range(DEPTH):
        w_in = a["w_in0"] if l == 0 else a["w_in_rest"][l - 1]
        rw = w_in[:, N_ATT + N_GATE:N_IN0]
        parts = {"att": _blocks(w_in[:, :N_ATT]), "gate": _blocks(w_in[:, N_ATT:N_ATT + N_GATE]),
                 "rkv": _blocks(rw[:, :3 * D]), "lora": _blocks(rw[:, 3 * D:]), "vres": _blocks(w_in[:, N_IN0:]),
                 "iq": _halves(a["w_iq"][l]), "uq": _halves(a["w_uq"][l]),
                 "oa": _blocks(a["w_oa"][l]), "ob": _blocks(a["w_ob"][l]), "out": _rows(a["w_out"][l]),
                 "up": _blocks(a["w_up"][l]), "down": _rows(a["w_down"][l])}
        stream += [parts[kind][i] for kind, i in stream_order(l)]
        mu = np.zeros(27 * P, np.float32)
        mu[:N_RWKV] = a["mu_rwkv"][l]
        v0 = np.zeros(D, np.float32)
        if l:
            mu[N_RWKV:N_RWKV + LORA_V] = a["mu_vres"][l - 1]
            v0 = a["v0"][l - 1]
            lora[l, :LORA_V, 2] = a["v2"][l - 1]
        for name, v in (("mu", mu), ("v0", v0), *((n, a[n][l]) for n, _ in CPAR if n not in ("mu", "v0"))):
            c = _columns(np.asarray(v).reshape(-1))
            cpar[:, l, CPAR_AT[name]:CPAR_AT[name] + c.shape[1]] = c
        lora[l, :LORA_W, 0], lora[l, LORA_W:, 0], lora[l, :, 1] = a["w2"][l], a["a2"][l], a["g2"][l]
        rpar[l] = np.concatenate([a[n][l] for n in ("ln1_g", "ln1_b", "ln2_g", "ln2_b", "g_ik", "b_ik")])
    const, masks = _consts()
    arrays = {"x_dram": a["x"][0], "pos_dram": np.ascontiguousarray(a["positions"][0].reshape(TT, P).T),
              "stream_dram": np.stack(stream), "lora_dram": lora.reshape(DEPTH, P, 3 * D),
              "cpar_dram": cpar.reshape(P, -1), "rpar_dram": rpar, "const_dram": const, "masks_dram": masks}
    nc = _bacc.Bacc("TRN2", target_bir_lowering=False, num_devices=1)
    args = []
    for name, v in arrays.items():
        arrays[name] = v = np.ascontiguousarray(v)
        args.append(nc.dram_tensor(name, v.shape, mybir.dt.from_np(v.dtype), kind="ExternalInput").ap())
    args.append(nc.dram_tensor("out_dram", (T, D), F32, kind="ExternalOutput").ap())
    trunk(nc, *args)
    r = _run(nc, [arrays], core_ids=[0])
    return r.results[0]["out_dram"].reshape(1, T, D)
```

```python
import math
from contextlib import ExitStack

import numpy as np

import concourse.bass as bass
from concourse import mybir

F32 = mybir.dt.float32
F32R = mybir.dt.float32r
I32 = mybir.dt.int32
U32 = mybir.dt.uint32
ALU = mybir.AluOpType
ACT = mybir.ActivationFunctionType
AX = mybir.AxisListType.X

P = 128
D = 1024
T = 256
DEPTH = 2
TT = T // P
KB = D // P
ALPHA = (2 * DEPTH) ** 0.25
H_A, DH_A, D_CQ, ROT_A = 8, 128, 256, 32
H_IDX, D_IDX, ROT_IDX = 8, 64, 16
TOPK = 64
THETA = 500000.0
N_R = 64
LORA_W, LORA_A, LORA_V, LORA_G = 64, 64, 32, 128
GN_EPS, LN_EPS, RMS_EPS = 64e-5, 1e-5, 1e-6
D_FF = ((8 * D // 3 + 127) // 128) * 128
FB = D_FF // P
N_ATT = D_CQ + 2 * DH_A + D_IDX + H_IDX
N_GATE = 2 * D
N_RWKV = 3 * D + LORA_W + LORA_A + LORA_G
N_IN0 = N_ATT + N_GATE + N_RWKV
C_K, C_V, C_IK, C_IW = D_CQ, D_CQ + DH_A, D_CQ + 2 * DH_A, D_CQ + 2 * DH_A + D_IDX
NFR = ROT_A // 2 + ROT_IDX // 2
DECAY = math.exp(-0.5)
CH = 64
NCH = T // CH
GROUPS = 4
GB = KB // GROUPS
NU = GB * NCH
NEG = -1e30
TAKEN = -3e38

RING = 4


GATES_FIRST = 3
GATES_CHUNKS = [1,1,1,2]
CHUNK_GAPS = 8
LEVEL_GAPS = [list(range(4, 12))] + [list(range(8))] * (GROUPS - 2)
GAPS = 14 + CHUNK_GAPS
LOGITS, Y_BACK, BONUS, PROBS, VALUES = 4, 7, 8, 11, 13


def level_before(g, t):
    return -(-(LEVEL_GAPS[g][4 * t + 3] - 3) // 2)


def mid_gaps():
    last = []
    for g in range(GROUPS):
        if g + 1 < GROUPS:
            last += [GAPS * g + n for n in LEVEL_GAPS[g][1::2]]
        last += [GAPS * g + 14 + chunk_gap(g, 2 * i + 1) for i in range(2 * len(chunk_pairs(g)))]
    return last


def chunk_pairs(g):
    start = GATES_FIRST + sum(GATES_CHUNKS[:g])
    v = [("rkv", 3 * (g + 1) + 2)] if g + 1 < GROUPS else []
    return v + [("gate", i) for i in range(start, start + GATES_CHUNKS[g])]


def chunk_gap(g, piece):
    return piece * CHUNK_GAPS // max(4 * len(chunk_pairs(g)), CHUNK_GAPS)


def pairs_done(g, c):
    return [p for i, p in enumerate(chunk_pairs(g)) if chunk_gap(g, 4 * i + 3) // 2 == c]


def gate_slots(pairs):
    return [("gate", 2 * i + b) for i in pairs for b in range(2)]


def stream_order(layer):
    s = [("att", i) for i in range(5)]
    s += [("lora", 0), ("lora", 1)] + ([("vres", 0)] if layer else [])
    s += rkv_slots(0)[:4] + [("iq", 0), ("uq", 0), ("uq", 1)] + rkv_slots(0)[4:]
    s += gate_slots(range(GATES_FIRST))
    for g in range(GROUPS):
        if g + 1 < GROUPS:
            s += rkv_slots(g + 1)
        s += gate_slots([i for kind, i in chunk_pairs(g) if kind == "gate"])
    s += [("oa", i) for i in range(KB)] + [("ob", i) for i in range(KB)] + [("out", i) for i in range(KB)]
    for i in range(FB):
        s += [("up", i), ("up", FB + i)]
    s += [("down", i) for i in range(FB)]
    return s


def rkv_slots(g):
    return [("rkv", 8 * t + GB * g + b) for t in range(3) for b in range(GB)]


SLOTS = [(l, *s) for l in range(DEPTH) for s in stream_order(l)]
SLOT_AT = {s: n for n, s in enumerate(SLOTS)}
SPLIT = ("oa", "ob", "out", "up", "down")
SPLITS = [s for s in SLOTS if s[1] in SPLIT]
SPLIT_AT = {s: m for m, s in enumerate(SPLITS)}
NS = 4
MIDS = [s for s in SLOTS if s[1] == "gate" and s[2] >= 2 * GATES_FIRST or s[1] == "rkv" and s[2] % KB >= GB]
MID_AT = {s: m for m, s in enumerate(MIDS)}
NM = 2
MID_PER_LAYER = len(MIDS) // DEPTH

CPAR = [("b_gate", 16), ("mu", 27), ("w0", 8), ("a0", 8), ("v0", 8), ("k_k", 8), ("k_a", 8), ("r_k", 8),
        ("g_lnx", 8), ("b_lnx", 8), ("g_cq", 2), ("conv_w", 3 * FB), ("conv_b", FB)]
CPAR_AT = {n: sum(w for _, w in CPAR[:i]) for i, (n, _) in enumerate(CPAR)}
NCPAR = sum(w for _, w in CPAR)
DPAR = [("omu", 27), ("hw0", 8), ("ha0", 8), ("hv0", 8), ("hgate", 16), ("hka", 8), ("omhka", 8)]
DPAR_AT = {n: sum(w for _, w in DPAR[:i]) for i, (n, _) in enumerate(DPAR)}
NDPAR = sum(w for _, w in DPAR)
CONST = [("ident", 128), ("stack", 64), ("strict", 64), ("incl", 64), ("hsel", 2), ("bones", 128),
         ("rowsel", 512), ("scan", 512), ("causal", 128), ("freq", NFR)]
CONST_AT = {n: sum(w for _, w in CONST[:i]) for i, (n, _) in enumerate(CONST)}
NCONST = sum(w for _, w in CONST)
LEVELS = 6


class Steps:

    def __init__(self, sem, names):
        self.sem, self.names, self.value, self.next = sem, names, {}, 0
        for r, steps in enumerate(names):
            for name in steps:
                self.value[r, name] = len(self.value) + 1

    def __call__(self, r, name):
        return self.sem, self.value[r, name]

    def inc(self, r, name):
        self.next += 1
        assert self.value[r, name] == self.next, (r, name, self.value[r, name], self.next)
        return self.sem, 1


def trunk(nc, x_in, pos_in, stream, lora_in, cpar_in, rpar_in, const_in, masks_in, out, x_dram, v_dram):
    ctx = ExitStack()
    with ctx:
        def sb(name, shape, dt=F32):
            return ctx.enter_context(nc.sbuf_tensor(name, shape, dt))

        rounded = {}

        def sb_or_parts(name, shape):
            with nc.sbuf_tensor(f"{name}_r", shape, F32R) as t:
                pass
            rounded[name] = t
            return sb(name, shape)

        def sem(name):
            return ctx.enter_context(nc.semaphore(name))

        ps = ctx.enter_context(nc.psum_tensor("ps", [P, 8, 512], F32))

        def bank(n):
            return ps[:, n, :]

        def units(n):
            return ps[:, n:n + 2, :].rearrange("p k (u s) -> p (k u) s", s=P)

        def unit64(n):
            return ps[:, n, :].rearrange("p (u s) -> p u s", s=CH)

        X_BANKS = (0, 1, 6, 7)

        def tok(n):
            return ps[:, n, :].rearrange("p (b t) -> p b t", t=T)

        ring = sb_or_parts("ring", [P, RING, D])
        x_tok = sb_or_parts("x_tok", [P, TT, D])
        xT = sb_or_parts("xT", [P, KB, T])
        gates = sb_or_parts("gates", [P, 2 * KB, T])
        yb = sb_or_parts("yb", [P, KB, T])
        oT = sb_or_parts("oT", [P, H_A, T])
        qT = oT
        mid_hi = [sb(f"mid_hi{i}", [P, D], F32R) for i in range(NM)]
        vf = sb("vf", [P, GB, T])
        lora_w = sb("lora_w", [P, 3, D])
        lora = sb("lora", [P, 3, T])
        cpar = sb("cpar", [P, DEPTH, NCPAR])
        dpar = sb("dpar", [P, NDPAR])
        const = sb("const", [P, NCONST])
        masks = sb("masks", [P, 2, LEVELS, CH], U32)
        half = sb("half", [P, 16])
        p_tok = sb("p_tok", [P, TT, N_ATT])
        kid = sb("kid", [P, TT, 2, D_IDX])
        kirow = sb("kirow", [P, 2 * D_IDX])
        cqT = sb("cqT", [P, 2, T])
        kT = sb("kT", [P, T])
        kiT = sb("kiT", [P, 2, T])
        keep = sb("keep", [P, TT, T])
        small = sb("small", [P, 64])
        scratch = sb("scratch", [P, 1536])
        rel = scratch[:, 0:1024].rearrange("p (a n) -> p a n", a=2)
        qi_tok = rel
        lg = scratch[:, 0:768]
        pT = scratch[:, 768:1536].rearrange("p (a n) -> p a n", a=2)
        sines = sb("sines", [P, 2, TT, NFR])
        ang = sb("ang", [P, 3, TT, NFR])
        pos = sb("pos", [P, TT], I32)
        posf = sb("posf", [P, TT])
        ln = sb("ln", [P, TT, 24])
        rs_ks, vs_dC = sb_or_parts("rs_ks", [P, 2, GB, T]), sb_or_parts("vs_dC", [P, 2, GB, T])
        tha_kkn, X_Y = sb_or_parts("tha_kkn", [P, 2, GB, T]), sb_or_parts("X_Y", [P, 2, NU, CH])
        rs, ks = rs_ks[:, 0, :, :], rs_ks[:, 1, :, :]
        vs_own, dC = vs_dC[:, 0, :, :], vs_dC[:, 1, :, :]
        tha, kkn = tha_kkn[:, 0, :, :], tha_kkn[:, 1, :, :]
        dA, dB, tmp = sb("dA", [P, GB, T]), sb("dB", [P, GB, T]), sb("tmp", [P, GB, T])
        gT = sb("gT", [P, GB, T])
        arc = sb_or_parts("arc", [P, NU, 2, CH])
        qiT = arc[:, :, :, :].rearrange("p (h a) b s -> p h (a b s)", h=4)
        vtmp = scratch[:, 1024:1536]
        a_bd, r_bd = sb_or_parts("a_bd", [P, NU, P]), sb_or_parts("r_bd", [P, NU, P])
        b_bd, k_bd, v_bd = sb_or_parts("b_bd", [P, NU, P]), sb_or_parts("k_bd", [P, NU, P]), sb("v_bd", [P, NU, P])
        W_bd = k_bd
        kt_bd = v_bd
        nT_bd, ak_bd = sb_or_parts("nT_bd", [P, NU, P]), sb_or_parts("ak_bd", [P, NU, P])
        rb_bd, rk_bd = sb_or_parts("rb_bd", [P, NU, P]), sb_or_parts("rk_bd", [P, NU, P])
        bt_bd = sb("bt_bd", [P, NU, P])
        Y_bd, y_bd = sb_or_parts("Y_bd", [P, NU, P]), sb("y_bd", [P, NU, P])
        X_bd = X_Y[:, :, :, :].rearrange("p a b c -> p (a b c)").rearrange("p (u s) -> p u s", s=P)
        sq = sb("sq", [P, NU, CH])
        Vc = sb("Vc", [P, NU, CH])
        Zs, Qs, S = sb("Zs", [P, GB, CH]), sb("Qs", [P, GB, CH]), sb("S", [P, 2, GB, CH])
        Sa = sb("Sa", [P, GB, CH])
        pend = sb("pend", [P, 2, GB, NCH])
        yt = sb("yt", [P, NU, CH])
        bv = sb("bv", [P, GB, T])
        ssm, rn = sb("ssm", [P, 8]), sb("rn", [P, 8])
        rnT = ang[:, :, :, :].rearrange("p a t n -> p (a t n)")[0:8, 0:P]
        g8 = sb("g8", [P, 5, NU])
        q_tok = [gates[:, 4 * j:4 * j + 4, :].rearrange("p (a b) s -> p a (b s)", a=TT) for j in range(2)]
        lnrow = [bt_bd[:, :, :].rearrange("p u s -> p (u s)"), v_bd[:, :, :].rearrange("p u s -> p (u s)")]
        def words(name):
            t = rounded[name]
            if len(t.shape) == 3:
                return t[:, :, :].rearrange("p a b -> p (a b)")
            return t[:, :, :, :].rearrange("p a b c -> p (a b c)")

        def f32(parts):
            return parts.bitcast(F32)

        w_hi = [words(t) for t in ("arc", "tha_kkn", "b_bd", "rb_bd")]
        w_lo = [words(t) for t in ("rs_ks", "X_Y", "vs_dC", "Y_bd")]
        o_hi = [words(t) for t in ("nT_bd", "k_bd")]
        yb_hi = [words(t) for t in ("a_bd", "r_bd")]
        mix_hi = [rounded["gates"][:, KB + i, :] for i in range(KB)]
        mix_lo = [rounded["gates"][:, i, :] for i in range(KB)]
        xT_hi, xT_lo = rounded["xT"], rounded["oT"]
        xr_hi = rounded["x_tok"][:, :, :].rearrange("p a b -> p (a b)")
        xr_lo = rounded["xT"]
        hid_hi = [words(t)[:, T * i:T * i + T] for t in ("a_bd", "r_bd", "k_bd", "nT_bd", "ak_bd", "rk_bd") for i in range(4)]
        hid_lo = ([rounded["gates"][:, i, :] for i in range(2 * KB)] + [rounded["yb"][:, i, :] for i in range(KB)])

        def block_of(t, i):
            return t[i // 4][:, T * (i % 4):T * (i % 4) + T]

        def blocks(t, i, n):
            return t[:, i:i + n, :].rearrange("p a b -> p (a b)")

        YB_RUNS = [[(0, 4), (4, 2)], [(6, 2)]]

        def yb_hi_run(i, n):
            return yb_hi[i // 4][:, T * (i % 4):T * (i % 4 + n)]

        conv = [dA, dB]

        def flat(t):
            return t[:, :, :].rearrange("p a b -> p (a b)")

        def by_unit(t):
            return t.rearrange("p b (c s) -> p (b c) s", s=CH)

        C = {n: const[:, CONST_AT[n]:CONST_AT[n] + w] for n, w in CONST}
        ident, stack = C["ident"], C["stack"]

        def cp(layer, name, i=0, n=1):
            a = CPAR_AT[name] + i
            return cpar[:, layer, a:a + n]

        def dp(name, i=0, n=1):
            a = DPAR_AT[name] + i
            return dpar[:, a:a + n]

        def q64(h):
            return slice(64 * h, 64 * h + 64)

        R = DEPTH * GROUPS
        L2 = range(DEPTH)
        lv = range(1, LEVELS)

        landed = [sem(f"slot{i}_landed") for i in range(RING)]
        slot_used = sem("slot_used")
        x_in_sbuf = sem("x_in_sbuf")
        inputs_in = sem("inputs_in")
        lora_landed = sem("lora_landed")
        rows_landed = sem("rows_landed")
        stored = sem("stored")
        x_saved = sem("x_saved")
        x_back = sem("x_back")
        v_saved = sem("v_saved")
        v_back = sem("v_back")
        zeroed = sem("zeroed")
        tables_dve = sem("tables_dve")
        kid_half = sem("kid_half")
        tables = sem("tables")

        def used(l, kind, i):
            return slot_used, SLOT_AT[l, kind, i] + 1

        def pair_slots(n):
            kind, i = n
            return {"lora": [("lora", 0), ("lora", 1)], "vres": [("vres", 0)],
                    "rkv": [("rkv", 8 * (i % 3) + GB * (i // 3) + b) for b in range(GB)],
                    "gate": [("gate", 2 * i), ("gate", 2 * i + 1)],
                    "oa": [("oa", 2 * i), ("oa", 2 * i + 1)], "ob": [("ob", 2 * i), ("ob", 2 * i + 1)],
                    "up": [("up", i), ("up", FB + i)]}[kind]

        pairs = []
        for l in L2:
            seen = []
            for s in stream_order(l):
                kind, i = s
                n = {"lora": ("lora", 0), "vres": ("vres", 0), "rkv": ("rkv", i % 8 // 2 * 3 + i // 8),
                     "gate": ("gate", i // 2), "oa": ("oa", i // 2), "ob": ("ob", i // 2),
                     "up": ("up", i % FB)}.get(kind)
                if n and n not in seen:
                    seen.append(n)
            pairs += [(l, n) for n in seen]
        pair_at = {n: d for d, n in enumerate(pairs)}

        def pair_done(l, n):
            return used(l, *pair_slots(n)[-1])

        shifted = ("lora", "vres", "rkv")
        act_dense = Steps(sem("act_dense"), [sum([[n] if n[0] in shifted + ("gate",) else
                                                  [n, (n, "tanh"), (n, "hi")] if n[0] == "up" else []
                                                  for k, n in pairs if k == l], []) for l in L2])
        dve_dense = Steps(sem("dve_dense"), [sum([[n] if n[0] in shifted + ("oa", "ob") else
                                                  [(n, "conv1"), (n, "conv"), (n, "silu"), (n, "whole"), n] if n[0] == "up" else []
                                                  for k, n in pairs if k == l], []) for l in L2])

        def pair_free(l, n):
            return act_dense(l, n) if n[0] == "gate" else dve_dense(l, (n, "whole") if n[0] == "up" else n)

        def by_layer(name, steps):
            return Steps(sem(name), [steps] * DEPTH)

        def by_round(name, steps):
            return Steps(sem(name), [steps] * R)

        per_layer = len(SPLITS) // DEPTH
        act_split = by_layer("act_split", list(range(per_layer)))
        dve_split = by_layer("dve_split", list(range(per_layer)))
        parts = ["o0", "o1", "yb0", "yb1"] + [f"mix{i}" for i in range(4)]
        act_parts = by_layer("act_parts", ["xr"] + parts)
        dve_parts = by_layer("dve_parts", ["xr"] + parts + [f"x{i}" for i in range(4)])
        act_mid = by_layer("act_mid", list(range(MID_PER_LAYER)))
        dve_mid = by_layer("dve_mid", list(range(MID_PER_LAYER)))
        mid_last = mid_gaps()

        def mids_by(gap):
            return sum(n <= gap for n in mid_last) + NM

        pe_x = by_layer("pe_x", [f"T{i}" for i in range(4)] + [f"A{k}" for k in range(3)]
                        + [f"U{i}" for i in range(4)] + [f"B{k}" for k in range(3)])
        act_x = by_layer("act_x", [f"T{i}" for i in range(4)] + ["Aax"] + [f"U{i}" for i in range(4)] + ["Bax"])
        dve_par = by_layer("dve_par", ["dpar", "lsig"])
        dve_x = by_layer("dve_x", [f"mix{i}" for i in range(4)]
                         + sum([sum([[f"{w}add{k}", f"{w}st{k}"] for k in range(4)], []) + [f"{w}mv", f"{w}c0", f"{w}c1", f"{w}n0", f"{w}n1"]
                                for w in "AB"], []))
        act_lora = by_layer("act_lora", ["tanh"])
        pool_x = by_layer("pool_x", ["Aeps", "A", "Beps", "B"])
        pe_att = by_layer("pe_att", ["cqT", "kT", "qiT", "qT"] + [f"s{i}" for i in range(6)]
                          + sum([[f"lg{g}", f"pT{g}", f"o{g}"] for g in range(GROUPS)], []))
        act_att = by_layer("act_att", ["p", "ssq", "cqT", "kT", "qi", "q0", "q1", "qiT", "qT"]
                           + [f"s{i}" for i in range(6)]
                           + sum([[f"e{g}", f"pT{g}", f"o{g}"] for g in range(GROUPS)], []))
        rope = lambda w: [f"{w}a", f"{w}"]
        dve_att = by_layer("dve_att", ["wi", "kst", "kmv"] + rope("rk") + ["cq", "kic", "ki"] + rope("rki") + rope("rqi")
                           + rope("rq0") + rope("rq1")
                           + [f"s{t}{h}" for t in range(TT) for h in range(H_IDX)]
                           + sum([[f"causal{t}"] + sum([[f"max{t}{i}", f"rep{t}{i}"] for i in range(8)], [])
                                  + [f"sel{t}", f"selb{t}", f"keep{t}"] for t in range(TT)], [])
                           + sum([[f"lg{g}", f"mx{g}", f"rc{g}", f"pn{g}"] for g in range(GROUPS)], []))
        pool_att = by_layer("pool_att", ["eps", "rs"])

        pe_prep = Steps(sem("pe_prep"), [["zw", "za"] + (["zv"] if r >= GROUPS else []) + ["ss", "rnT", "rnx"]
                                         for r in range(R)])
        act_prep = Steps(sem("act_prep"), [["kk2", "thw", "tha", "P", "Pp", "iP", "kt"]
                                           + (["thv"] if r >= GROUPS else []) for r in range(R)])
        dve_prep = Steps(sem("dve_prep"), [["s", "cum", "cp", "pend", "ss", "rnT"]
                                           + (["v1", "v2", "v"] if r >= GROUPS else [])
                                           + ["kkn", "k2", "kb", "arc", "bneg", "kp", "rkk"] for r in range(R)])
        pool_prep = by_round("pool_prep", ["rn"])
        pe_wkv = by_round("pe_wkv", ["gramB", "gramK", "V", "nX", "tokB", "tokK"]
                          + sum([[f"W{l}0", f"W{l}1"] + sum([([f"XW{l}{k}"] if l < LEVELS - 1 else []) + [f"WtY{l}{k}"]
                                                     for k in range(2)], []) for l in lv], [])
                          + sum([[f"Z{c}", f"Q{c}"] + ([f"S{c}"] if c < NCH - 1 else []) + [f"y{c}"]
                                 for c in range(NCH)], []))
        pe_bonus = by_round("pe_bonus", ["bonus", "zg"])
        act_g = by_round("act_g", ["g"])
        dve_bv = by_round("dve_bv", ["bv"])
        pe_yT = by_round("pe_yT", ["yT"])
        act_wkv = by_round("act_wkv", ["vbd", "resetY", "resetX", "Vc", "tokB", "tokK"] + [f"W{l}{k}" for l in lv for k in range(2)]
                           + sum([[f"Z{c}", f"Q{c}"] for c in range(NCH)], []))
        act_y = by_round("act_y", ["y", "sq", "yn"])
        dve_wkv = by_round("dve_wkv", ["nT", "Arb", "Y0", "Aak", "Ark", "X00", "X01"]
                           + sum([([f"X{l}{k}"] if l < LEVELS - 1 else []) + [f"Y{l}{k}"] for l in lv for k in range(2)], [])
                           + sum([[f"S{c}a"] * (c > 0) + [f"S{c}"] for c in range(NCH - 1)], []))
        dve_y = by_round("dve_y", ["m", "m2", "yc", "v8", "yr", "yb1", "yb"])
        pool_bd = by_round("pool_bd", ["abd0", "abd1", "rbd0", "rbd"])
        pool_y = by_round("pool_y", ["eps", "rstd"])

        block = ctx.enter_context(nc.Block())

        @block.sync
        def _(sp):
            sp.dma_start(x_tok[:, 0, :], x_in[0:P]).then_inc(x_in_sbuf, 16)
            sp.dma_start(ident, const_in[:, 0:P]).then_inc(x_in_sbuf, 16)
            sp.dma_start(x_tok[:, 1, :], x_in[P:T]).then_inc(x_in_sbuf, 16)
            for n in range(RING):
                sp.dma_start(ring[:, n, :], stream[n]).then_inc(landed[n], 16)
            sp.dma_start(const[:, P:NCONST], const_in[:, P:NCONST]).then_inc(inputs_in, 16)
            sp.dma_start(pos[:, :], pos_in).then_inc(inputs_in, 16)
            sp.dma_start(flat(cpar), cpar_in).then_inc(inputs_in, 16)
            sp.dma_start(masks[:, :, :, :].rearrange("p a l c -> p (a l c)"), masks_in).then_inc(inputs_in, 16)
            def refill(n, k, wait, value):
                sp.wait_ge(wait, value)
                src = stream[n] if isinstance(n, int) else stream[bass.ds(n, 1)].rearrange("a p d -> p (a d)")
                sp.dma_start(ring[:, k, :], src).then_inc(landed[k], 16)

            def save_x():
                sp.wait_ge(*dve_x(0, "Bn1"))
                sp.dma_start(x_dram.rearrange("(a p) d -> p a d", p=P), x_tok[:, :, :]).then_inc(x_saved, 16)

            def load_x(l):
                sp.wait_ge(*used(l, "gate", 2 * KB - 1))
                if l:
                    sp.wait_ge(x_saved, 16)
                sp.dma_start(x_tok[:, :, :], (x_dram if l else x_in).rearrange("(a p) d -> p a d", p=P)
                             ).then_inc(x_back, 16)

            between = {SLOT_AT[l, "gate", 2 * KB - 1] + RING: (lambda l=l: load_x(l)) for l in L2}
            between[SLOT_AT[1, "att", 0] + RING] = save_x
            n = RING
            while n < len(SLOTS):
                if n in between:
                    between[n]()
                split = SLOTS[n - RING] in SPLIT_AT
                end = n + 1
                while end < len(SLOTS) and (SLOTS[end - RING] in SPLIT_AT) == split and end not in between:
                    end += 1
                wait = dve_split.sem if split else slot_used
                less = n - SPLIT_AT[SLOTS[n - RING]] - 1 if split else RING - 1
                first, last = -(-n // RING), end // RING
                for m in range(n, min(first * RING, end)):
                    refill(m, m % RING, wait, m - less)
                if last > first:
                    with sp.Fori(first, last) as i:
                        for k in range(RING):
                            refill(i * RING + k, k, wait, i * RING + (k - less))
                for m in range(max(n, last * RING) if last >= first else end, end):
                    refill(m, m % RING, wait, m - less)
                n = end
            sp.wait_ge(*dve_x(DEPTH - 1, "Bn1"))
            sp.dma_start(out.rearrange("(a p) d -> p a d", p=P), x_tok[:, :, :]).then_inc(stored, 16)
            sp.wait_ge(stored, 16)

        @block.gpsimd
        def _(pool):
            def zero_bd(l):
                again = [a_bd, r_bd, b_bd, k_bd, v_bd, nT_bd, ak_bd, y_bd]
                if l:
                    pool.wait_ge(*dve_x(l - 1, "Bn1"))
                    again = [a_bd, r_bd, b_bd, k_bd, v_bd, nT_bd, ak_bd, rb_bd, rk_bd]
                else:
                    pool.memset(kiT[:, :, :], 0.0)
                    again += [rb_bd, rk_bd]
                for t in again:
                    last = pool.memset(t[:, :, :], 0.0)
                last.then_inc(zeroed, 1)

            def small_rows(l):
                if l:
                    pool.wait_ge(*pe_bonus(GROUPS * l - 1, "zg"))
                    pool.wait_ge(*pe_prep(GROUPS * l - 1, "za"))
                    pool.wait_ge(*dve_att(l - 1, "ki"))
                pool.dma_start(flat(lora_w), lora_in[l]).then_inc(lora_landed, 16)
                pool.dma_start(kirow[:, :], rpar_in[l:l + 1, 4 * D:4 * D + 2 * D_IDX].broadcast_to([P, 2 * D_IDX])
                               ).then_inc(lora_landed, 16)

            def norm_rows(l, w):
                i = "AB".index(w)
                if i == 0:
                    pool.wait_ge(*pe_wkv(GROUPS * (l + 1) - 1, f"y{NCH - 1}"))
                else:
                    pool.wait_ge(*dve_x(l, "An1"))
                for j in range(2):
                    a = (2 * i + j) * D
                    pool.dma_start(lnrow[j], rpar_in[l:l + 1, a:a + D].broadcast_to([P, D])
                                   ).then_inc(rows_landed, 16)

            def norm_rsqrt(l, w):
                pool.wait_ge(*dve_x(l, f"{w}mv"))
                pool.tensor_scalar(ln[:, :, 20], ln[:, :, 13], 1.0, LN_EPS, ALU.mult, ALU.add
                                   ).then_inc(*pool_x.inc(l, f"{w}eps"))
                pool.wait_ge(*pool_x(l, f"{w}eps"))
                pool.tensor_tensor(ln[:, :, 21], ln[:, :, 20], half[:, 0:TT], ALU.pow
                                   ).then_inc(*pool_x.inc(l, w))

            def head_norm(r):
                pool.wait_ge(*dve_prep(r, "ss"))
                pool.tensor_tensor(rn[:, :], ssm[:, :], half[:, 0:8], ALU.pow).then_inc(*pool_prep.inc(r, "rn"))

            pool.memset(half[:, :], -0.5).then_inc(zeroed, 1)
            zero_bd(0)
            pool.wait_ge(landed[RING - 1], 16)
            small_rows(0)
            pool.wait_ge(zeroed, 2)
            for l in L2:
                if l:
                    zero_bd(l)
                    small_rows(l)
                pool.wait_ge(*act_att(l, "ssq"))
                pool.wait_ge(*dve_att(l, "kmv"))
                pool.tensor_scalar(small[:, 4:6], small[:, 0:2], 1.0 / D_CQ, RMS_EPS, ALU.mult, ALU.add)
                pool.tensor_scalar(small[:, 6:8], ln[:, :, 13], 1.0, LN_EPS, ALU.mult, ALU.add
                                   ).then_inc(*pool_att.inc(l, "eps"))
                pool.wait_ge(*pool_att(l, "eps"))
                pool.tensor_tensor(small[:, 8:12], small[:, 4:8], half[:, 0:4], ALU.pow
                                   ).then_inc(*pool_att.inc(l, "rs"))
                head_norm(GROUPS * l)
                for g in range(GROUPS):
                    r = GROUPS * l + g
                    pool.wait_ge(*dve_prep(r, "arc"))
                    if r:
                        pool.wait_ge(*pe_wkv(r - 1, f"y{NCH - 1}"))
                    pool.wait_ge(*(pool_y(r - 1, "rstd") if g else pool_prep(r, "rn")))
                    steps = [("abd0", a_bd, 0, 0), ("abd1", a_bd, 0, 1), ("rbd0", r_bd, 1, 0), ("rbd", r_bd, 1, 1)]
                    for name, dst, j, h in steps:
                        pool.tensor_copy(dst[q64(h), :, q64(h)], arc[q64(h), :, j, :]).then_inc(*pool_bd.inc(r, name))
                        pool.wait_ge(*pool_bd(r, name))
                    if g + 1 < GROUPS:
                        head_norm(r + 1)
                    pool.wait_ge(*dve_y(r, "v8"))
                    pool.tensor_scalar(g8[:, 3, :], g8[:, 2, :], 1.0 / N_R, GN_EPS, ALU.mult, ALU.add
                                       ).then_inc(*pool_y.inc(r, "eps"))
                    pool.wait_ge(*pool_y(r, "eps"))
                    pool.tensor_tensor(g8[:, 4, :], g8[:, 3, :], half[:, 0:NU], ALU.pow
                                       ).then_inc(*pool_y.inc(r, "rstd"))
                norm_rows(l, "A")
                norm_rsqrt(l, "A")
                norm_rows(l, "B")
                norm_rsqrt(l, "B")

        @block.tensor
        def _(pe):
            def slot(l, kind, i):
                n = SLOT_AT[l, kind, i]
                pe.wait_ge(landed[n % RING], 16 * (n // RING + 1))
                return ring[:, n % RING, :]

            def pair_pieces(l, n, rhs):
                d = pair_at[l, n]
                dst = tok(d % 2)

                def piece(b, name, k0):
                    if b == 0 and k0 == 0 and d >= 2:
                        pe.wait_ge(*pair_free(*pairs[d - 2]))
                    if (l, *name) in MID_AT:
                        m = MID_AT[l, *name] % MID_PER_LAYER
                        pe.wait_ge(*dve_mid(l, m))
                        hi, lo = mid_hi[m % NM], rounded["ring"][:, SLOT_AT[l, *name] % RING, :]
                        for kb in range(k0, k0 + 4):
                            c = slice(kb * P, kb * P + P)
                            mm = product(dst[:, b, :], (hi[:, c], lo[:, c]), (xr_hi[:, kb * T:kb * T + T], xr_lo[:, kb, :]),
                                         kb == 0, kb == KB - 1)
                    else:
                        w = slot(l, *name)
                        for kb in range(k0, k0 + 4):
                            mm = pe.matmul(dst[:, b, :], w[:, kb * P:kb * P + P], rhs[:, kb, :],
                                           start=(kb == 0), stop=(kb == KB - 1))
                    if k0:
                        mm.then_inc(slot_used, 1)

                return [lambda b=b, name=name, k0=k0: piece(b, name, k0)
                        for b, name in enumerate(pair_slots(n)) for k0 in (0, 4)]

            def pair(l, n, rhs):
                for p in pair_pieces(l, n, rhs):
                    p()

            def slot_parts(l, kind, i):
                m = SPLIT_AT[l, kind, i] % per_layer
                pe.wait_ge(*dve_split(l, m))
                return w_hi[m % NS], w_lo[m % NS]

            def product(dst, left, right, start, stop):
                (lh, ll), (rh, rl) = left, right
                pe.matmul(dst, lh, rh, start=start, stop=False)
                pe.matmul(dst, lh, rl, start=False, stop=False)
                return pe.matmul(dst, ll, rh, start=False, stop=stop)

            def split_pair(l, n, rhs):
                d = pair_at[l, n]
                pe.wait_ge(*pair_free(*pairs[d - 2]))
                for b, name in enumerate(pair_slots(n)):
                    w = slot_parts(l, *name)
                    for kb in range(KB):
                        mm = product(tok(d % 2)[:, b, :], [x[:, kb * P:kb * P + P] for x in w], rhs(kb),
                                     kb == 0, kb == KB - 1)
                    mm.then_inc(slot_used, 1)

            def transposed_x(l, w):
                for t in range(TT):
                    if w == "U":
                        pe.wait_ge(*dve_x(l, f"An{t}"))
                    elif l:
                        pe.wait_ge(*dve_x(l - 1, f"Bn{t}"))
                    for i in range(4):
                        for b in range(2):
                            mm = pe.transpose(tok(X_BANKS[i])[:, b, t * P:t * P + P],
                                              x_tok[:, t, (2 * i + b) * P:(2 * i + b + 1) * P], ident)
                        if t:
                            mm.then_inc(*pe_x.inc(l, f"{w}{i}"))

            def prep_1(r):
                l, g = divmod(r, GROUPS)
                if g == 0:
                    pe.wait_ge(*act_lora(l, "tanh"))
                    pe.wait_ge(lora_landed, 32 * (l + 1))
                    pe.wait_ge(*act_att(l, "qT"))
                else:
                    pe.wait_ge(*act_att(l, f"o{g - 1}"))
                for b in range(GB):
                    c = (GB * g + b) * P
                    mm = pe.matmul(tok(6)[:, b, :], lora_w[0:64, 0, c:c + P], lora[0:64, 0, :], start=True, stop=True)
                mm.then_inc(*pe_prep.inc(r, "zw"))
                for b in range(GB):
                    c = (GB * g + b) * P
                    mm = pe.matmul(tok(7)[:, b, :], lora_w[64:128, 0, c:c + P], lora[64:128, 0, :], start=True, stop=True)
                mm.then_inc(*pe_prep.inc(r, "za"))

            def prep_2(r):
                l, g = divmod(r, GROUPS)
                if l:
                    pe.wait_ge(*dve_par(l, "lsig"))
                    pe.wait_ge(*act_prep(r, "thw"))
                    for b in range(GB):
                        c = (GB * g + b) * P
                        mm = pe.matmul(tok(6)[:, b, :], lora_w[:, 2, c:c + P], lora[:, 2, :], start=True, stop=True)
                    mm.then_inc(*pe_prep.inc(r, "zv"))
                pe.wait_ge(*act_prep(r, "tha"))
                pe.wait_ge(*act_prep(r, "kk2"))
                for b in range(GB):
                    for t in range(TT):
                        j = 2 * (TT * b + t)
                        mm = pe.matmul(bank(7)[:, j:j + 2], tmp[:, b, t * P:t * P + P], C["hsel"], start=True, stop=True)
                mm.then_inc(*pe_prep.inc(r, "ss"))

            def prep_3(r):
                pe.wait_ge(*pool_prep(r, "rn"))
                pe.transpose(bank(7)[0:8, 128:256], rn[:, :], ident).then_inc(*pe_prep.inc(r, "rnT"))

            def prep_4(r):
                pe.wait_ge(*dve_prep(r, "rnT"))
                pe.wait_ge(*act_prep(r, "thv" if r >= GROUPS else "thw"))
                for b in range(GB):
                    for t in range(TT):
                        j = TT * b + t
                        mm = pe.matmul(tok(6)[:, b, t * P:t * P + P], C["rowsel"][0:8, j * P:j * P + P], rnT[:, :],
                                       start=True, stop=True)
                mm.then_inc(*pe_prep.inc(r, "rnx"))

            def y_back(r):
                pe.wait_ge(*dve_y(r, "yr"))
                if (r + 1) % GROUPS:
                    pe.wait_ge(*dve_att(r // GROUPS, f"lg{(r + 1) % GROUPS}"))
                else:
                    pe.wait_ge(*act_att(r // GROUPS, f"o{GROUPS - 1}"))
                for u in range(NU):
                    mm = pe.transpose(units(6)[:, u, :], y_bd[:, u, :], ident)
                mm.then_inc(*pe_yT.inc(r, "yT"))

            def bonus(r):
                l, g = divmod(r, GROUPS)
                pe.wait_ge(*dve_prep(r, "rkk"))
                pe.wait_ge(*(act_y(r - 1, "yn") if g else dve_att(l, f"lg{g}")))
                pe.matmul(bank(6), C["bones"], flat(tmp), start=True, stop=True).then_inc(*pe_bonus.inc(r, "bonus"))
                for b in range(GB):
                    c = (GB * g + b) * P
                    mm = pe.matmul(tok(7)[:, b, :], lora_w[:, 1, c:c + P], lora[:, 1, :], start=True, stop=True)
                mm.then_inc(*pe_bonus.inc(r, "zg"))

            def att_logits(l, g):
                r = GROUPS * l + g
                pe.wait_ge(*act_wkv(r, "Vc"))
                for h in range(2):
                    pe.matmul(bank(6)[:, h * T:h * T + T], qT[:, 2 * g + h, P:T], kT[:, :], start=True, stop=True)
                for h in range(2):
                    mm = pe.matmul(bank(7)[:, h * P:h * P + P], qT[:, 2 * g + h, 0:P], kT[:, 0:P], start=True, stop=True)
                mm.then_inc(*pe_att.inc(l, f"lg{g}"))

            def att_probs(l, g):
                pe.wait_ge(*dve_att(l, f"pn{g}"))
                pe.wait_ge(*dve_bv(GROUPS * l + g, "bv"))
                pe.wait_ge(*act_g(GROUPS * l + g, "g"))
                for h in range(2):
                    b = bank(6 + h)
                    pe.transpose(b[:, 0:P], lg[:, 512 + h * P:512 + h * P + P], ident)
                    for s in range(2):
                        mm = pe.transpose(b[:, P + s * P:2 * P + s * P], lg[:, h * T + s * P:h * T + s * P + P], ident)
                mm.then_inc(*pe_att.inc(l, f"pT{g}"))

            def att_values(l, g):
                pe.wait_ge(*act_att(l, f"pT{g}"))
                v0, v1 = p_tok[:, 0, C_V:C_V + DH_A], p_tok[:, 1, C_V:C_V + DH_A]
                for h in range(2):
                    o = tok(6)[:, h, :]
                    pe.matmul(o[:, 0:P], v0, pT[:, h, 0:P], start=True, stop=True)
                    pe.matmul(o[:, P:T], v0, pT[:, h, P:2 * P], start=True, stop=False)
                    mm = pe.matmul(o[:, P:T], v1, pT[:, h, 2 * P:3 * P], start=False, stop=True)
                mm.then_inc(*pe_att.inc(l, f"o{g}"))

            def wkv(r, fill):
                l, g = divmod(r, GROUPS)
                bc = lambda c: [NCH * b + c for b in range(GB)]
                pe.wait_ge(*dve_prep(r, "bneg"))
                if g == 0:
                    pe.wait_ge(zeroed, l + 2)
                    pe.wait_ge(*act_att(l, "s5"))
                else:
                    pe.wait_ge(*act_wkv(r - 1, f"Q{NCH - 1}"))
                rhs = arc[:, :, :, :].rearrange("p u a s -> p u (a s)")
                for u in range(NU):
                    mm = pe.matmul(units(2)[:, u, :], b_bd[:, u, :], rhs[:, u, :], start=True, stop=True)
                mm.then_inc(*pe_wkv.inc(r, "gramB"))
                pe.wait_ge(*dve_prep(r, "kp"))
                if g:
                    pe.wait_ge(*act_y(r - 1, "y"))
                for u in range(NU):
                    mm = pe.matmul(units(4)[:, u, :], k_bd[:, u, :], rhs[:, u, :], start=True, stop=True)
                mm.then_inc(*pe_wkv.inc(r, "gramK"))
                pe.wait_ge(*act_wkv(r, "vbd"))
                pe.wait_ge(*dve_prep(r, "rnT"))
                for u in range(NU):
                    mm = pe.transpose(units(6)[:, u, :], v_bd[:, u, :], ident)
                mm.then_inc(*pe_wkv.inc(r, "V"))
                fill(0)
                pe.wait_ge(*dve_wkv(r, "Y0"))
                for u in range(NU):
                    mm = pe.transpose(units(2)[:, u, :], nT_bd[:, u, :], ident)
                mm.then_inc(*pe_wkv.inc(r, "nX"))
                fill(1)
                pe.wait_ge(*dve_wkv(r, "Ark"))
                for u in range(NU):
                    mm = pe.transpose(units(4)[:, u, :], b_bd[:, u, :], ident)
                mm.then_inc(*pe_wkv.inc(r, "tokB"))
                fill(2)
                pe.wait_ge(*act_wkv(r, "tokB"))
                for u in range(NU):
                    mm = pe.transpose(units(4)[:, u, :], k_bd[:, u, :], ident)
                mm.then_inc(*pe_wkv.inc(r, "tokK"))
                fill(3)
                for lev in lv:
                    for k in range(2):
                        if lev == 1:
                            pe.wait_ge(*dve_wkv(r, f"X0{k}"))
                        else:
                            pe.wait_ge(*dve_wkv(r, f"Y{lev - 1}{k}"))
                        for u in range(4 * k, 4 * k + 4):
                            mm = pe.matmul(units(2)[:, u, :], nT_bd[:, u, :], X_bd[:, u, :], start=True, stop=True)
                        mm.then_inc(*pe_wkv.inc(r, f"W{lev}{k}"))
                        if k == 0:
                            fill(2 + 2 * lev)
                            if lev == 1:
                                pe.wait_ge(*act_wkv(r, "tokK"))
                    for k in range(2):
                        pe.wait_ge(*act_wkv(r, f"W{lev}{k}"))
                        if lev < LEVELS - 1:
                            for u in range(4 * k, 4 * k + 4):
                                mm = pe.matmul(units(4)[:, u, :], Y_bd[:, u, :], W_bd[:, u, :], start=True, stop=True)
                            mm.then_inc(*pe_wkv.inc(r, f"XW{lev}{k}"))
                        for u in range(4 * k, 4 * k + 4):
                            mm = pe.matmul(units(2)[:, u, :], W_bd[:, u, :], Y_bd[:, u, :], start=True, stop=True)
                        mm.then_inc(*pe_wkv.inc(r, f"WtY{lev}{k}"))
                        if k == 0:
                            fill(3 + 2 * lev)
                if g + 1 < GROUPS:
                    prep_1(r + 1)
                for c in range(NCH):
                    if c == 0:
                        pe.wait_ge(*pool_bd(r, "rbd"))
                        pe.wait_ge(*dve_wkv(r, f"Y{LEVELS - 1}1"))
                    else:
                        pe.wait_ge(*dve_wkv(r, f"S{c - 1}"))
                    s_old = S[:, (c + 1) % 2, :, :]
                    for b, u in enumerate(bc(c)):
                        z = bank(2)[:, b * CH:b * CH + CH]
                        if c:
                            pe.matmul(z, a_bd[:, u, :], s_old[:, b, :], start=True, stop=False)
                        mm = pe.matmul(z, ak_bd[:, u, :], Vc[:, u, :], start=(c == 0), stop=True)
                    mm.then_inc(*pe_wkv.inc(r, f"Z{c}"))
                    fill(14 + 2 * c)
                    pe.wait_ge(*act_wkv(r, f"Z{c}"))
                    for b, u in enumerate(bc(c)):
                        mm = pe.matmul(bank(3)[:, b * CH:b * CH + CH], Y_bd[:, u, :], Zs[:, b, :], start=True, stop=True)
                    mm.then_inc(*pe_wkv.inc(r, f"Q{c}"))
                    fill(15 + 2 * c)
                    pe.wait_ge(*act_wkv(r, f"Q{c}"))
                    if c < NCH - 1:
                        for b, u in enumerate(bc(c)):
                            s_new = bank(4)[:, b * CH:b * CH + CH]
                            pe.matmul(s_new, bt_bd[:, u, :], Qs[:, b, :], start=True, stop=False)
                            mm = pe.matmul(s_new, kt_bd[:, u, :], Vc[:, u, :], start=False, stop=True)
                        mm.then_inc(*pe_wkv.inc(r, f"S{c}"))
                    for b, u in enumerate(bc(c)):
                        y = unit64(5)[:, u, :]
                        pe.matmul(y, rb_bd[:, u, :], Qs[:, b, :], start=True, stop=False)
                        mm = pe.matmul(y, rk_bd[:, u, :], Vc[:, u, :], start=False, stop=(c == 0))
                        if c:
                            mm = pe.matmul(y, r_bd[:, u, :], s_old[:, b, :], start=False, stop=True)
                    mm.then_inc(*pe_wkv.inc(r, f"y{c}"))
                    if g + 1 < GROUPS and c < 3:
                        [prep_2, prep_3, prep_4][c](r + 1)

            pe.wait_ge(x_in_sbuf, 16 * 3)
            for l in L2:
                transposed_x(l, "T")
                pe.wait_ge(*act_x(l, "T3"))
                for c in range(5):
                    w = slot(l, "att", c)
                    n = min(P, N_ATT - c * P)
                    for t in range(TT):
                        dst = bank(2 + t)[:, c * P:c * P + n] if c < 4 else bank(4)[:, t * P:t * P + n]
                        for kb in range(KB):
                            mm = pe.matmul(dst, xT[:, kb, t * P:t * P + P], w[:, kb * P:kb * P + n],
                                           start=(kb == 0), stop=(kb == KB - 1))
                    mm.then_inc(slot_used, 1)
                if l == 0:
                    pe.wait_ge(inputs_in, 16 * 4)
                pair(l, ("lora", 0), xT)
                if l:
                    w = slot(l, "vres", 0)
                    d = pair_at[l, ("vres", 0)]
                    pe.wait_ge(*pair_free(*pairs[d - 2]))
                    for kb in range(KB):
                        mm = pe.matmul(tok(d % 2)[:, 0, :], w[:, kb * P:kb * P + P], xT[:, kb, :],
                                       start=(kb == 0), stop=(kb == KB - 1))
                    mm.then_inc(slot_used, 1)
                pair(l, ("rkv", 0), xT)
                pe.wait_ge(*dve_att(l, "cq"))
                for kb in range(2):
                    for t in range(TT):
                        mm = pe.transpose(tok(6)[:, kb, t * P:t * P + P], p_tok[:, t, kb * P:kb * P + P], ident)
                mm.then_inc(*pe_att.inc(l, "cqT"))
                pe.wait_ge(*dve_att(l, "rki"))
                for t in range(TT):
                    pe.transpose(bank(7)[:, t * P:t * P + P], p_tok[:, t, C_K:C_K + DH_A], ident)
                for t in range(TT):
                    mm = pe.transpose(bank(7)[:, T + t * P:T + t * P + P],
                                      kid[:, t, :, :].rearrange("p a b -> p (a b)"), ident)
                mm.then_inc(*pe_att.inc(l, "kT"))
                pair(l, ("rkv", 1), xT)
                pe.wait_ge(*act_att(l, "cqT"))
                w = slot(l, "iq", 0)
                for t in range(TT):
                    for kb in range(2):
                        mm = pe.matmul(bank(2 + t), cqT[:, kb, t * P:t * P + P], w[:, kb * 512:kb * 512 + 512],
                                       start=(kb == 0), stop=(kb == 1))
                mm.then_inc(slot_used, 1)
                for j in range(2):
                    w = slot(l, "uq", j)
                    if j:
                        pe.wait_ge(*act_att(l, "kT"))
                    for t in range(TT):
                        for kb in range(2):
                            mm = pe.matmul(bank(4 + 2 * j + t), cqT[:, kb, t * P:t * P + P], w[:, kb * 512:kb * 512 + 512],
                                           start=(kb == 0), stop=(kb == 1))
                    mm.then_inc(slot_used, 1)
                pair(l, ("rkv", 2), xT)
                pe.wait_ge(*dve_att(l, "rqi"))
                for i in range(4):
                    for t in range(TT):
                        mm = pe.transpose(tok(2 + i // 2)[:, i % 2, t * P:t * P + P], qi_tok[:, t, i * P:i * P + P], ident)
                mm.then_inc(*pe_att.inc(l, "qiT"))
                pe.wait_ge(*dve_att(l, "rq1"))
                for h in range(H_A):
                    for t in range(TT):
                        mm = pe.transpose(tok(4 + h // 2)[:, h % 2, t * P:t * P + P],
                                          q_tok[h // 4][:, t, h % 4 * P:h % 4 * P + P], ident)
                mm.then_inc(*pe_att.inc(l, "qT"))
                for i in range(6):
                    pe.wait_ge(*act_att(l, "qiT" if i < 2 else f"s{i - 2}"))
                    heads, t = (range(4 * i, 4 * i + 4), 0) if i < 2 else (range(2 * (i - 2), 2 * (i - 2) + 2), 1)
                    n = T // 2 * (t + 1)
                    for j, h in enumerate(heads):
                        mm = pe.matmul(bank(2 + i % 2)[:, j * n:j * n + n], qiT[:, h // 2, t * P:t * P + P],
                                       kiT[:, h % 2, 0:n], start=True, stop=True)
                    mm.then_inc(*pe_att.inc(l, f"s{i}"))
                r0 = GROUPS * l
                first = sum([pair_pieces(l, ("gate", i), xT) for i in range(GATES_FIRST)], [])
                for k, p in enumerate((prep_1, prep_2, prep_3, prep_4)):
                    p(r0)
                    for piece in first[2 * k:2 * k + 2]:
                        piece()
                for piece in first[8:]:
                    piece()
                for g in range(GROUPS):
                    gaps = {n: [] for n in range(14 + CHUNK_GAPS)}
                    if g + 1 < GROUPS:
                        more = pair_pieces(l, ("rkv", 3 * (g + 1)), xT) + pair_pieces(l, ("rkv", 3 * (g + 1) + 1), xT)
                        for n, p in enumerate(more):
                            gaps[LEVEL_GAPS[g][n]].append(p)
                    for n, p in enumerate(sum([pair_pieces(l, p, xT) for p in chunk_pairs(g)], [])):
                        gaps[14 + chunk_gap(g, n)].append(p)
                    gaps[LOGITS].append(lambda: att_logits(l, g))
                    if g:
                        gaps[Y_BACK].append(lambda: y_back(r0 + g - 1))
                    gaps[BONUS].append(lambda: bonus(r0 + g))
                    gaps[PROBS].append(lambda: att_probs(l, g))
                    gaps[VALUES].append(lambda: att_values(l, g))

                    def fill(n):
                        for p in gaps[n]:
                            p()

                    wkv(r0 + g, fill)
                pe.wait_ge(*dve_parts(l, "o1"))
                split_pair(l, ("oa", 0), lambda kb: (block_of(o_hi, kb), rounded["oT"][:, kb, :]))
                split_pair(l, ("oa", 1), lambda kb: (block_of(o_hi, kb), rounded["oT"][:, kb, :]))
                y_back(r0 + GROUPS - 1)
                for i in (2, 3):
                    split_pair(l, ("oa", i), lambda kb: (block_of(o_hi, kb), rounded["oT"][:, kb, :]))
                pe.wait_ge(*dve_parts(l, "yb1"))
                for i in range(4):
                    split_pair(l, ("ob", i), lambda kb: (block_of(yb_hi, kb), rounded["yb"][:, kb, :]))

                def token_major(kind, n, lhs, wait, w_norm):
                    for i in range(n):
                        w = slot_parts(l, kind, i)
                        wait(i)
                        for t in range(TT):
                            for j in range(2):
                                mm = product(bank(2 + 2 * t + j), [x[:, t * P:t * P + P] for x in lhs(i)],
                                             [x[:, j * 512:j * 512 + 512] for x in w], i == 0, i == n - 1)
                                if i == n - 1 and (t, j) != (1, 1):
                                    mm.then_inc(*pe_x.inc(l, f"{w_norm}{2 * t + j}"))
                        mm.then_inc(slot_used, 1)

                token_major("out", KB, lambda i: (mix_hi[i], mix_lo[i]),
                            lambda i: pe.wait_ge(*dve_parts(l, f"mix{i // 2}")), "A")
                transposed_x(l, "U")
                pe.wait_ge(*dve_parts(l, "x3"))
                for i in range(FB):
                    split_pair(l, ("up", i), lambda kb: (xT_hi[:, kb, :], xT_lo[:, kb, :]))
                token_major("down", FB, lambda i: (hid_hi[i], hid_lo[i]),
                            lambda i: pe.wait_ge(*dve_dense(l, ("up", i))), "B")

        @block.scalar
        def _(act):
            def shift_scaled(l, n, dst, blocks):
                act.wait_ge(*pair_done(l, n))
                src = tok(pair_at[l, n] % 2)
                for b, m in enumerate(blocks):
                    last = act.activation(dst[:, b, :], src[:, b, :], ACT.Identity, scale=dp("omu", m))
                last.then_inc(*act_dense.inc(l, n))

            def mids_up_to(l, end):
                for m in range(act_mid.next - l * MID_PER_LAYER, min(end, MID_PER_LAYER)):
                    k = l * MID_PER_LAYER + m
                    n = SLOT_AT[MIDS[k]]
                    act.wait_ge(landed[n % RING], 16 * (n // RING + 1))
                    if m >= NM:
                        act.wait_ge(*used(*MIDS[k - NM]))
                    act.copy(mid_hi[m % NM][:, :], ring[:, n % RING, :]).then_inc(*act_mid.inc(l, m))

            def rkv(l, g, t):
                r = GROUPS * l + g
                if t == 0 and g:
                    act.wait_ge(*dve_prep(r - 1, "rkk"))
                if t == 2 and g:
                    act.wait_ge(*dve_bv(r - 1, "bv"))
                    if l == 0:
                        act.wait_ge(v_saved, 16 * g)
                dst = [rs[:, :, :], ks[:, :, :], vs_own][t]
                shift_scaled(l, ("rkv", 3 * g + t), dst, [8 * t + GB * g + b for b in range(GB)])

            def gate(l, i):
                act.wait_ge(*pair_done(l, ("gate", i)))
                src = tok(pair_at[l, ("gate", i)] % 2)
                for b in range(2):
                    last = act.activation(gates[:, 2 * i + b, :], src[:, b, :], ACT.Tanh, scale=0.5,
                                          bias=dp("hgate", 2 * i + b))
                last.then_inc(*act_dense.inc(l, ("gate", i)))

            def xT_out(l, w):
                for i in range(4):
                    act.wait_ge(*pe_x(l, f"{w}{i}"))
                    dst = xT if w == "T" else xT_hi
                    act.copy(dst[:, 2 * i:2 * i + 2, :], tok(X_BANKS[i])).then_inc(*act_x.inc(l, f"{w}{i}"))

            def split_hi(l, m):
                k = l * per_layer + m
                n = SLOT_AT[SPLITS[k]]
                act.wait_ge(landed[n % RING], 16 * (n // RING + 1))
                if m >= NS:
                    act.wait_ge(*used(*SPLITS[k - NS]))
                act.copy(w_hi[m % NS], ring[:, n % RING, :]).then_inc(*act_split.inc(l, m))

            def splits_up_to(l, end):
                for m in range(act_split.next - l * per_layer, min(end, per_layer)):
                    split_hi(l, m)

            def prep_kk(r):
                l, g = divmod(r, GROUPS)
                act.wait_ge(*dve_dense(l, ("rkv", 3 * g + 1)))
                if r:
                    act.wait_ge(*pe_bonus(r - 1, "bonus"))
                for b in range(GB):
                    last = act.activation(tmp[:, b, :], ks[:, b, :], ACT.Square, scale=cp(l, "k_k", GB * g + b))
                last.then_inc(*act_prep.inc(r, "kk2"))

            def prep_tanh(r, what, bias, dst, src):
                g = r % GROUPS
                act.wait_ge(*pe_prep(r, {"thw": "zw", "tha": "za", "thv": "zv"}[what]))
                for b in range(GB):
                    last = act.activation(dst[:, b, :], tok(src)[:, b, :], ACT.Tanh, scale=0.5, bias=dp(bias, GB * g + b))
                last.then_inc(*act_prep.inc(r, what))

            def prep_exp(r):
                g = r % GROUPS
                act.wait_ge(*dve_prep(r, "cp"))
                act.activation(flat(dA), flat(dB), ACT.Exp, scale=-DECAY).then_inc(*act_prep.inc(r, "P"))
                act.activation(flat(dC), flat(dC), ACT.Exp, scale=-DECAY).then_inc(*act_prep.inc(r, "Pp"))
                act.activation(flat(dB), flat(dB), ACT.Exp, scale=DECAY).then_inc(*act_prep.inc(r, "iP"))
                act.wait_ge(*pe_prep(r, "ss"))
                act.wait_ge(*act_prep(r, "tha"))
                for b in range(GB):
                    last = act.activation(tmp[:, b, :], tha[:, b, :], ACT.Identity, scale=dp("hka", GB * g + b),
                                          bias=dp("omhka", GB * g + b))
                last.then_inc(*act_prep.inc(r, "kt"))

            def y_square(r):
                act.wait_ge(*dve_y(r, "yc"))
                act.activation(sq[:, :, :], yt[:, :, :], ACT.Square).then_inc(*act_y.inc(r, "sq"))

            def y_norm(r):
                l, g = divmod(r, GROUPS)
                act.wait_ge(*pe_yT(r, "yT"))
                for b in range(GB):
                    u = slice(NCH * b, NCH * b + NCH)
                    for h in range(2):
                        last = act.activation(yt[q64(h), u, :], units(6)[q64(h), u, q64(h)], ACT.Identity,
                                              scale=cp(l, "g_lnx", GB * g + b)[q64(h)], bias=cp(l, "b_lnx", GB * g + b)[q64(h)])
                last.then_inc(*act_y.inc(r, "yn"))

            def att_exp(l, g):
                act.wait_ge(*dve_att(l, f"mx{g}"))
                for j in range(4):
                    a, n = (j * T, T) if j < 2 else (2 * T + (j - 2) * P, P)
                    last = act.activation(lg[:, a:a + n], lg[:, a:a + n], ACT.Exp, bias=small[:, 32 + j:33 + j],
                                          accum_out=small[:, 36 + j:37 + j])
                last.then_inc(*act_att.inc(l, f"e{g}"))

            def att_pT(l, g):
                act.wait_ge(*pe_att(l, f"pT{g}"))
                act.copy(pT, ps[:, 6:8, 0:384]).then_inc(*act_att.inc(l, f"pT{g}"))

            def att_o(l, g):
                act.wait_ge(*pe_att(l, f"o{g}"))
                act.copy(oT[:, 2 * g:2 * g + 2, :], tok(6)).then_inc(*act_att.inc(l, f"o{g}"))

            def levels(r, lev):
                for k in range(2):
                    act.wait_ge(*pe_wkv(r, f"W{lev}{k}"))
                    if lev == 1 and k == 0:
                        act.wait_ge(*pe_wkv(r, "tokK"))
                    act.copy(W_bd[:, 4 * k:4 * k + 4, :], units(2)[:, 4 * k:4 * k + 4, :]
                             ).then_inc(*act_wkv.inc(r, f"W{lev}{k}"))
                    mids_up_to(r // GROUPS, mids_by(GAPS * (r % GROUPS) + 1 + 2 * lev + k))

            def chunk(r, c):
                for name, dst, n in (("Z", Zs, 2), ("Q", Qs, 3)):
                    act.wait_ge(*pe_wkv(r, f"{name}{c}"))
                    act.copy(dst[:, :, :], bank(n)[:, 0:GB * CH].rearrange("p (b s) -> p b s", s=CH)
                             ).then_inc(*act_wkv.inc(r, f"{name}{c}"))

            for l in L2:
                r0 = GROUPS * l
                if l:
                    act.wait_ge(v_saved, 16 * GROUPS)
                    act.dma_start(flat(vf), v_dram[0]).then_inc(v_back, 16)
                xT_out(l, "T")
                if l == 0:
                    act.wait_ge(tables, 1)
                    act.activation(sines[:, 0, :, :], ang[:, 0, :, :], ACT.Sin)
                    act.activation(sines[:, 1, :, :], ang[:, 1, :, :], ACT.Sin).then_inc(tables, 1)
                act.wait_ge(*used(l, "att", 4))
                for t in range(TT):
                    act.copy(p_tok[:, t, 0:512], bank(2 + t))
                act.copy(p_tok[:, :, 512:N_ATT], bank(4)[:, 0:T].rearrange("p (t n) -> p t n", t=TT)[:, :, 0:N_ATT - 512]
                         ).then_inc(*act_att.inc(l, "p"))
                act.wait_ge(*act_att(l, "p"))
                for t in range(TT):
                    last = act.activation(scratch[:, t * D_CQ:t * D_CQ + D_CQ], p_tok[:, t, 0:D_CQ], ACT.Square,
                                          accum_out=small[:, t:t + 1])
                last.then_inc(*act_att.inc(l, "ssq"))
                act.wait_ge(*dve_par(l, "dpar"))
                shift_scaled(l, ("lora", 0), lora[:, 0:2, :], [24, 25])
                act.wait_ge(*dve_dense(l, ("lora", 0)))
                act.activation(lora[0:64, 0, :], lora[0:64, 0, :], ACT.Tanh)
                act.activation(lora[:, 1, :], lora[:, 1, :], ACT.Tanh, scale=0.5).then_inc(*act_lora.inc(l, "tanh"))
                if l:
                    shift_scaled(l, ("vres", 0), lora[:, 2:3, :], [26])
                rkv(l, 0, 0)
                act.wait_ge(*pe_att(l, "cqT"))
                for kb in range(2):
                    last = act.activation(cqT[:, kb, :], tok(6)[:, kb, :], ACT.Identity, scale=cp(l, "g_cq", kb))
                last.then_inc(*act_att.inc(l, "cqT"))
                act.wait_ge(*pe_att(l, "kT"))
                act.wait_ge(zeroed, l + 2)
                act.copy(kT[:, :], bank(7)[:, 0:T])
                act.copy(kiT[q64(0), 0, :], bank(7)[q64(0), T:2 * T])
                act.copy(kiT[q64(1), 1, :], bank(7)[q64(1), T:2 * T]).then_inc(*act_att.inc(l, "kT"))
                rkv(l, 0, 1)
                act.wait_ge(*used(l, "iq", 0))
                for t in range(TT):
                    last = act.copy(qi_tok[:, t, :], bank(2 + t))
                last.then_inc(*act_att.inc(l, "qi"))
                for j in range(2):
                    act.wait_ge(*used(l, "uq", j))
                    for t in range(TT):
                        last = act.copy(q_tok[j][:, t, :], bank(4 + 2 * j + t))
                    last.then_inc(*act_att.inc(l, f"q{j}"))
                rkv(l, 0, 2)
                act.wait_ge(*pe_att(l, "qiT"))
                for i in range(2):
                    last = act.copy(qiT[:, 2 * i:2 * i + 2, :], tok(2 + i))
                last.then_inc(*act_att.inc(l, "qiT"))
                act.wait_ge(*pe_att(l, "qT"))
                for i in range(4):
                    last = act.copy(qT[:, 2 * i:2 * i + 2, :], tok(4 + i))
                last.then_inc(*act_att.inc(l, "qT"))
                for i in range(6):
                    act.wait_ge(*pe_att(l, f"s{i}"))
                    if i >= 2:
                        act.wait_ge(*dve_att(l, f"s0{4 * i - 5}" if i < 4 else f"s1{2 * (i - 4) + 1}"))
                    act.activation(rel[:, i % 2, :], bank(2 + i % 2), ACT.Relu).then_inc(*act_att.inc(l, f"s{i}"))
                prep_kk(r0)
                prep_tanh(r0, "thw", "hw0", dA, 6)
                prep_tanh(r0, "tha", "ha0", tha, 7)
                prep_exp(r0)
                gate(l, 0)
                if l:
                    prep_tanh(r0, "thv", "hv0", kkn, 6)
                for i in range(1, GATES_FIRST):
                    gate(l, i)
                if l:
                    act.wait_ge(x_saved, 16)
                act.copy(xr_hi, flat(xT)).then_inc(*act_parts.inc(l, "xr"))
                for g in range(GROUPS):
                    r = r0 + g
                    nxt = g + 1 < GROUPS
                    if r:
                        act.wait_ge(*pe_wkv(r - 1, f"y{NCH - 1}"))
                    act.wait_ge(*(dve_prep(r, "v") if l else dve_dense(l, ("rkv", 3 * g + 2))))
                    for h in range(2):
                        last = act.copy(v_bd[q64(h), :, q64(h)], by_unit(vs_own)[q64(h)])
                    last.then_inc(*act_wkv.inc(r, "vbd"))
                    act.copy(Y_bd[:, :, :], ident.unsqueeze(1).broadcast_to([P, NU, P])
                             ).then_inc(*act_wkv.inc(r, "resetY"))
                    act.copy(X_bd, ident.unsqueeze(1).broadcast_to([P, NU, P])).then_inc(*act_wkv.inc(r, "resetX"))
                    if l == 0:
                        act.dma_start(v_dram[g], flat(vs_own)).then_inc(v_saved, 16)
                    elif nxt:
                        act.dma_start(flat(vf), v_dram[g + 1]).then_inc(v_back, 16)
                    mids_up_to(l, mids_by(GAPS * g - 1))
                    act.wait_ge(*pe_wkv(r, "V"))
                    for h in range(2):
                        last = act.copy(Vc[q64(h), :, :], units(6)[q64(h), :, q64(h)])
                    last.then_inc(*act_wkv.inc(r, "Vc"))
                    act.wait_ge(*pe_wkv(r, "tokB"))
                    for k in range(2):
                        last = act.copy(bt_bd[:, 4 * k:4 * k + 4, :], units(4)[:, 4 * k:4 * k + 4, :])
                    last.then_inc(*act_wkv.inc(r, "tokB"))
                    mids_up_to(l, mids_by(GAPS * g + 1))
                    act.wait_ge(*pe_wkv(r, "tokK"))
                    for k in range(2):
                        last = act.copy(kt_bd[:, 4 * k:4 * k + 4, :], units(4)[:, 4 * k:4 * k + 4, :])
                    last.then_inc(*act_wkv.inc(r, "tokK"))
                    mids_up_to(l, mids_by(GAPS * g + 2))
                    if g:
                        y_square(r - 1)
                    mids_up_to(l, mids_by(GAPS * g + 3))
                    for lev in range(LEVELS):
                        if lev:
                            levels(r, lev)
                        if lev == 2 and g:
                            y_norm(r - 1)
                        if lev == 2:
                            att_exp(l, g)
                        if lev == 3:
                            act.wait_ge(*pe_bonus(r, "zg"))
                            if g:
                                act.wait_ge(*dve_y(r - 1, "yb"))
                            act.copy(gT[:, :, :], tok(7)).then_inc(*act_g.inc(r, "g"))
                        for t in range(2):
                            if nxt and level_before(g, t) == lev:
                                rkv(l, g + 1, t)
                        if lev == 4:
                            att_pT(l, g)
                    att_o(l, g)
                    if nxt:
                        prep_kk(r + 1)
                        prep_tanh(r + 1, "thw", "hw0", dA, 6)
                        prep_tanh(r + 1, "tha", "ha0", tha, 7)
                    for c in range(NCH):
                        chunk(r, c)
                        mids_up_to(l, mids_by(GAPS * g + 14 + 2 * c))
                        if c == 0 and nxt:
                            prep_exp(r + 1)
                        for kind, i in pairs_done(g, c):
                            if kind == "gate":
                                gate(l, i)
                            else:
                                rkv(l, g + 1, 2)
                        if c == 1 and nxt and l:
                            prep_tanh(r + 1, "thv", "hv0", kkn, 6)
                        if not nxt and c in (1, 2):
                            act.wait_ge(*act_att(l, f"o{g}"))
                            act.copy(o_hi[c - 1], blocks(oT, 4 * (c - 1), 4)).then_inc(*act_parts.inc(l, f"o{c - 1}"))
                        if not nxt and c >= 2:
                            splits_up_to(l, c)
                    act.wait_ge(*pe_wkv(r, f"y{NCH - 1}"))
                    act.copy(yt[:, :, :], unit64(5)).then_inc(*act_y.inc(r, "y"))
                def yb_high(j):
                    act.wait_ge(*dve_y(r0 + GROUPS - 2 + j, "yb"))
                    for i, n in YB_RUNS[j]:
                        last = act.copy(yb_hi_run(i, n), blocks(yb, i, n))
                    last.then_inc(*act_parts.inc(l, f"yb{j}"))

                y_square(r0 + GROUPS - 1)
                splits_up_to(l, NS)
                yb_high(0)
                splits_up_to(l, 2 * NS)
                y_norm(r0 + GROUPS - 1)
                yb_high(1)
                for i in range(4):
                    splits_up_to(l, 2 * i + 2 + NS)
                for i in range(4):
                    splits_up_to(l, KB + 2 * i + 2 + NS)
                    act.wait_ge(*dve_x(l, f"mix{i}"))
                    act.copy(rounded["gates"][:, KB + 2 * i:KB + 2 * i + 2, :], gates[:, 2 * i:2 * i + 2, :]
                             ).then_inc(*act_parts.inc(l, f"mix{i}"))
                act.wait_ge(x_back, 16 * (l + 1))
                act.mul(flat(x_tok), flat(x_tok), ALPHA).then_inc(*act_x.inc(l, "Aax"))
                splits_up_to(l, 3 * KB + NS)
                xT_out(l, "U")
                act.mul(flat(x_tok), flat(x_tok), ALPHA).then_inc(*act_x.inc(l, "Bax"))
                for i in range(FB):
                    n = ("up", i)
                    act.wait_ge(*pair_done(l, n))
                    if i >= 2:
                        act.wait_ge(*dve_dense(l, ("up", i - 2)))
                    c, th = conv[i % 2][:, 0, :], conv[i % 2][:, 1, :]
                    act.activation(c, tok(pair_at[l, n] % 2)[:, 0, :], ACT.Identity, scale=cp(l, "conv_w", 2 * FB + i),
                                   bias=cp(l, "conv_b", i)).then_inc(*act_dense.inc(l, n))
                    splits_up_to(l, 3 * KB + 2 * i + 1 + NS)
                    act.wait_ge(*dve_dense(l, (n, "conv")))
                    act.activation(th, c, ACT.Tanh, scale=0.5).then_inc(*act_dense.inc(l, (n, "tanh")))
                    splits_up_to(l, 3 * KB + 2 * i + 2 + NS)
                    act.wait_ge(*dve_dense(l, (n, "whole")))
                    act.copy(hid_hi[i], th).then_inc(*act_dense.inc(l, (n, "hi")))
                splits_up_to(l, per_layer)

        @block.vector
        def _(dve):
            def shift_add(l, n, dst, blocks):
                dve.wait_ge(*act_dense(l, n))
                src = tok(pair_at[l, n] % 2)
                for b, m in enumerate(blocks):
                    last = dve.scalar_tensor_tensor(out=dst[:, b, 1:T], in0=src[:, b, 0:T - 1], scalar=cp(l, "mu", m),
                                                    in1=dst[:, b, 1:T], op0=ALU.mult, op1=ALU.add)
                last.then_inc(*dve_dense.inc(l, n))

            def mids_up_to(l, end):
                for m in range(dve_mid.next - l * MID_PER_LAYER, min(end, MID_PER_LAYER)):
                    k = SLOT_AT[MIDS[l * MID_PER_LAYER + m]] % RING
                    dve.wait_ge(*act_mid(l, m))
                    dve.tensor_tensor(rounded["ring"][:, k, :], ring[:, k, :], f32(mid_hi[m % NM][:, :]), ALU.subtract
                                      ).then_inc(*dve_mid.inc(l, m))

            def rkv(l, g, t):
                dst = [rs[:, :, :], ks[:, :, :], vs_own][t]
                shift_add(l, ("rkv", 3 * g + t), dst, [8 * t + GB * g + b for b in range(GB)])

            def rotate(l, name, x1, x2, f0, nf, heads, out1=None, out2=None):
                o1, o2 = out1 or x1, out2 or x2
                n = TT * heads * nf
                t = [yt[:, :, :].rearrange("p u s -> p (u s)")[:, 0:n], sq[:, :, :].rearrange("p u s -> p (u s)")[:, 0:n],
                     *[X_Y[:, i, :, :].rearrange("p u s -> p (u s)")[:, 0:n] for i in range(2)]]
                t = [a.rearrange("p (t h f) -> p t h f", t=TT, h=heads) for a in t]
                sin, cos = [sines[:, i, :, f0:f0 + nf].unsqueeze(2).broadcast_to([P, TT, heads, nf]) for i in range(2)]
                dve.tensor_tensor(t[0], x1, cos, ALU.mult)
                dve.tensor_tensor(t[1], x2, sin, ALU.mult)
                dve.tensor_tensor(t[2], x2, cos, ALU.mult)
                dve.tensor_tensor(t[3], x1, sin, ALU.mult).then_inc(*dve_att.inc(l, f"{name}a"))
                dve.wait_ge(*dve_att(l, f"{name}a"))
                dve.tensor_tensor(o1, t[0], t[1], ALU.subtract)
                return dve.tensor_tensor(o2, t[2], t[3], ALU.add)

            def prep_decay(r):
                if r:
                    dve.wait_ge(*dve_bv(r - 1, "bv"))
                dve.wait_ge(*act_prep(r, "thw"))
                dve.tensor_scalar(flat(dA), flat(dA), 0.5, 0.5, ALU.mult, ALU.add).then_inc(*dve_prep.inc(r, "s"))
                dve.wait_ge(*dve_prep(r, "s"))
                dve.tensor_tensor_scan(flat(dB), C["scan"], flat(dA), 0.0, ALU.mult, ALU.add).then_inc(*dve_prep.inc(r, "cum"))
                dve.wait_ge(*dve_prep(r, "cum"))
                dve.tensor_tensor(flat(dC), flat(dB), flat(dA), ALU.subtract).then_inc(*dve_prep.inc(r, "cp"))

            def prep_sum(r):
                dve.wait_ge(*act_prep(r, "P"))
                dve.tensor_copy(pend[:, r % 2, :, :], dA[:, :, CH - 1::CH]).then_inc(*dve_prep.inc(r, "pend"))
                dve.wait_ge(*pe_prep(r, "ss"))
                dve.tensor_scalar(ssm[:, :], bank(7)[:, 0:8], 1e-24, None, ALU.max).then_inc(*dve_prep.inc(r, "ss"))

            def prep_rn(r):
                dve.wait_ge(*pe_prep(r, "rnT"))
                dve.tensor_copy(rnT[:, :], bank(7)[0:8, 128:256]).then_inc(*dve_prep.inc(r, "rnT"))
                if r >= GROUPS:
                    g = r % GROUPS
                    dve.wait_ge(*act_prep(r, "thv"))
                    dve.wait_ge(*dve_dense(r // GROUPS, ("rkv", 3 * g + 2)))
                    dve.wait_ge(v_back, 16 * (g + 1))
                    if g:
                        dve.wait_ge(*pe_att(r // GROUPS, f"o{g - 1}"))
                    dve.tensor_tensor(y_bd_free(r), flat(vf), flat(vs_own), ALU.subtract
                                      ).then_inc(*dve_prep.inc(r, "v1"))
                    dve.wait_ge(*dve_prep(r, "v1"))
                    dve.scalar_tensor_tensor(out=y_bd_free(r), in0=flat(kkn), scalar=1.0, in1=y_bd_free(r), op0=ALU.add,
                                             op1=ALU.mult).then_inc(*dve_prep.inc(r, "v2"))
                    dve.wait_ge(*dve_prep(r, "v2"))
                    dve.scalar_tensor_tensor(out=flat(vs_own), in0=y_bd_free(r), scalar=0.5, in1=flat(vs_own), op0=ALU.mult,
                                             op1=ALU.add).then_inc(*dve_prep.inc(r, "v"))

            def y_bd_free(r):
                return vtmp[:, :]

            def flat2(t):
                return t.rearrange("p a b -> p (a b)")

            def prep_rest(r):
                l, g = divmod(r, GROUPS)
                dve.wait_ge(*pe_prep(r, "rnx"))
                for b in range(GB):
                    last = dve.scalar_tensor_tensor(out=kkn[:, b, :], in0=ks[:, b, :], scalar=cp(l, "k_k", GB * g + b),
                                                    in1=tok(6)[:, b, :], op0=ALU.mult, op1=ALU.mult)
                last.then_inc(*dve_prep.inc(r, "kkn"))
                dve.wait_ge(*act_prep(r, "kt"))
                dve.wait_ge(*dve_prep(r, "kkn"))
                dve.tensor_tensor(flat(ks), flat(ks), flat(tmp), ALU.mult).then_inc(*dve_prep.inc(r, "k2"))
                dve.scalar_tensor_tensor(out=flat(tha), in0=flat(tha), scalar=1.0, in1=flat(kkn), op0=ALU.add, op1=ALU.mult
                                         ).then_inc(*dve_prep.inc(r, "kb"))
                dve.tensor_tensor(arc[:, :, 0, :], by_unit(kkn[:, :, :]), by_unit(dC[:, :, :]), ALU.mult)
                dve.tensor_tensor(arc[:, :, 1, :], by_unit(rs[:, :, :]), by_unit(dA[:, :, :]), ALU.mult
                                  ).then_inc(*dve_prep.inc(r, "arc"))
                if g == 0:
                    dve.wait_ge(zeroed, l + 2)
                dve.wait_ge(*act_prep(r, "iP"))
                dve.wait_ge(*dve_prep(r, "kb"))
                for h in range(2):
                    last = dve.scalar_tensor_tensor(out=b_bd[q64(h), :, q64(h)], in0=by_unit(tha[:, :, :])[q64(h)], scalar=-0.5,
                                                    in1=by_unit(dB[:, :, :])[q64(h)], op0=ALU.mult, op1=ALU.mult)
                last.then_inc(*dve_prep.inc(r, "bneg"))
                for h in range(2):
                    last = dve.tensor_tensor(k_bd[q64(h), :, q64(h)], by_unit(ks[:, :, :])[q64(h)],
                                             by_unit(dB[:, :, :])[q64(h)], ALU.mult)
                last.then_inc(*dve_prep.inc(r, "kp"))

            def prep_bonus(r):
                l, g = divmod(r, GROUPS)
                dve.wait_ge(*dve_prep(r, "kp"))
                for b in range(GB):
                    last = dve.scalar_tensor_tensor(out=tmp[:, b, :], in0=rs[:, b, :], scalar=cp(l, "r_k", GB * g + b),
                                                    in1=ks[:, b, :], op0=ALU.mult, op1=ALU.mult)
                last.then_inc(*dve_prep.inc(r, "rkk"))

            def masked(r, name, dst, src, half_, mask):
                for h in range(2):
                    last = dve.tensor_tensor(dst[q64(h), :, q64(h)], units(src)[q64(h), :, half_ * CH:half_ * CH + CH],
                                             mask[q64(h)].unsqueeze(1).broadcast_to([64, NU, CH]), ALU.mult)
                last.then_inc(*dve_wkv.inc(r, name))

            def mask_of(which, lev, q=slice(0, P)):
                m = masks[q, which, lev, :]
                return m.unsqueeze(1).broadcast_to([q.stop - q.start, NU, CH])

            def update(r, dst, name, which, lev, k, src):
                by_head = lambda t: t[:, 4 * k:4 * k + 4, :].rearrange("p u (h s) -> p (u h) s", h=2)
                dve.copy_predicated(by_head(dst), mask_of(which, lev), by_head(units(src))
                                    ).then_inc(*dve_wkv.inc(r, name))

            def grams(r):
                dve.wait_ge(*pe_wkv(r, "gramB"))
                if r % GROUPS == 0:
                    dve.wait_ge(zeroed, r // GROUPS + 2)
                masked(r, "nT", nT_bd, 2, 0, C["strict"])
                masked(r, "Arb", rb_bd, 2, 1, C["incl"])
                dve.wait_ge(*act_wkv(r, "resetY"))
                for h in range(2):
                    last = dve.copy_predicated(Y_bd[q64(h), :, q64(h)], mask_of(0, 0, q64(h)), units(2)[q64(h), :, 0:CH])
                last.then_inc(*dve_wkv.inc(r, "Y0"))
                if r % GROUPS:
                    mids_up_to(r // GROUPS, mids_by(GAPS * (r % GROUPS) - 1) - 1)
                dve.wait_ge(*pe_wkv(r, "gramK"))
                masked(r, "Aak", ak_bd, 4, 0, C["strict"])
                masked(r, "Ark", rk_bd, 4, 1, C["incl"])
                dve.wait_ge(*pe_wkv(r, "nX"))
                for k in range(2):
                    dve.wait_ge(*act_wkv(r, "resetX"))
                    update(r, X_bd, f"X0{k}", 1, 0, k, 2)
                if r % GROUPS == 0:
                    l = r // GROUPS
                    dve.wait_ge(*act_parts(l, "xr"))
                    dve.tensor_tensor(flat(xr_lo), flat(xT), f32(xr_hi), ALU.subtract).then_inc(*dve_parts.inc(l, "xr"))
                mids_up_to(r // GROUPS, mids_by(GAPS * (r % GROUPS) + 2))

            def level(r, lev):
                for k in range(2):
                    mids_up_to(r // GROUPS, mids_by(GAPS * (r % GROUPS) + 1 + 2 * lev + k))
                    if lev < LEVELS - 1:
                        dve.wait_ge(*pe_wkv(r, f"XW{lev}{k}"))
                        update(r, X_bd, f"X{lev}{k}", 1, lev, k, 4)
                    dve.wait_ge(*pe_wkv(r, f"WtY{lev}{k}"))
                    update(r, Y_bd, f"Y{lev}{k}", 0, lev, k, 2)

            def chunk(r, c):
                two = lambda n: bank(n)[:, 0:GB * CH].rearrange("p (b s) -> p b s", s=CH)
                if c < NCH - 1:
                    src = two(4)
                    dve.wait_ge(*pe_wkv(r, f"S{c}"))
                    if c:
                        dve.tensor_tensor(Sa[:, :, :], src, S[:, (c + 1) % 2, :, :], ALU.add
                                          ).then_inc(*dve_wkv.inc(r, f"S{c}a"))
                        dve.wait_ge(*dve_wkv(r, f"S{c}a"))
                        src = Sa[:, :, :]
                    dve.tensor_tensor(S[:, c % 2, :, :], src, pend[:, r % 2, :, c:c + 1].broadcast_to([P, GB, CH]), ALU.mult
                                      ).then_inc(*dve_wkv.inc(r, f"S{c}"))

            def y_center(r):
                dve.wait_ge(*act_y(r, "y"))
                dve.tensor_reduce(g8[:, 0, :], yt[:, :, :], AX, ALU.add).then_inc(*dve_y.inc(r, "m"))
                dve.wait_ge(*dve_y(r, "m"))
                dve.tensor_scalar(g8[:, 1, :], g8[:, 0, :], -1.0 / N_R, None, ALU.mult).then_inc(*dve_y.inc(r, "m2"))
                dve.wait_ge(*dve_y(r, "m2"))
                dve.tensor_tensor(yt[:, :, :], yt[:, :, :], g8[:, 1, :].unsqueeze(2).broadcast_to([P, NU, CH]), ALU.add
                                  ).then_inc(*dve_y.inc(r, "yc"))

            def y_var(r):
                dve.wait_ge(*act_y(r, "sq"))
                dve.tensor_reduce(g8[:, 2, :], sq[:, :, :], AX, ALU.add).then_inc(*dve_y.inc(r, "v8"))

            def y_scale(r):
                dve.wait_ge(*pool_y(r, "rstd"))
                for h in range(2):
                    last = dve.tensor_tensor(y_bd[q64(h), :, q64(h)], yt[q64(h), :, :],
                                             g8[q64(h), 4, :].unsqueeze(2).broadcast_to([64, NU, CH]), ALU.mult)
                last.then_inc(*dve_y.inc(r, "yr"))

            def y_out(r):
                g = r % GROUPS
                dve.wait_ge(*act_y(r, "yn"))
                dve.tensor_tensor(flat(yt), flat(yt), flat(bv), ALU.add).then_inc(*dve_y.inc(r, "yb1"))
                dve.wait_ge(*dve_y(r, "yb1"))
                dve.tensor_tensor(flat2(yb[:, GB * g:GB * g + GB, :]), flat(yt), flat(gT), ALU.mult
                                  ).then_inc(*dve_y.inc(r, "yb"))

            def bonus(r):
                dve.wait_ge(*pe_bonus(r, "bonus"))
                dve.tensor_tensor(flat(bv), bank(6), flat(vs_own), ALU.mult).then_inc(*dve_bv.inc(r, "bv"))

            def att_masked(l, g):
                dve.wait_ge(*pe_att(l, f"lg{g}"))
                if g == 0:
                    dve.wait_ge(*dve_att(l, "keep1"))
                for t, a, n in ((1, 0, T), (0, 2 * T, P)):
                    last = dve.scalar_tensor_tensor(
                        out=lg[:, a:a + 2 * n].rearrange("p (h s) -> p h s", h=2),
                        in0=bank(7 - t)[:, 0:2 * n].rearrange("p (h s) -> p h s", h=2), scalar=DH_A ** -0.5,
                        in1=keep[:, t, 0:n].unsqueeze(1).broadcast_to([P, 2, n]), op0=ALU.mult, op1=ALU.add)
                last.then_inc(*dve_att.inc(l, f"lg{g}"))
                dve.wait_ge(*dve_att(l, f"lg{g}"))
                for j, a, n in ((32, 0, T), (34, 2 * T, P)):
                    last = dve.tensor_reduce(small[:, j:j + 2], lg[:, a:a + 2 * n].rearrange("p (h s) -> p h s", h=2), AX,
                                             ALU.max, negate=True)
                last.then_inc(*dve_att.inc(l, f"mx{g}"))

            def att_norm(l, g):
                dve.wait_ge(*act_att(l, f"e{g}"))
                dve.reciprocal(small[:, 40:44], small[:, 36:40]).then_inc(*dve_att.inc(l, f"rc{g}"))
                dve.wait_ge(*dve_att(l, f"rc{g}"))
                for j in range(4):
                    a, n = (j * T, T) if j < 2 else (2 * T + (j - 2) * P, P)
                    last = dve.tensor_scalar(lg[:, a:a + n], lg[:, a:a + n], small[:, 40 + j:41 + j], None, ALU.mult)
                last.then_inc(*dve_att.inc(l, f"pn{g}"))

            def splits_up_to(l, end):
                for m in range(dve_split.next - l * per_layer, min(end, per_layer)):
                    k = l * per_layer + m
                    n = SLOT_AT[SPLITS[k]]
                    dve.wait_ge(*act_split(l, m))
                    if m == 2 and l == 0:
                        dve.wait_ge(v_saved, 16 * GROUPS)
                    dve.tensor_tensor(w_lo[m % NS], ring[:, n % RING, :], f32(w_hi[m % NS]), ALU.subtract
                                      ).then_inc(*dve_split.inc(l, m))

            def mix_rest(l, i):
                dve.wait_ge(*act_parts(l, f"mix{i}"))
                parts = rounded["gates"]
                dve.tensor_tensor(parts[:, 2 * i:2 * i + 2, :], gates[:, 2 * i:2 * i + 2, :],
                                  f32(parts[:, KB + 2 * i:KB + 2 * i + 2, :]), ALU.subtract
                                  ).then_inc(*dve_parts.inc(l, f"mix{i}"))

            def layer_norm(l, w, kind, n):
                s = 0.5 if w == "A" else 1.0
                i = 2 * l + "AB".index(w)
                dve.wait_ge(*act_x(l, f"{w}ax"))
                quarter = lambda k: x_tok[:, k // 2, 512 * (k % 2):512 * (k % 2) + 512]
                for k in range(4):
                    dve.wait_ge(*(pe_x(l, f"{w}{k}") if k < 3 else used(l, kind, n - 1)))
                    dve.scalar_tensor_tensor(out=quarter(k), in0=bank(2 + k), scalar=s, in1=quarter(k), op0=ALU.mult,
                                             op1=ALU.add).then_inc(*dve_x.inc(l, f"{w}add{k}"))
                    dve.wait_ge(*dve_x(l, f"{w}add{k}"))
                    dve.bn_stats(ln[:, k // 2, 6 * (k % 2):6 * (k % 2) + 6], quarter(k)).then_inc(*dve_x.inc(l, f"{w}st{k}"))
                dve.wait_ge(*dve_x(l, f"{w}st3"))
                for t in range(TT):
                    last = dve.bn_aggr(ln[:, t, 12:14], ln[:, t, 0:12])
                last.then_inc(*dve_x.inc(l, f"{w}mv"))
                dve.wait_ge(*dve_x(l, f"{w}mv"))
                dve.wait_ge(rows_landed, 32 * (i + 1))
                for t in range(TT):
                    dve.scalar_tensor_tensor(out=x_tok[:, t, :], in0=x_tok[:, t, :], scalar=ln[:, t, 12:13],
                                             in1=lnrow[0], op0=ALU.subtract, op1=ALU.mult).then_inc(*dve_x.inc(l, f"{w}c{t}"))
                dve.wait_ge(*pool_x(l, w))
                for t in range(TT):
                    dve.wait_ge(*dve_x(l, f"{w}c{t}"))
                    dve.scalar_tensor_tensor(out=x_tok[:, t, :], in0=x_tok[:, t, :], scalar=ln[:, t, 21:22],
                                             in1=lnrow[1], op0=ALU.mult, op1=ALU.add).then_inc(*dve_x.inc(l, f"{w}n{t}"))

            turn = 2 * math.pi
            c1 = 6.28125
            c2 = 0.0019340515136718750
            c3 = turn - c1 - c2
            magic = 1.5 * 2 ** 23
            dve.wait_ge(inputs_in, 16 * 4)
            dve.tensor_copy(posf[:, :], pos[:, :]).then_inc(tables_dve, 1)
            dve.wait_ge(tables_dve, 1)
            for t in range(TT):
                last = dve.tensor_scalar(ang[:, 0, t, :], C["freq"], posf[:, t:t + 1], None, ALU.mult)
            last.then_inc(tables_dve, 1)
            dve.wait_ge(tables_dve, 2)
            a0, a1 = ang[:, 0, :, :], ang[:, 1, :, :]
            dve.tensor_scalar(a1, a0, 1.0 / turn, magic, ALU.mult, ALU.add).then_inc(tables_dve, 1)
            dve.wait_ge(tables_dve, 3)
            dve.tensor_scalar(a1, a1, magic, None, ALU.subtract).then_inc(tables_dve, 1)
            for i, c in enumerate((c1, c2, c3)):
                dve.wait_ge(tables_dve, 4 + i)
                dve.scalar_tensor_tensor(out=a0, in0=a1, scalar=-c, in1=a0, op0=ALU.mult, op1=ALU.add).then_inc(tables_dve, 1)
            dve.wait_ge(tables_dve, 7)
            dve.tensor_scalar(a0, a0, math.pi, -math.pi, ALU.min, ALU.max).then_inc(tables_dve, 1)
            dve.wait_ge(tables_dve, 8)
            dve.scalar_tensor_tensor(out=a1, in0=a0, scalar=-1.0, in1=a0, op0=ALU.mult, op1=ALU.max).then_inc(tables_dve, 1)
            dve.wait_ge(tables_dve, 9)
            dve.tensor_scalar(a1, a1, -1.0, math.pi / 2, ALU.mult, ALU.add).then_inc(tables, 1)

            for l in L2:
                r0 = GROUPS * l
                if l:
                    dve.wait_ge(*act_dense(l - 1, ("gate", 7)))
                dve.tensor_scalar(dp("omu", 0, 27), cp(l, "mu", 0, 27), -1.0, 1.0, ALU.mult, ALU.add)
                for a, b, n in (("hw0", "w0", 8), ("ha0", "a0", 8), ("hv0", "v0", 8), ("hgate", "b_gate", 16), ("hka", "k_a", 8)):
                    dve.tensor_scalar(dp(a, 0, n), cp(l, b, 0, n), 0.5, None, ALU.mult)
                dve.tensor_scalar(dp("omhka", 0, 8), cp(l, "k_a", 0, 8), -0.5, 1.0, ALU.mult, ALU.add
                                  ).then_inc(*dve_par.inc(l, "dpar"))
                dve.wait_ge(*act_att(l, "p"))
                dve.tensor_scalar(p_tok[:, :, C_IW:C_IW + H_IDX], p_tok[:, :, C_IW:C_IW + H_IDX],
                                  H_IDX ** -0.5 * D_IDX ** -0.5, None, ALU.mult).then_inc(*dve_att.inc(l, "wi"))
                for t in range(TT):
                    last = dve.bn_stats(ln[:, t, 0:6], p_tok[:, t, C_IK:C_IK + D_IDX])
                last.then_inc(*dve_att.inc(l, "kst"))
                dve.wait_ge(*dve_att(l, "kst"))
                for t in range(TT):
                    last = dve.bn_aggr(ln[:, t, 12:14], ln[:, t, 0:6])
                last.then_inc(*dve_att.inc(l, "kmv"))
                dve.wait_ge(tables, 2)
                kv = p_tok[:, :, C_K:C_K + ROT_A].rearrange("p t (h f) -> p t h f", h=1)
                if l:
                    dve.wait_ge(*act_y(r0 - 1, "yn"))
                rotate(l, "rk", kv[:, :, :, 0:16], kv[:, :, :, 16:32], 0, 16, 1).then_inc(*dve_att.inc(l, "rk"))
                shift_add(l, ("lora", 0), lora[:, 0:2, :], [24, 25])
                dve.wait_ge(*pool_att(l, "rs"))
                for t in range(TT):
                    last = dve.tensor_scalar(p_tok[:, t, 0:D_CQ], p_tok[:, t, 0:D_CQ], small[:, 8 + t:9 + t], None, ALU.mult)
                last.then_inc(*dve_att.inc(l, "cq"))
                dve.wait_ge(lora_landed, 32 * (l + 1))
                ik = p_tok[:, :, C_IK:C_IK + D_IDX]
                for t in range(TT):
                    last = dve.scalar_tensor_tensor(out=ik[:, t, :], in0=ik[:, t, :], scalar=ln[:, t, 12:13],
                                                    in1=kirow[:, 0:D_IDX], op0=ALU.subtract, op1=ALU.mult)
                last.then_inc(*dve_att.inc(l, "kic"))
                dve.wait_ge(*dve_att(l, "kic"))
                for t in range(TT):
                    last = dve.scalar_tensor_tensor(out=ik[:, t, :], in0=ik[:, t, :], scalar=small[:, 10 + t:11 + t],
                                                    in1=kirow[:, D_IDX:2 * D_IDX], op0=ALU.mult, op1=ALU.add)
                last.then_inc(*dve_att.inc(l, "ki"))
                dve.wait_ge(*dve_att(l, "ki"))
                dve.wait_ge(*dve_att(l, "rk"))
                ikh = ik.rearrange("p t (h f) -> p t h f", h=1)
                rotate(l, "rki", ikh[:, :, :, 0:8], ikh[:, :, :, 8:16], 16, 8, 1,
                       out1=kid[:, :, 0:1, 0:8], out2=kid[:, :, 0:1, 8:16])
                dve.tensor_copy(kid[:, :, 0, 16:64], ik[:, :, 16:64]).then_inc(kid_half, 1)
                dve.wait_ge(kid_half, l + 1)
                dve.tensor_copy(kid[:, :, 1, :], kid[:, :, 0, :]).then_inc(*dve_att.inc(l, "rki"))
                dve.wait_ge(*act_lora(l, "tanh"))
                dve.tensor_scalar(lora[:, 1, :], lora[:, 1, :], 0.5, 0.5, ALU.mult, ALU.add)
                if l:
                    shift_add(l, ("vres", 0), lora[:, 2:3, :], [26])
                rkv(l, 0, 0)
                dve.tensor_copy(vtmp[:, 0:1], const[:, 0:1]).then_inc(*dve_par.inc(l, "lsig"))
                rkv(l, 0, 1)
                dve.wait_ge(*act_att(l, "qi"))
                qv = qi_tok.rearrange("p t (h f) -> p t h f", h=H_IDX)
                rotate(l, "rqi", qv[:, :, :, 0:8], qv[:, :, :, 8:16], 16, 8, H_IDX).then_inc(*dve_att.inc(l, "rqi"))
                for j in range(2):
                    dve.wait_ge(*act_att(l, f"q{j}"))
                    dve.wait_ge(*dve_att(l, "rqi" if j == 0 else "rq0"))
                    qv = q_tok[j].rearrange("p t (h f) -> p t h f", h=4)
                    rotate(l, f"rq{j}", qv[:, :, :, 0:16], qv[:, :, :, 16:32], 0, 16, 4).then_inc(*dve_att.inc(l, f"rq{j}"))
                rkv(l, 0, 2)
                for i in range(6):
                    dve.wait_ge(*act_att(l, f"s{i}"))
                    heads, t = (range(4 * i, 4 * i + 4), 0) if i < 2 else (range(2 * (i - 2), 2 * (i - 2) + 2), 1)
                    n = P * (t + 1)
                    for j, h in enumerate(heads):
                        wi = p_tok[:, t, C_IW + h:C_IW + h + 1]
                        src = rel[:, i % 2, j * n:j * n + n]
                        if h == 0:
                            last = dve.tensor_scalar(keep[:, t, 0:n], src, wi, None, ALU.mult)
                        else:
                            dve.wait_ge(*dve_att(l, f"s{t}{h - 1}"))
                            last = dve.scalar_tensor_tensor(out=keep[:, t, 0:n], in0=src, scalar=wi, in1=keep[:, t, 0:n],
                                                            op0=ALU.mult, op1=ALU.add)
                        last.then_inc(*dve_att.inc(l, f"s{t}{h}"))
                def topk(t):
                    dve.wait_ge(*dve_att(l, f"s{t}{H_IDX - 1}"))
                    kp = keep[:, t, 0:P * (t + 1)]
                    dve.tensor_tensor(keep[:, t, t * P:t * P + P], keep[:, t, t * P:t * P + P], C["causal"], ALU.add
                                      ).then_inc(*dve_att.inc(l, f"causal{t}"))
                    for i in range(TOPK // 8):
                        dve.wait_ge(*dve_att(l, f"causal{t}" if i == 0 else f"rep{t}{i - 1}"))
                        dve.max(small[:, 16:24], kp).then_inc(*dve_att.inc(l, f"max{t}{i}"))
                        dve.wait_ge(*dve_att(l, f"max{t}{i}"))
                        dve.match_replace(kp, small[:, 16:24], kp, TAKEN).then_inc(*dve_att.inc(l, f"rep{t}{i}"))
                    dve.wait_ge(*dve_att(l, f"rep{t}{TOPK // 8 - 1}"))
                    dve.tensor_scalar(kp, kp, TAKEN / 2, -NEG, ALU.is_lt, ALU.mult).then_inc(*dve_att.inc(l, f"sel{t}"))
                    dve.wait_ge(*dve_att(l, f"sel{t}"))
                    dve.tensor_scalar(kp, kp, NEG, None, ALU.add).then_inc(*dve_att.inc(l, f"selb{t}"))
                    dve.wait_ge(*dve_att(l, f"selb{t}"))
                    dve.tensor_tensor(keep[:, t, t * P:t * P + P], keep[:, t, t * P:t * P + P], C["causal"], ALU.add
                                      ).then_inc(*dve_att.inc(l, f"keep{t}"))

                prep_decay(r0)
                prep_sum(r0)
                topk(0)
                prep_rn(r0)
                topk(1)
                prep_rest(r0)
                prep_bonus(r0)
                for g in range(GROUPS):
                    r = r0 + g
                    nxt = g + 1 < GROUPS
                    grams(r)
                    if g:
                        y_center(r - 1)
                        y_var(r - 1)
                    mids_up_to(l, mids_by(GAPS * g + 3))
                    for lev in range(LEVELS):
                        if lev:
                            level(r, lev)
                        if lev == 1:
                            att_masked(l, g)
                            if g:
                                y_scale(r - 1)
                        if lev == 2 and g:
                            y_out(r - 1)
                        if lev == 3:
                            bonus(r)
                        for t in range(2):
                            if nxt and level_before(g, t) == lev:
                                rkv(l, g + 1, t)
                        if lev == 3:
                            att_norm(l, g)
                    if nxt:
                        prep_decay(r + 1)
                    for c in range(NCH):
                        chunk(r, c)
                        mids_up_to(l, mids_by(GAPS * g + 13 + 2 * c))
                        if any(kind == "rkv" for kind, _ in pairs_done(g, c)):
                            rkv(l, g + 1, 2)
                        if nxt and c < NCH - 1:
                            [prep_sum, prep_rn, prep_rest][c](r + 1)
                        if not nxt and c in (1, 2):
                            dve.wait_ge(*act_parts(l, f"o{c - 1}"))
                            dve.tensor_tensor(blocks(rounded["oT"], 4 * (c - 1), 4), blocks(oT, 4 * (c - 1), 4),
                                              f32(o_hi[c - 1]), ALU.subtract).then_inc(*dve_parts.inc(l, f"o{c - 1}"))
                        if not nxt and c >= 2:
                            splits_up_to(l, c)
                    if nxt:
                        prep_bonus(r + 1)
                def yb_low(j):
                    dve.wait_ge(*act_parts(l, f"yb{j}"))
                    for i, n in YB_RUNS[j]:
                        last = dve.tensor_tensor(blocks(rounded["yb"], i, n), blocks(yb, i, n), f32(yb_hi_run(i, n)),
                                                 ALU.subtract)
                    last.then_inc(*dve_parts.inc(l, f"yb{j}"))

                def gated_o(i):
                    dve.wait_ge(*pair_done(l, ("oa", i)))
                    dve.wait_ge(*act_dense(l, ("gate", 7)))
                    dst = flat2(gates[:, 2 * i:2 * i + 2, :])
                    dve.scalar_tensor_tensor(out=dst, in0=dst, scalar=1.0, in1=bank(pair_at[l, ("oa", i)] % 2), op0=ALU.add,
                                             op1=ALU.mult).then_inc(*dve_dense.inc(l, ("oa", i)))

                y_center(r0 + GROUPS - 1)
                y_var(r0 + GROUPS - 1)
                splits_up_to(l, NS)
                y_scale(r0 + GROUPS - 1)
                splits_up_to(l, NS + 1)
                gated_o(0)
                yb_low(0)
                splits_up_to(l, 2 * NS)
                y_out(r0 + GROUPS - 1)
                yb_low(1)
                for i in range(1, 4):
                    splits_up_to(l, 2 * i + 2 + NS)
                    gated_o(i)
                for i in range(4):
                    splits_up_to(l, KB + 2 * i + 2 + NS)
                    dve.wait_ge(*pair_done(l, ("ob", i)))
                    dst = flat2(gates[:, KB + 2 * i:KB + 2 * i + 2, :])
                    dve.scalar_tensor_tensor(out=dst, in0=dst, scalar=1.0, in1=bank(pair_at[l, ("ob", i)] % 2), op0=ALU.add,
                                             op1=ALU.mult).then_inc(*dve_dense.inc(l, ("ob", i)))
                    dve.wait_ge(*dve_dense(l, ("ob", i)))
                    a = flat2(gates[:, 2 * i:2 * i + 2, :])
                    dve.tensor_tensor(a, a, dst, ALU.add).then_inc(*dve_x.inc(l, f"mix{i}"))
                    if i:
                        mix_rest(l, i - 1)
                mix_rest(l, 3)
                splits_up_to(l, 3 * KB + 2)
                layer_norm(l, "A", "out", KB)
                for i in range(4):
                    dve.wait_ge(*act_x(l, f"U{i}"))
                    dve.tensor_tensor(xT_lo[:, 2 * i:2 * i + 2, :], tok(X_BANKS[i]), f32(xT_hi[:, 2 * i:2 * i + 2, :]), ALU.subtract
                                      ).then_inc(*dve_parts.inc(l, f"x{i}"))
                splits_up_to(l, 3 * KB + NS)
                for i in range(FB):
                    n = ("up", i)
                    c, th = conv[i % 2][:, 0, :], conv[i % 2][:, 1, :]
                    src = tok(pair_at[l, n] % 2)
                    for k in (1, 2):
                        dve.wait_ge(*(act_dense(l, n) if k == 1 else dve_dense(l, (n, "conv1"))))
                        dve.scalar_tensor_tensor(out=c[:, k:T], in0=src[:, 0, 0:T - k], scalar=cp(l, "conv_w", (2 - k) * FB + i),
                                                 in1=c[:, k:T], op0=ALU.mult, op1=ALU.add
                                                 ).then_inc(*dve_dense.inc(l, (n, "conv1" if k == 1 else "conv")))
                    splits_up_to(l, 3 * KB + 2 * i + 1 + NS)
                    dve.wait_ge(*act_dense(l, (n, "tanh")))
                    dve.scalar_tensor_tensor(out=c, in0=th, scalar=1.0, in1=c, op0=ALU.add, op1=ALU.mult
                                             ).then_inc(*dve_dense.inc(l, (n, "silu")))
                    dve.wait_ge(*dve_dense(l, (n, "silu")))
                    dve.scalar_tensor_tensor(out=th, in0=c, scalar=0.5, in1=src[:, 1, :], op0=ALU.mult, op1=ALU.mult
                                             ).then_inc(*dve_dense.inc(l, (n, "whole")))
                    splits_up_to(l, 3 * KB + 2 * i + 2 + NS)
                    dve.wait_ge(*act_dense(l, (n, "hi")))
                    dve.tensor_tensor(hid_lo[i], th, f32(hid_hi[i]), ALU.subtract).then_inc(*dve_dense.inc(l, n))
                splits_up_to(l, per_layer)
                layer_norm(l, "B", "down", FB)


def _blocks(w):
    n = -(-w.shape[1] // P) * P
    w = np.pad(w, ((0, 0), (0, n - w.shape[1])))
    return w.reshape(KB, P, n // P, P).transpose(2, 1, 0, 3).reshape(n // P, P, D)


def _rows(w):
    return w.reshape(-1, P, D)


def _halves(w):
    return w.reshape(2, P, -1, 512).transpose(2, 1, 0, 3).reshape(-1, P, D)


def _columns(v):
    return v.reshape(-1, P).T


def _consts():
    c = np.zeros((P, NCONST), np.float32)
    at = {n: slice(CONST_AT[n], CONST_AT[n] + w) for n, w in CONST}
    p, s = np.arange(P)[:, None], np.arange(CH)[None]
    c[:, at["ident"]] = np.eye(P)
    c[:, at["stack"]] = p % CH == s
    c[:, at["strict"]] = p % CH < s
    c[:, at["incl"]] = p % CH <= s
    c[:, at["hsel"]] = p // CH == np.arange(2)[None]
    c[:, at["bones"]] = p // CH == np.arange(P)[None] // CH
    col = np.arange(512)[None]
    c[:8, at["rowsel"]] = np.arange(8)[:, None] == 2 * (col // P) + col % P // CH
    c[:, at["scan"]] = col % CH != 0
    c[:, at["causal"]] = np.where(np.arange(P)[None] <= p, 0, NEG)
    f = [THETA ** (-2 * i / ROT_A) for i in range(ROT_A // 2)] + [THETA ** (-2 * i / ROT_IDX) for i in range(ROT_IDX // 2)]
    c[:, at["freq"]] = np.array(f)
    m = np.zeros((P, 2, LEVELS, CH), np.uint32)
    for lev in range(LEVELS):
        n = 1 << lev
        row, colm = p % CH, s
        upper = (row // (2 * n) == colm // (2 * n)) & (row % (2 * n) < n) & (colm % (2 * n) >= n)
        lower = (row // (2 * n) == colm // (2 * n)) & (row % (2 * n) >= n) & (colm % (2 * n) < n)
        m[:, 0, lev], m[:, 1, lev] = upper, lower
    return c, m.reshape(P, -1)


def kernel(**inputs):
    import concourse.bacc as _bacc
    from concourse.bass_utils import run_bass_kernel_spmd as _run

    a = {n: np.asarray(v) for n, v in inputs.items()}
    stream = []
    cpar = np.zeros((P, DEPTH, NCPAR), np.float32)
    lora = np.zeros((DEPTH, P, 3, D), np.float32)
    rpar = np.zeros((DEPTH, 4 * D + 2 * D_IDX), np.float32)
    for l in range(DEPTH):
        w_in = a["w_in0"] if l == 0 else a["w_in_rest"][l - 1]
        rw = w_in[:, N_ATT + N_GATE:N_IN0]
        parts = {"att": _blocks(w_in[:, :N_ATT]), "gate": _blocks(w_in[:, N_ATT:N_ATT + N_GATE]),
                 "rkv": _blocks(rw[:, :3 * D]), "lora": _blocks(rw[:, 3 * D:]), "vres": _blocks(w_in[:, N_IN0:]),
                 "iq": _halves(a["w_iq"][l]), "uq": _halves(a["w_uq"][l]),
                 "oa": _blocks(a["w_oa"][l]), "ob": _blocks(a["w_ob"][l]), "out": _rows(a["w_out"][l]),
                 "up": _blocks(a["w_up"][l]), "down": _rows(a["w_down"][l])}
        stream += [parts[kind][i] for kind, i in stream_order(l)]
        mu = np.zeros(27 * P, np.float32)
        mu[:N_RWKV] = a["mu_rwkv"][l]
        v0 = np.zeros(D, np.float32)
        if l:
            mu[N_RWKV:N_RWKV + LORA_V] = a["mu_vres"][l - 1]
            v0 = a["v0"][l - 1]
            lora[l, :LORA_V, 2] = a["v2"][l - 1]
        for name, v in (("mu", mu), ("v0", v0), *((n, a[n][l]) for n, _ in CPAR if n not in ("mu", "v0"))):
            c = _columns(np.asarray(v).reshape(-1))
            cpar[:, l, CPAR_AT[name]:CPAR_AT[name] + c.shape[1]] = c
        lora[l, :LORA_W, 0], lora[l, LORA_W:, 0], lora[l, :, 1] = a["w2"][l], a["a2"][l], a["g2"][l]
        rpar[l] = np.concatenate([a[n][l] for n in ("ln1_g", "ln1_b", "ln2_g", "ln2_b", "g_ik", "b_ik")])
    const, masks = _consts()
    arrays = {"x_dram": a["x"][0], "pos_dram": np.ascontiguousarray(a["positions"][0].reshape(TT, P).T),
              "stream_dram": np.stack(stream), "lora_dram": lora.reshape(DEPTH, P, 3 * D),
              "cpar_dram": cpar.reshape(P, -1), "rpar_dram": rpar, "const_dram": const, "masks_dram": masks}
    nc = _bacc.Bacc("TRN2", target_bir_lowering=False, num_devices=1)
    args = []
    for name, v in arrays.items():
        arrays[name] = v = np.ascontiguousarray(v)
        args.append(nc.dram_tensor(name, v.shape, mybir.dt.from_np(v.dtype), kind="ExternalInput").ap())
    args.append(nc.dram_tensor("out_dram", (T, D), F32, kind="ExternalOutput").ap())
    args.append(nc.dram_tensor("x_saved_dram", (T, D), F32, kind="Internal").ap())
    args.append(nc.dram_tensor("v_saved_dram", (GROUPS, P, GB * T), F32, kind="Internal").ap())
    trunk(nc, *args)
    r = _run(nc, [arrays], core_ids=[0])
    return r.results[0]["out_dram"].reshape(1, T, D)
```
